# Optimizing a Trainium2 kernel written in Bass

```python
import math
import jax, jax.numpy as jnp
from jax import lax
import numpy as np

D_MODEL = 1024
BATCH = 1
SEQ = 512
DEPTH = 2

MIX_WIDTH = 2 * D_MODEL
RET_WIDTH = MIX_WIDTH // 4
SSD_WIDTH = MIX_WIDTH // 2
FOX_WIDTH = MIX_WIDTH // 4
RET_HEAD_DIM = 128
RET_HEADS = RET_WIDTH // RET_HEAD_DIM
SSD_HEAD_DIM = 64
SSD_HEADS = SSD_WIDTH // SSD_HEAD_DIM
SSD_GROUPS = 2
SSD_STATE = 128
CONV_K = 4
CONV_DIM = SSD_WIDTH + 2 * SSD_GROUPS * SSD_STATE
FOX_HEAD_DIM = 64
FOX_HEADS = FOX_WIDTH // FOX_HEAD_DIM
CHUNK = 128
Q_BLOCK = 128
ROPE_BASE = 10000.0
EPS = 1e-6

IN_SIZES = (RET_WIDTH, RET_WIDTH, RET_WIDTH, RET_WIDTH,
            CONV_DIM, SSD_HEADS, SSD_WIDTH,
            FOX_WIDTH, FOX_WIDTH, FOX_WIDTH, FOX_WIDTH,
            FOX_HEADS)
N_IN = sum(IN_SIZES)
IN_OFFSETS = tuple(int(v) for v in np.cumsum(IN_SIZES)[:-1])


def _rmsnorm(t, gain=None):
    t32 = t.astype(jnp.float32)
    t32 = t32 * lax.rsqrt(jnp.mean(t32 * t32, axis=-1, keepdims=True) + EPS)
    if gain is not None:
        t32 = t32 * gain.astype(jnp.float32)
    return t32.astype(t.dtype)

def _rotary(t, positions):
    half = t.shape[-1] // 2
    freq = ROPE_BASE ** (-jnp.arange(half, dtype=jnp.float32) / half)
    ang = positions.astype(jnp.float32)[..., None] * freq
    cos = jnp.cos(ang)[:, :, None, :]
    sin = jnp.sin(ang)[:, :, None, :]
    t1 = t[..., :half].astype(jnp.float32)
    t2 = t[..., half:].astype(jnp.float32)
    return jnp.concatenate([t1 * cos - t2 * sin, t1 * sin + t2 * cos], axis=-1).astype(t.dtype)

def _retention(q, k, v, positions):
    b, L, H, dh = q.shape
    n = L // CHUNK
    q = _rotary(q, positions)
    k = _rotary(k, positions) * (dh ** -0.5)
    log_g = jnp.log(1.0 - 2.0 ** (-5.0 - jnp.arange(H, dtype=jnp.float32)))
    idx = jnp.arange(CHUNK, dtype=jnp.float32)
    diff = idx[:, None] - idx[None, :]
    decay_intra = jnp.where(diff >= 0, jnp.exp(log_g[:, None, None] * jnp.maximum(diff, 0.0)), 0.0)
    decay_q = jnp.exp(log_g[:, None] * (idx + 1.0))
    decay_k = jnp.exp(log_g[:, None] * (CHUNK - 1.0 - idx))
    decay_chunk = jnp.exp(log_g * CHUNK)

    def to_chunks(t):
        return t.reshape(b, n, CHUNK, H, dh).transpose(1, 0, 3, 2, 4)

    def step(S, inp):
        qc, kc, vc = inp
        s = jnp.einsum('bhid,bhjd->bhij', qc, kc) * decay_intra
        o = (jnp.einsum('bhij,bhjd->bhid', s, vc)
             + jnp.einsum('bhid,bhde->bhie', qc, S) * decay_q[:, :, None])
        S = S * decay_chunk[:, None, None] + jnp.einsum('bhjd,hj,bhje->bhde', kc, decay_k, vc)
        return S, o

    S0 = jnp.zeros((b, H, dh, dh), jnp.float32)
    _, o = lax.scan(step, S0, (to_chunks(q), to_chunks(k), to_chunks(v)))
    o = o.transpose(1, 0, 3, 2, 4).reshape(b, L, H, dh)
    return _rmsnorm(o).astype(v.dtype)

def _ssd(xs, dt, A, Bm, Cm):
    b, L, H, P = xs.shape
    G, N = Bm.shape[2], Bm.shape[3]
    hpg = H // G
    n = L // CHUNK
    a = (dt * A).astype(jnp.float32)
    xdt = xs * dt[..., None]
    xc_all = xdt.reshape(b, n, CHUNK, G, hpg, P).transpose(1, 0, 2, 3, 4, 5)
    a_all = a.reshape(b, n, CHUNK, G, hpg).transpose(1, 0, 3, 4, 2)
    b_all = Bm.reshape(b, n, CHUNK, G, N).transpose(1, 0, 2, 3, 4)
    c_all = Cm.reshape(b, n, CHUNK, G, N).transpose(1, 0, 2, 3, 4)
    causal = jnp.tril(jnp.ones((CHUNK, CHUNK), dtype=bool))

    def step(S, inp):
        xc, ac, bc, cc = inp
        acum = jnp.cumsum(ac, axis=-1)
        seg = acum[..., :, None] - acum[..., None, :]
        Lm = jnp.exp(jnp.where(causal, seg, -jnp.inf))
        cb = jnp.einsum('bign,bjgn->bgij', cc, bc)
        y = jnp.einsum('bgij,bghij,bjghp->bighp', cb, Lm, xc)
        y = y + jnp.einsum('bign,bghpn,bghi->bighp', cc, S, jnp.exp(acum))
        last = acum[..., -1:]
        S = (S * jnp.exp(last)[..., None]
             + jnp.einsum('bjgn,bghj,bjghp->bghpn', bc, jnp.exp(last - acum), xc))
        return S, y

    S0 = jnp.zeros((b, G, hpg, P, N), jnp.float32)
    _, y = lax.scan(step, S0, (xc_all, a_all, b_all, c_all))
    return y.transpose(1, 0, 2, 3, 4, 5).reshape(b, L, H, P)

def _causal_dwconv(u, w, bias):
    out = lax.conv_general_dilated(
        u, w[:, None, :].astype(u.dtype), window_strides=(1,), padding=[(CONV_K - 1, 0)],
        dimension_numbers=('NWC', 'WIO', 'NWC'), feature_group_count=u.shape[-1])
    return out + bias

def _forgetting_attention(q, k, v, log_f):
    b, L, H, dh = q.shape
    nb = L // Q_BLOCK
    Ft = jnp.cumsum(log_f.astype(jnp.float32), axis=1).transpose(0, 2, 1)
    q_blocks = q.reshape(b, nb, Q_BLOCK, H, dh).transpose(1, 0, 2, 3, 4)
    f_blocks = Ft.reshape(b, H, nb, Q_BLOCK).transpose(2, 0, 1, 3)
    kpos = jnp.arange(L)
    scale = dh ** -0.5

    def block(inp):
        qi, fi, i = inp
        s = jnp.einsum('bqhd,bkhd->bhqk', qi, k).astype(jnp.float32) * scale
        s = s + fi[..., None] - Ft[:, :, None, :]
        qpos = i * Q_BLOCK + jnp.arange(Q_BLOCK)
        s = jnp.where(qpos[:, None] >= kpos[None, :], s, -jnp.inf)
        p = jax.nn.softmax(s, axis=-1)
        return jnp.einsum('bhqk,bkhd->bqhd', p.astype(v.dtype), v)

    o = lax.map(block, (q_blocks, f_blocks, jnp.arange(nb)))
    return o.transpose(1, 0, 2, 3, 4).reshape(b, L, H, dh)

def _layer(x, c, positions, norm_g, w_ada, b_ada, w_in, conv_w, conv_b,
           dt_bias, a_log, d_skip, ssd_norm_g, b_forget, w_out):
    b, L, _ = x.shape
    mod = jax.nn.silu(c) @ w_ada + b_ada
    shift, scale, gate = jnp.split(mod, 3, axis=-1)
    h = _rmsnorm(x, norm_g) * (1.0 + scale[:, None, :]) + shift[:, None, :]

    proj = h @ w_in
    (rq, rk, rv, rg, xbc, dt_raw, z, fq, fk, fv, fg, f_raw) = jnp.split(proj, IN_OFFSETS, axis=-1)

    ret = _retention(rq.reshape(b, L, RET_HEADS, RET_HEAD_DIM),
                     rk.reshape(b, L, RET_HEADS, RET_HEAD_DIM),
                     rv.reshape(b, L, RET_HEADS, RET_HEAD_DIM), positions)
    ret = ret.reshape(b, L, RET_WIDTH) * jax.nn.silu(rg)

    xbc = jax.nn.silu(_causal_dwconv(xbc, conv_w, conv_b))
    xs, Bm, Cm = jnp.split(xbc, (SSD_WIDTH, SSD_WIDTH + SSD_GROUPS * SSD_STATE), axis=-1)
    xs = xs.reshape(b, L, SSD_HEADS, SSD_HEAD_DIM)
    Bm = Bm.reshape(b, L, SSD_GROUPS, SSD_STATE)
    Cm = Cm.reshape(b, L, SSD_GROUPS, SSD_STATE)
    dt = jax.nn.softplus(dt_raw + dt_bias)
    A = -jnp.exp(a_log.astype(jnp.float32))
    y = _ssd(xs, dt, A, Bm, Cm) + d_skip[:, None] * xs
    ssd = _rmsnorm(y.reshape(b, L, SSD_WIDTH).astype(x.dtype) * jax.nn.silu(z), ssd_norm_g)

    log_f = jax.nn.log_sigmoid((f_raw + b_forget).astype(jnp.float32))
    fox = _forgetting_attention(fq.reshape(b, L, FOX_HEADS, FOX_HEAD_DIM),
                                fk.reshape(b, L, FOX_HEADS, FOX_HEAD_DIM),
                                fv.reshape(b, L, FOX_HEADS, FOX_HEAD_DIM), log_f)
    fox = fox.reshape(b, L, FOX_WIDTH) * jax.nn.silu(fg)

    mixed = jnp.concatenate([ret.astype(x.dtype), ssd.astype(x.dtype), fox.astype(x.dtype)], axis=-1)
    out = mixed @ w_out
    return x + gate[:, None, :] * out

def first_inputs(seed: int = 0) -> dict:
    key = jax.random.key(seed)
    ks = jax.random.split(key, 16)
    f32 = jnp.float32
    x = jax.random.normal(ks[0], (BATCH, SEQ, D_MODEL), f32)
    c = jax.random.normal(ks[1], (BATCH, D_MODEL), f32)
    offsets = jax.random.randint(ks[2], (BATCH, 1), 0, 4096, dtype=jnp.int32)
    positions = (jnp.arange(SEQ, dtype=jnp.int32)[None, :] + offsets).astype(jnp.int32)
    norm_g = 1.0 + 0.02 * jax.random.normal(ks[3], (DEPTH, D_MODEL), f32)
    w_ada = 0.5 * D_MODEL ** -0.5 * jax.random.normal(ks[4], (DEPTH, D_MODEL, 3 * D_MODEL), f32)
    b_ada = 0.02 * jax.random.normal(ks[5], (DEPTH, 3 * D_MODEL), f32)
    w_in = D_MODEL ** -0.5 * jax.random.normal(ks[6], (DEPTH, D_MODEL, N_IN), f32)
    conv_w = CONV_K ** -0.5 * jax.random.normal(ks[7], (DEPTH, CONV_K, CONV_DIM), f32)
    conv_b = 0.02 * jax.random.normal(ks[8], (DEPTH, CONV_DIM), f32)
    dt0 = jnp.exp(jax.random.uniform(ks[9], (DEPTH, SSD_HEADS), f32, math.log(1e-3), math.log(1e-1)))
    dt_bias = dt0 + jnp.log(-jnp.expm1(-dt0))
    a_log = jnp.log(jax.random.uniform(ks[10], (DEPTH, SSD_HEADS), f32, 1.0, 16.0))
    d_skip = 1.0 + 0.1 * jax.random.normal(ks[11], (DEPTH, SSD_HEADS), f32)
    ssd_norm_g = 1.0 + 0.02 * jax.random.normal(ks[12], (DEPTH, SSD_WIDTH), f32)
    b_forget = jax.random.uniform(ks[13], (DEPTH, FOX_HEADS), f32, 2.0, 5.0)
    w_out = MIX_WIDTH ** -0.5 * jax.random.normal(ks[14], (DEPTH, MIX_WIDTH, D_MODEL), f32)
    final_g = 1.0 + 0.02 * jax.random.normal(ks[15], (D_MODEL,), f32)
    return {"x": x, "c": c, "positions": positions, "norm_g": norm_g, "w_ada": w_ada,
            "b_ada": b_ada, "w_in": w_in, "conv_w": conv_w, "conv_b": conv_b,
            "dt_bias": dt_bias, "a_log": a_log, "d_skip": d_skip, "ssd_norm_g": ssd_norm_g,
            "b_forget": b_forget, "w_out": w_out, "final_g": final_g}

def first_block(x, c, positions, norm_g, w_ada, b_ada, w_in, conv_w, conv_b,
              dt_bias, a_log, d_skip, ssd_norm_g, b_forget, w_out, final_g):
    for layer in range(DEPTH):
        x = _layer(x, c, positions, norm_g[layer], w_ada[layer], b_ada[layer], w_in[layer],
                   conv_w[layer], conv_b[layer], dt_bias[layer], a_log[layer], d_skip[layer],
                   ssd_norm_g[layer], b_forget[layer], w_out[layer])
    return _rmsnorm(x, final_g)


HEAD_DIM = 64
N_A_LAYERS = DEPTH // 2
N_B_LAYERS = DEPTH - N_A_LAYERS
MEM_LEN = 256
MEM_HEADS = 4
MEM_W = MEM_HEADS * HEAD_DIM
RWKV_HEADS = (D_MODEL - MEM_W) // HEAD_DIM
RWKV_W = RWKV_HEADS * HEAD_DIM
DECAY_LORA = 64
AAA_LORA = 64
GATE_LORA = 128
RWKV_SHIFT_W = 3 * RWKV_W + DECAY_LORA + AAA_LORA + GATE_LORA
A_IN_W = RWKV_SHIFT_W + MEM_W
DIL_GROUPS = ((128, 1), (512, 4), (2048, 16))
DIL_GROUP_HEADS = 4
DIL_HEADS = len(DIL_GROUPS) * DIL_GROUP_HEADS
DIL_W = DIL_HEADS * HEAD_DIM
DIL_OUT_W = DIL_GROUP_HEADS * HEAD_DIM
BLOCK = 128
NUM_BUCKETS = 32
MAX_DISTANCE = 2048
D_FF = 2816
NORM_EPS = 1e-6
LNX_EPS = 64e-5
NEG_INF = -1e30


def rms_norm(x, g):
    xf = x.astype(jnp.float32)
    y = xf * lax.rsqrt(jnp.mean(xf * xf, axis=-1, keepdims=True) + NORM_EPS)
    return (y * g.astype(jnp.float32)).astype(x.dtype)

def split_heads(t):
    return t.reshape(t.shape[:-1] + (t.shape[-1] // HEAD_DIM, HEAD_DIM))

def swiglu_ffn(x, norm_g, w_in, w_out):
    gate, up = jnp.split(rms_norm(x, norm_g) @ w_in, 2, axis=-1)
    return (jax.nn.silu(gate) * up) @ w_out

def token_shift(p, mu):
    prev = jnp.pad(p, ((0, 0), (1, 0), (0, 0)))[:, :-1]
    return p + mu * (prev - p)

def rwkv7_scan(r, w, k, v, kk, a):
    b, _, h, n = r.shape

    def step(state, inp):
        r_t, w_t, k_t, v_t, kk_t, a_t = inp
        sa = jnp.einsum('bhvk,bhk->bhv', state, -kk_t)
        state = (state * w_t[:, :, None, :]
                 + sa[..., None] * (kk_t * a_t)[:, :, None, :]
                 + v_t[..., None] * k_t[:, :, None, :])
        return state, jnp.einsum('bhvk,bhk->bhv', state, r_t)

    xs = tuple(jnp.moveaxis(t.astype(jnp.float32), 1, 0) for t in (r, w, k, v, kk, a))
    _, ys = lax.scan(step, jnp.zeros((b, h, n, n), jnp.float32), xs)
    return jnp.moveaxis(ys, 0, 1)

def rwkv7_mix(p, mu, w0, w_up, a0, a_up, g_up, kk_scale, k_a, r_k, lnx_g, lnx_b):
    out_dtype = p.dtype
    b, s = p.shape[:2]
    p = token_shift(p, mu).astype(jnp.float32)
    cuts = [RWKV_W, 2 * RWKV_W, 3 * RWKV_W, 3 * RWKV_W + DECAY_LORA,
            3 * RWKV_W + DECAY_LORA + AAA_LORA]
    r, k, v, w_lo, a_lo, g_lo = jnp.split(p, cuts, axis=-1)
    w_log = -jax.nn.softplus(-(w0 + jnp.tanh(w_lo) @ w_up)) - 0.5
    decay = jnp.exp(-jnp.exp(w_log))
    a = jax.nn.sigmoid(a0 + a_lo @ a_up)
    g = jax.nn.sigmoid(g_lo) @ g_up
    kk = split_heads(k * kk_scale)
    kk = kk / jnp.maximum(jnp.linalg.norm(kk, axis=-1, keepdims=True), 1e-12)
    k = k * (1.0 + (a - 1.0) * k_a)
    r_h, k_h, v_h, a_h, w_h = (split_heads(t) for t in (r, k, v, a, decay))
    y = rwkv7_scan(r_h, w_h, k_h, v_h, kk, a_h)
    mean = jnp.mean(y, axis=-1, keepdims=True)
    var = jnp.mean(jnp.square(y - mean), axis=-1, keepdims=True)
    y = ((y - mean) * lax.rsqrt(var + LNX_EPS)).reshape(b, s, RWKV_W) * lnx_g + lnx_b
    bonus = jnp.sum(r_h * k_h * r_k, axis=-1, keepdims=True) * v_h
    y = (y + bonus.reshape(b, s, RWKV_W)) * g
    return y.astype(out_dtype)

def memory_attention(q, mem, mem_norm_g, w_kv, q_gain, k_gain):
    k, v = jnp.split(rms_norm(mem, mem_norm_g) @ w_kv, 2, axis=-1)
    k = rms_norm(split_heads(k), k_gain)
    v = split_heads(v)
    q = rms_norm(q, q_gain)
    logits = jnp.einsum('bshd,bmhd->bhsm', q, k).astype(jnp.float32) / math.sqrt(HEAD_DIM)
    probs = jax.nn.softmax(logits, axis=-1)
    return jnp.einsum('bhsm,bmhd->bshd', probs.astype(v.dtype), v)

def padded_len(seq_len, dil):
    unit = dil * BLOCK
    return -(-seq_len // unit) * unit

def strided_blocks(t, dil, s_pad):
    b, s = t.shape[:2]
    t = jnp.pad(t, ((0, 0), (0, s_pad - s)) + ((0, 0),) * (t.ndim - 2))
    t = t.reshape((b, s_pad // dil, dil) + t.shape[2:])
    t = jnp.moveaxis(t, 2, 1)
    return t.reshape((b, dil, s_pad // (dil * BLOCK), BLOCK) + t.shape[3:])

def unstride_blocks(t, seq_len):
    b, dil, nb, blk = t.shape[:4]
    t = t.reshape((b, dil, nb * blk) + t.shape[4:])
    t = jnp.moveaxis(t, 1, 2)
    return t.reshape((b, dil * nb * blk) + t.shape[3:])[:, :seq_len]

def with_prev_block(t):
    prev = jnp.pad(t[:, :, :-1], ((0, 0), (0, 0), (1, 0), (0, 0), (0, 0), (0, 0)))
    return jnp.concatenate([prev, t], axis=3)

def t5_bucket(dist):
    max_exact = NUM_BUCKETS // 2
    d_f = jnp.maximum(dist, 1).astype(jnp.float32)
    large = max_exact + (jnp.log(d_f / max_exact) / math.log(MAX_DISTANCE / max_exact)
                         * (NUM_BUCKETS - max_exact)).astype(jnp.int32)
    large = jnp.minimum(large, NUM_BUCKETS - 1)
    return jnp.where(dist < max_exact, dist, large)

def band_mask_and_bias(window, dil, n_blocks, table):
    span = window // dil
    qi = jnp.arange(BLOCK)[:, None]
    kj = jnp.arange(2 * BLOCK)[None, :]
    dsub = BLOCK + qi - kj
    band = (dsub >= 0) & (dsub <= span)
    first = (jnp.arange(n_blocks)[:, None, None] > 0) | (kj[None] >= BLOCK)
    mask = band[None] & first
    bias = jnp.transpose(table[t5_bucket(jnp.maximum(dsub, 0) * dil)], (2, 0, 1))
    return mask, bias

def shared_kv_blocks(x, kv_norm, kv_w, k_gain):
    k, v = jnp.split(rms_norm(x, kv_norm) @ kv_w, 2, axis=-1)
    k = rms_norm(split_heads(k), k_gain)
    v = split_heads(v)
    seq_len = x.shape[1]
    k_blocks, v_blocks = [], []
    for g, (_, dil) in enumerate(DIL_GROUPS):
        hs = slice(g * DIL_GROUP_HEADS, (g + 1) * DIL_GROUP_HEADS)
        s_pad = padded_len(seq_len, dil)
        k_blocks.append(strided_blocks(k[:, :, hs], dil, s_pad))
        v_blocks.append(strided_blocks(v[:, :, hs], dil, s_pad))
    return k_blocks, v_blocks

def dilated_attention(q, k_blocks, v_blocks, q_gain, rel_bias, seq_len):
    q = rms_norm(q, q_gain)
    scale = 1.0 / math.sqrt(HEAD_DIM)
    outs, lses = [], []
    for g, (window, dil) in enumerate(DIL_GROUPS):
        hs = slice(g * DIL_GROUP_HEADS, (g + 1) * DIL_GROUP_HEADS)
        qb = strided_blocks(q[:, :, hs], dil, padded_len(seq_len, dil))
        kw = with_prev_block(k_blocks[g])
        vw = with_prev_block(v_blocks[g]).astype(jnp.float32)
        mask, bias = band_mask_and_bias(window, dil, qb.shape[2], rel_bias[:, hs])
        logits = jnp.einsum('brnqhd,brnkhd->brnhqk', qb, kw).astype(jnp.float32) * scale
        logits = jnp.where(mask[:, None], logits + bias, NEG_INF)
        m = jnp.max(logits, axis=-1, keepdims=True)
        p = jnp.exp(logits - m)
        l = jnp.sum(p, axis=-1, keepdims=True)
        o = jnp.einsum('brnhqk,brnkhd->brnqhd', p, vw) / jnp.swapaxes(l, 3, 4)
        lse = jnp.swapaxes(m + jnp.log(l), 3, 4)
        outs.append(unstride_blocks(o, seq_len))
        lses.append(unstride_blocks(lse, seq_len))
    weights = jax.nn.softmax(jnp.stack(lses), axis=0)
    return jnp.sum(weights * jnp.stack(outs), axis=0).astype(q.dtype)

def second_inputs(seed: int = 0) -> dict:
    key = jax.random.key(seed)
    keys = iter(jax.random.split(key, 48))

    def normal(shape, scale):
        return jax.random.normal(next(keys), shape, jnp.float32) * scale

    def gain(shape):
        return 1.0 + normal(shape, 0.02)

    def uniform(shape, lo, hi):
        return jax.random.uniform(next(keys), shape, jnp.float32, lo, hi)

    d, f = D_MODEL, D_FF
    return {
        'x': normal((BATCH, SEQ, d), 1.0),
        'mem': normal((BATCH, MEM_LEN, d), 1.0),
        'ffn_pre_norm': gain((DEPTH, d)),
        'ffn_pre_w_in': normal((DEPTH, d, 2 * f), d ** -0.5),
        'ffn_pre_w_out': normal((DEPTH, f, d), f ** -0.5),
        'mix_norm': gain((DEPTH, d)),
        'ffn_post_norm': gain((DEPTH, d)),
        'ffn_post_w_in': normal((DEPTH, d, 2 * f), d ** -0.5),
        'ffn_post_w_out': normal((DEPTH, f, d), f ** -0.5),
        'mem_norm': gain((DEPTH, d)),
        'mem_w_kv': normal((DEPTH, d, 2 * MEM_W), d ** -0.5),
        'mem_q_norm': gain((DEPTH, HEAD_DIM)),
        'mem_k_norm': gain((DEPTH, HEAD_DIM)),
        'a_w_in': normal((N_A_LAYERS, d, A_IN_W), d ** -0.5),
        'a_shift_mu': uniform((N_A_LAYERS, RWKV_SHIFT_W), 0.0, 1.0),
        'a_w0': uniform((N_A_LAYERS, RWKV_W), -6.0, -1.0),
        'a_w_up': normal((N_A_LAYERS, DECAY_LORA, RWKV_W), 0.5 * DECAY_LORA ** -0.5),
        'a_a0': normal((N_A_LAYERS, RWKV_W), 0.1),
        'a_a_up': normal((N_A_LAYERS, AAA_LORA, RWKV_W), AAA_LORA ** -0.5),
        'a_g_up': normal((N_A_LAYERS, GATE_LORA, RWKV_W), GATE_LORA ** -0.5),
        'a_kk_scale': 0.85 + normal((N_A_LAYERS, RWKV_W), 0.02),
        'a_k_a': gain((N_A_LAYERS, RWKV_W)),
        'a_r_k': normal((N_A_LAYERS, RWKV_HEADS, HEAD_DIM), 0.1),
        'a_lnx_g': gain((N_A_LAYERS, RWKV_W)),
        'a_lnx_b': normal((N_A_LAYERS, RWKV_W), 0.01),
        'a_w_out': normal((N_A_LAYERS, RWKV_W + MEM_W, d), (RWKV_W + MEM_W) ** -0.5),
        'b_w_q': normal((N_B_LAYERS, d, DIL_W + MEM_W), d ** -0.5),
        'b_q_norm': gain((N_B_LAYERS, HEAD_DIM)),
        'b_w_out': normal((N_B_LAYERS, DIL_OUT_W + MEM_W, d), (DIL_OUT_W + MEM_W) ** -0.5),
        'kv_norm': gain((d,)),
        'kv_w': normal((d, 2 * DIL_W), d ** -0.5),
        'kv_k_norm': gain((HEAD_DIM,)),
        'rel_bias': normal((NUM_BUCKETS, DIL_HEADS), 0.2),
    }

def second_block(x, mem, ffn_pre_norm, ffn_pre_w_in, ffn_pre_w_out, mix_norm,
              ffn_post_norm, ffn_post_w_in, ffn_post_w_out,
              mem_norm, mem_w_kv, mem_q_norm, mem_k_norm,
              a_w_in, a_shift_mu, a_w0, a_w_up, a_a0, a_a_up, a_g_up,
              a_kk_scale, a_k_a, a_r_k, a_lnx_g, a_lnx_b, a_w_out,
              b_w_q, b_q_norm, b_w_out, kv_norm, kv_w, kv_k_norm, rel_bias):
    b, s = x.shape[:2]
    k_blocks, v_blocks = None, None
    for layer in range(DEPTH):
        x = x + 0.5 * swiglu_ffn(x, ffn_pre_norm[layer], ffn_pre_w_in[layer], ffn_pre_w_out[layer])
        u = rms_norm(x, mix_norm[layer])
        if layer < N_A_LAYERS:
            i = layer
            proj = u @ a_w_in[i]
            y_main = rwkv7_mix(proj[..., :RWKV_SHIFT_W], a_shift_mu[i], a_w0[i], a_w_up[i],
                               a_a0[i], a_a_up[i], a_g_up[i], a_kk_scale[i], a_k_a[i],
                               a_r_k[i], a_lnx_g[i], a_lnx_b[i])
            y_mem = memory_attention(split_heads(proj[..., RWKV_SHIFT_W:]), mem, mem_norm[layer],
                                     mem_w_kv[layer], mem_q_norm[layer], mem_k_norm[layer])
            y = jnp.concatenate([y_main, y_mem.reshape(b, s, MEM_W)], axis=-1) @ a_w_out[i]
        else:
            j = layer - N_A_LAYERS
            q_all = u @ b_w_q[j]
            y_dil = dilated_attention(split_heads(q_all[..., :DIL_W]), k_blocks, v_blocks,
                                      b_q_norm[j], rel_bias, s)
            y_mem = memory_attention(split_heads(q_all[..., DIL_W:]), mem, mem_norm[layer],
                                     mem_w_kv[layer], mem_q_norm[layer], mem_k_norm[layer])
            y = jnp.concatenate([y_dil.reshape(b, s, DIL_OUT_W),
                                 y_mem.reshape(b, s, MEM_W)], axis=-1) @ b_w_out[j]
        x = x + y
        x = x + 0.5 * swiglu_ffn(x, ffn_post_norm[layer], ffn_post_w_in[layer], ffn_post_w_out[layer])
        if layer == N_A_LAYERS - 1:
            k_blocks, v_blocks = shared_kv_blocks(x, kv_norm, kv_w, kv_k_norm)
    return x


def setup_inputs(seed=0):
    out = dict(first_inputs(seed))
    for name, value in second_inputs(seed + 1).items():
        if name != "x":
            out[name + "_2"] = value
    return out


def reference(
    x, c, positions, norm_g, w_ada, b_ada, w_in, conv_w, conv_b, dt_bias, a_log, d_skip,
    ssd_norm_g, b_forget, w_out, final_g, mem_2, ffn_pre_norm_2, ffn_pre_w_in_2,
    ffn_pre_w_out_2, mix_norm_2, ffn_post_norm_2, ffn_post_w_in_2, ffn_post_w_out_2, mem_norm_2,
    mem_w_kv_2, mem_q_norm_2, mem_k_norm_2, a_w_in_2, a_shift_mu_2, a_w0_2, a_w_up_2, a_a0_2,
    a_a_up_2, a_g_up_2, a_kk_scale_2, a_k_a_2, a_r_k_2, a_lnx_g_2, a_lnx_b_2, a_w_out_2,
    b_w_q_2, b_q_norm_2, b_w_out_2, kv_norm_2, kv_w_2, kv_k_norm_2, rel_bias_2,
):
    x = first_block(
        x, c, positions, norm_g, w_ada, b_ada, w_in, conv_w, conv_b, dt_bias, a_log, d_skip,
        ssd_norm_g, b_forget, w_out, final_g,
    )
    return second_block(
        x, mem_2, ffn_pre_norm_2, ffn_pre_w_in_2, ffn_pre_w_out_2, mix_norm_2, ffn_post_norm_2,
        ffn_post_w_in_2, ffn_post_w_out_2, mem_norm_2, mem_w_kv_2, mem_q_norm_2, mem_k_norm_2,
        a_w_in_2, a_shift_mu_2, a_w0_2, a_w_up_2, a_a0_2, a_a_up_2, a_g_up_2, a_kk_scale_2,
        a_k_a_2, a_r_k_2, a_lnx_g_2, a_lnx_b_2, a_w_out_2, b_w_q_2, b_q_norm_2, b_w_out_2,
        kv_norm_2, kv_w_2, kv_k_norm_2, rel_bias_2,
    )


_drawn_inputs = setup_inputs


def setup_inputs(seed=0):
    import zlib

    import numpy as np

    out = dict(_drawn_inputs(seed))
    spreads = {}
    factors = {'norm_g': 4.22,
     'conv_b': 5.12,
     'ssd_norm_g': 6.94,
     'b_forget': 2.754,
     'ffn_pre_norm_2': 4.432,
     'mix_norm_2': 3.249,
     'ffn_post_norm_2': 5.507,
     'mem_norm_2': 8.0,
     'mem_q_norm_2': 8.0,
     'mem_k_norm_2': 8.0,
     'a_w_up_2': 4.86,
     'a_a0_2': 3.374,
     'a_kk_scale_2': 56.28,
     'a_k_a_2': 5.947,
     'a_lnx_g_2': 36.013,
     'a_lnx_b_2': 64.0,
     'b_q_norm_2': 8.0,
     'kv_norm_2': 8.0,
     'kv_k_norm_2': 8.0,
     'rel_bias_2': 13.362}
    for name, (base, spread) in spreads.items():
        noise = np.random.default_rng([zlib.crc32(name.encode()), seed]).standard_normal(out[name].shape)
        drawn = base * np.exp(spread * noise) if base else spread * noise
        out[name] = __import__('jax').numpy.asarray(drawn.astype(out[name].dtype))
    for name, factor in factors.items():
        out[name] = (out[name] * factor).astype(out[name].dtype)
    return out
```

```python
from contextlib import ExitStack, contextmanager

import numpy as np

import concourse.bass as bass
from concourse import mybir

F32 = mybir.dt.float32
U32 = mybir.dt.uint32
I32 = mybir.dt.int32
ALU = mybir.AluOpType
ACT = mybir.ActivationFunctionType
AX_X = mybir.AxisListType.X

P = 128
T = 512
NT = T // P
D = 1024
KD = D // P
DEPTH = 2
RING = 4

RET_HEADS = 4
SSD_HEADS, SSD_DIM = 16, 64
SSD_GROUPS = 2
FOX_HEADS, FOX_DIM = 8, 64
CONV_K = 4
NXBC = 12
MIX = 16
RET_T, SSD_T, FOX_T = 0, 4, 12
DTF_F = 32
NDTF = 64

FF = 2816
KF = FF // P
RW = 6
RW_HEADS = 12
NSHIFT = 20
A_TILES = 22
MEM = 256
MEM_HEADS = 4
HD = 64
DIL = 3
DIL_HEADS = 4
NREL = 384
BUCKETS = 32

EPS = 1e-6
LNX_EPS = 64e-5
NEG = -1e30
TWO_PI = 2 * np.pi
C1 = 6.28125
C2 = float(np.float32(np.round((TWO_PI - C1) * 2 ** 22) / 2 ** 22))
C3 = float(np.float32(TWO_PI - C1 - C2))
ROUND = 1.5 * 2.0 ** 23
DECAY_SCALE = -float(np.exp(-0.5))

RET_TILES = 16
SSD_TILES = NXBC + 8 + 1
FOX_TILES = 16


def vec_columns():
    at, out = 0, {}

    def add(name, count):
        nonlocal at
        out[name] = (at, count)
        at += count

    for l in range(DEPTH):
        add(f"norm_g{l}", KD)
        add(f"b_ada{l}", 3 * KD)
        for k in range(CONV_K):
            add(f"conv_w{l}_{k}", NXBC)
        add(f"conv_b{l}", NXBC)
        add(f"d_skip{l}", 8)
        add(f"ssd_g{l}", 8)
        add(f"dtf_b{l}", 1)
        add(f"a_log{l}", 1)
    add("final_g", KD)
    for l in range(DEPTH):
        for name in ("pre_g", "mix_g", "post_g", "mem_g"):
            add(f"{name}{l}", KD)
        add(f"memq_g{l}", 1)
        add(f"memk_g{l}", 1)
    add("mu", NSHIFT)
    for name in ("w0", "a0", "kk_scale", "k_a", "r_k", "lnx_g", "lnx_b"):
        add(name, RW)
    add("bq_g", 1)
    add("kv_g", KD)
    add("kvk_g", 1)
    return out, at


VEC, NVEC = vec_columns()


def const_tables():
    i = np.arange(P)
    row, col = i[:, None], i[None, :]
    parts = {"ident": np.eye(P), "ones": np.ones((P, P)),
             "mean": np.full((P, 1), 1.0),
             "head2": np.stack([i < HD, i >= HD], 1),
             "head2_scaled": np.stack([i < HD, i >= HD], 1) * HD ** -0.5,
             "blk": row // HD == col // HD,
             "blkmean": (row // HD == col // HD) / HD}
    rot = np.zeros((P, P))
    rot[i[:HD] + HD, i[:HD]] = -1.0
    rot[i[:HD], i[:HD] + HD] = 1.0
    parts["rot"] = rot
    parts["neg_q"] = np.where(col <= row, 0.0, NEG)
    parts["neg_k"] = np.where(row <= col, 0.0, NEG)
    parts["incl"] = row <= col
    parts["strict_t"] = row < col
    parts["strict"] = row > col
    for level in range(7):
        b = 1 << level
        m = (row // (2 * b) == col // (2 * b)) & (row % (2 * b) >= b) & (col % (2 * b) < b)
        parts[f"level{level}"] = m
        if level == 0:
            parts["level0_t"] = m.T
    half = HD
    parts["freq"] = (10000.0 ** (-(i % half).astype(np.float64) / half))[:, None]
    parts["sign"] = np.where(i < DTF_F, 1.0, -1.0)[:, None]
    at, where, arrays = 0, {}, []
    for name, a in parts.items():
        where[name] = (at, a.shape[1])
        at += a.shape[1]
        arrays.append(np.asarray(a, np.float32))
    return where, np.concatenate(arrays, 1)


CONST, CONST_ARRAY = const_tables()


def decay_table():
    out = np.zeros((P, RET_HEADS, T), np.float64)
    d = np.arange(T)[None, :] - np.arange(P)[:, None]
    for h in range(RET_HEADS):
        out[:, h] = np.where(d >= 0, (1.0 - 2.0 ** (-5.0 - h)) ** np.maximum(d, 0), 0.0) * P ** -0.5
    return out.astype(np.float32)


def bucket_table():
    out = np.zeros((P, DIL, NREL), np.float32)
    e = 255 - np.arange(NREL)
    exact = BUCKETS // 2
    for g, (window, dil) in enumerate(((128, 1), (512, 4), (2048, 16))):
        dist = e * (1 if g == 0 else 4)
        ok = (dist >= 0) & (dist % dil == 0) & (dist // dil <= window // dil)
        f = np.maximum(dist, 1).astype(np.float32)
        large = exact + (np.log(f / np.float32(exact)) / np.float32(np.log(2048 / exact))
                         * np.float32(BUCKETS - exact)).astype(np.int32)
        bucket = np.where(dist < exact, dist, np.minimum(large, BUCKETS - 1))
        for x in range(NREL):
            out[bucket[x] if ok[x] else BUCKETS, g, x] = 1.0
    return out


class Signal:

    def __init__(self, handle):
        self.handle, self.total, self.base = handle, 0, 0

    def inc(self, k=1):
        self.total += k
        return self.handle, k

    def ge(self, n):
        return self.handle, self.base + n

    def so_far(self):
        return self.handle, self.total


def rep(ap, n):
    return bass.AP(ap.tensor, ap.offset, [*[list(d) for d in ap.ap], [0, n]])


def tiled(ap, n):
    first, *rest = [list(d) for d in ap.ap]
    return bass.AP(ap.tensor, ap.offset, [first, [0, n], *rest])


class Core:

    def __init__(self, nc, ctx, dram):
        self.nc, self.dram, self.ctx = nc, dram, ctx
        self.signals = {}
        self.stream = dram["stream"]
        self.piece = 0
        self.ring = [self.sb(f"ring{s}", [P, KF, P]) for s in range(RING)]
        self.const = self.sb("const", [P, CONST_ARRAY.shape[1]])
        self.vec = self.sb("vec", [P, NVEC])
        self.x = self.sb("x", [P, KD, T])
        self.xn = self.sb("xn", [P, KD, T])
        self.acc = [ctx.enter_context(nc.psum_tensor(f"acc{s}", [P, T], F32)) for s in range(RING)]
        self.aux = [ctx.enter_context(nc.psum_tensor(f"aux{s}", [P, T], F32)) for s in range(4)]
        self.weights_ready = [self.sig(f"weights_ready{s}") for s in range(RING)]
        self.tile_done = self.sig("tile_done")
        self.bank_free = self.sig("bank_free")
        self.dve_order = self.sig("dve_order")
        self.act_order = self.sig("act_order")
        self.pool_order = self.sig("pool_order")
        self.loaded = self.sig("loaded")

    def sb(self, name, shape, dtype=F32, ctx=None):
        return (ctx or self.ctx).enter_context(self.nc.sbuf_tensor(name, shape, dtype))

    def sig(self, name):
        if name not in self.signals:
            self.signals[name] = Signal(self.ctx.enter_context(self.nc.semaphore(name)))
        return self.signals[name]

    def c(self, name, rows=P):
        at, n = CONST[name]
        return self.const[0:rows, at:at + n]

    def v(self, name, j=0, rows=P):
        at, _ = VEC[name]
        return self.vec[0:rows, at + j:at + j + 1]

    @contextmanager
    def phase(self):
        for s in self.signals.values():
            s.base = s.total
        with self.nc.Block() as block:
            yield block

    def load_piece(self, sp, g, index=None):
        tensor, at, k = self.stream[g]
        src = self.dram[tensor][at] if index is None else \
            self.dram[tensor][bass.ds(index, 1)].rearrange("a p n -> (a p) n")
        dst = self.ring[g % RING][:, 0:k, :].rearrange("p k m -> p (k m)")
        sp.dma_start(dst, src).then_inc(*self.weights_ready[g % RING].inc(16))

    def stream_ahead(self, sp, count):
        g, end = self.piece, self.piece + count
        last = len(self.stream)
        while g < end and g + RING < last:
            tensor, at, k = self.stream[g + RING]
            run = 0
            while g + run < end and g + run + RING < last and \
                    self.stream[g + run + RING] == (tensor, at + run, k):
                run += 1
            loops = run // RING
            if loops >= 2:
                with sp.Fori(0, loops) as i:
                    for u in range(RING):
                        sp.wait_ge(self.tile_done.handle, i * RING + (g + u + 1))
                        self.load_piece(sp, g + u + RING, i * RING + (at + u))
                for u in range(RING):
                    self.weights_ready[(g + u) % RING].total += 16 * (loops - 1)
                g += loops * RING
            else:
                for u in range(min(run, RING)):
                    sp.wait_ge(self.tile_done.handle, g + u + 1)
                    self.load_piece(sp, g + u + RING)
                g += min(run, RING)

    def linear(self, pe, start, count, moving, n=T):
        g0 = self.piece + start

        def one(g, i, per):
            s = g % RING
            k_tiles = self.stream[g][2]
            pe.wait_ge(self.weights_ready[s].handle, i * (16 * per // RING) + 16 * (g // RING + 1))
            pe.wait_ge(self.bank_free.handle, i * per + (g + 1))
            for k in range(k_tiles):
                mm = pe.matmul(self.acc[s][:, 0:n], self.ring[s][:, k, :], moving(k),
                               start=(k == 0), stop=(k == k_tiles - 1))
            mm.then_inc(self.tile_done.handle, 1)

        loops = count // RING
        if loops >= 2:
            with pe.Fori(0, loops) as i:
                for u in range(RING):
                    one(g0 + u, i, RING)
        else:
            loops = 0
        for j in range(loops * RING, count):
            one(g0 + j, 0, RING)
        self.tile_done.total += count

    def read_out(self, eng, start, count, body, per_piece=1, free=True):
        g0 = self.piece + start
        units = count // per_piece
        step = RING // per_piece

        def one(j, i):
            g = g0 + j * per_piece
            eng.wait_ge(self.tile_done.handle, i * RING + (g + per_piece))
            banks = [self.acc[(g + q) % RING] for q in range(per_piece)]
            last = body(i * step + j, *banks)
            if free:
                last.then_inc(self.bank_free.handle, per_piece)

        loops = units // step
        if loops >= 2:
            with eng.Fori(0, loops) as i:
                for j in range(step):
                    one(j, i)
        else:
            loops = 0
        for j in range(loops * step, units):
            one(j, 0)
        if free:
            self.bank_free.total += count

    def end_linear(self, count):
        self.piece += count


def at(buf, j, lo=0, hi=T):
    if isinstance(j, int):
        return buf[:, j, lo:hi]
    return buf[:, bass.ds(j, 1), lo:hi].rearrange("p a t -> p (a t)")

SECOND = True


def column(ap, n=P):
    return bass.AP(ap.tensor, ap.offset, [list(ap.ap[0]), [0, n]])


def norm(core, tiles, kind, scale, finish, eps=EPS, floor=None, n=T):
    nj, nt = len(tiles), n // P
    per = {"all": 0, "tile": 1, "half": 2}[kind]
    cols = max(1, per * nj)
    squares, sums, roots = core.squares, core.sums, core.roots
    sq_act, sq_dve = core.sig("squares_act"), core.sig("squares_dve")
    summed, eps_added, rooted = core.sig("summed"), core.sig("eps_added"), core.sig("rooted")
    inverse, spread, applied = core.sig("inverse"), core.sig("spread"), core.sig("applied")
    stats = core.aux[0]
    banks = core.aux[1:4]
    n_spread = 1 if kind == "all" else nj

    with core.phase() as block:
        @block.scalar
        def _(act):
            for j in range(0, nj, 2):
                act.activation(squares[:, j, 0:n], tiles[j], ACT.Square).then_inc(*sq_act.inc())
            act.wait_ge(*eps_added.ge(1))
            act.activation(roots[:, 0:nt * cols], sums[:, 0:nt * cols], ACT.Sqrt).then_inc(*rooted.inc())

        @block.tensor
        def _(pe):
            pe.wait_ge(*sq_act.ge((nj + 1) // 2))
            if nj > 1:
                pe.wait_ge(*sq_dve.ge(nj // 2))
            for t in range(nt):
                for j in range(nj):
                    w = max(1, per)
                    c0 = t * cols + (j * per if per else 0)
                    rhs = core.c("head2") if kind == "half" else core.c("mean")
                    mm = pe.matmul(stats[:, c0:c0 + w], squares[:, j, t * P:(t + 1) * P], rhs,
                                   start=(j == 0 or per > 0), stop=(j == nj - 1 or per > 0))
            mm.then_inc(*summed.inc())
            pe.wait_ge(*inverse.ge(1))
            for j in range(n_spread):
                if j >= 3:
                    pe.wait_ge(*applied.ge(j - 2))
                for t in range(nt):
                    c0 = t * cols + j * per
                    parts = max(1, per)
                    for e in range(parts):
                        rows = slice(e * P // parts, (e + 1) * P // parts)
                        mm = pe.matmul(banks[j % 3][rows, t * P:(t + 1) * P],
                                       column(sums[:, c0 + e:c0 + e + 1], P // parts),
                                       core.c("ident"), start=True, stop=True)
                mm.then_inc(*spread.inc())

        @block.vector
        def _(dve):
            for j in range(1, nj, 2):
                dve.tensor_tensor(squares[:, j, 0:n], tiles[j], tiles[j], ALU.mult).then_inc(*sq_dve.inc())
            dve.wait_ge(*summed.ge(1))
            dve.tensor_scalar(sums[:, 0:nt * cols], stats[:, 0:nt * cols], 1.0 if floor else scale,
                              0.0 if floor else eps, ALU.mult, ALU.add).then_inc(*eps_added.inc())
            dve.wait_ge(*rooted.ge(1))
            if floor:
                dve.tensor_scalar(roots[:, 0:nt * cols], roots[:, 0:nt * cols], floor, None,
                                  ALU.max).then_inc(*core.dve_order.inc())
                dve.wait_ge(*core.dve_order.so_far())
            dve.reciprocal(sums[:, 0:nt * cols], roots[:, 0:nt * cols]).then_inc(*inverse.inc())
            for j in range(nj):
                dve.wait_ge(*spread.ge(1 if kind == "all" else j + 1))
                bank = banks[0 if kind == "all" else j % 3]
                finish(dve, j, bank[:, 0:n]).then_inc(*applied.inc())


def gained(core, dst, src, gain):
    def finish(dve, j, bank):
        return dve.scalar_tensor_tensor(out=dst(j), in0=src(j), scalar=gain(j), in1=bank,
                                        op0=ALU.mult, op1=ALU.mult)
    return finish


def rms_all(core, gain):
    norm(core, [core.x[:, k, :] for k in range(KD)], "all", 1.0 / D,
         gained(core, lambda j: core.xn[:, j, :], lambda j: core.x[:, j, :], lambda j: core.v(gain, j)))


def setup(core):
    dram = core.dram
    cond = core.sig("cond_ready")
    with core.phase() as block:
        @block.sync
        def _(sp):
            for dst, src in ((core.const[:, :], dram["const"]), (core.vec[:, :], dram["vec"]),
                             (core.cond[:, :], dram["c"])):
                sp.dma_start(dst, src).then_inc(*core.loaded.inc(16))
            for g in range(RING):
                core.load_piece(sp, g)
            sp.dma_start(core.x[:, :, :], dram["x"]).then_inc(*core.loaded.inc(16))
            sp.wait_ge(*core.loaded.ge(64))

        @block.vector
        def _(dve):
            dve.sem_inc(*core.bank_free.inc(RING))

        @block.scalar
        def _(act):
            act.wait_ge(*core.loaded.ge(64))
            act.activation(core.cond[:, :], core.cond[:, :], ACT.Silu).then_inc(*cond.inc())
            act.wait_ge(*cond.ge(1))


def modulation(core):
    n = DEPTH * 3 * KD
    b0 = [VEC[f"b_ada{l}"][0] for l in range(DEPTH)]
    for l in range(DEPTH):
        count = 3 * KD
        with core.phase() as block:
            @block.sync
            def _(sp):
                core.stream_ahead(sp, count)

            @block.tensor
            def _(pe):
                core.linear(pe, 0, count, lambda k: core.cond[:, k:k + 1], n=1)

            @block.scalar
            def _(act):
                def body(j, bank):
                    bias = core.vec[:, bass.ds(j + b0[l], 1)] if not isinstance(j, int) else \
                        core.vec[:, b0[l] + j:b0[l] + j + 1]
                    dst = core.mod[:, l, bass.ds(j, 1)] if not isinstance(j, int) else core.mod[:, l, j:j + 1]
                    return act.activation(dst, bank[:, 0:1], ACT.Identity, bias=bias)
                core.read_out(act, 0, count, body)
        core.end_linear(count)


def layer_norm_in(core, l):
    gs = core.gs
    made = core.sig("gs_made")
    with core.phase() as block:
        @block.vector
        def _(dve):
            g0 = VEC[f"norm_g{l}"][0]
            dve.scalar_tensor_tensor(out=gs[:, :], in0=core.mod[:, l, KD:2 * KD], scalar=1.0,
                                     in1=core.vec[:, g0:g0 + KD], op0=ALU.add,
                                     op1=ALU.mult).then_inc(*made.inc())
    norm(core, [core.x[:, k, :] for k in range(KD)], "all", 1.0 / D,
         gained(core, lambda j: core.xn[:, j, :], lambda j: core.x[:, j, :], lambda j: gs[:, j:j + 1]))
    shifted = core.sig("shifted")
    with core.phase() as block:
        @block.scalar
        def _(act):
            for j in range(0, KD, 2):
                act.activation(core.xn[:, j, :], core.xn[:, j, :], ACT.Identity,
                               bias=core.mod[:, l, j:j + 1]).then_inc(*shifted.inc())

        @block.vector
        def _(dve):
            for j in range(1, KD, 2):
                dve.tensor_scalar(core.xn[:, j, :], core.xn[:, j, :], core.mod[:, l, j:j + 1], None,
                                  ALU.add).then_inc(*shifted.inc())


def project(core, moving, segments, n=T):
    count = sum(s[0] for s in segments)
    with core.phase() as block:
        @block.sync
        def _(sp):
            core.stream_ahead(sp, count)

        @block.tensor
        def _(pe):
            start = 0
            for c, _, _ in segments:
                core.linear(pe, start, c, moving, n)
                start += c

        @block.scalar
        def _(act):
            start = 0
            for c, make in [(s[0], s[2]) for s in segments]:
                core.read_out(act, start, c, lambda j, bank: make(act, j, bank[:, 0:n]))
                start += c
    core.end_linear(count)


def copy_to(buf, lo=0, hi=T, scale=1.0, func=ACT.Copy):
    return lambda act, j, bank: act.activation(at(buf, j, lo, hi), bank, func, scale=scale)


def token_major(core, src, count, dst, n=T, tag="v"):
    turned, stored = core.sig("turned"), core.sig("stored")
    units = [(t, j0) for t in range(n // P) for j0 in range(0, count, 4)]
    with core.phase() as block:
        @block.tensor
        def _(pe):
            for u, (t, j0) in enumerate(units):
                if u >= 4:
                    pe.wait_ge(*stored.ge(u - 3))
                for j in range(j0, min(j0 + 4, count)):
                    mm = pe.transpose(core.aux[u % 4][:, (j - j0) * P:(j - j0 + 1) * P],
                                      src(j)[:, t * P:(t + 1) * P], core.c("ident"))
                mm.then_inc(*turned.inc())

        @block.vector
        def _(dve):
            for u, (t, j0) in enumerate(units):
                w = (min(j0 + 4, count) - j0) * P
                dve.wait_ge(*turned.ge(u + 1))
                dve.tensor_copy(dst[:, t, j0 * P:j0 * P + w],
                                core.aux[u % 4][:, 0:w]).then_inc(*stored.inc())


def feature_major(core, src, count, dst, order=None, after=None):
    turned, stored = core.sig("turned"), core.sig("stored")
    with core.phase() as block:
        @block.tensor
        def _(pe):
            for j in range(count):
                if j >= 4:
                    pe.wait_ge(*stored.ge(j - 3))
                for t in range(NT):
                    out = core.aux[j % 4][:, t * P:(t + 1) * P]
                    mm = pe.transpose(out, src[:, t, j * P:(j + 1) * P], core.c("ident"))
                mm.then_inc(*turned.inc())

        @block.vector
        def _(dve):
            for j in range(count):
                dve.wait_ge(*turned.ge(j + 1))
                after(dve, j, core.aux[j % 4][:, :]).then_inc(*stored.inc())


def retention(core, l, mixed, ctx):
    qk = core.squares
    v = core.sb(f"ret_v{l}", [P, RET_HEADS, T], ctx=ctx)
    v_tok = core.sb(f"ret_vtok{l}", [P, NT, RET_HEADS * P], ctx=ctx)
    o = v
    decay = core.sb(f"ret_decay{l}", [P, RET_HEADS, T], ctx=ctx)
    part = core.sb(f"ret_part{l}", [P, 2, T], ctx=ctx)
    part2 = core.sb(f"ret_part2{l}", [P, 2, T], ctx=ctx)
    weights = core.sb(f"ret_w{l}", [P, 2, T], ctx=ctx)
    project(core, lambda k: core.xn[:, k, :], [
        (2 * RET_HEADS, None, copy_to(qk)),
        (RET_HEADS, None, copy_to(v)),
        (RET_HEADS, None, copy_to(mixed, func=ACT.Silu))])

    swapped, cosed, sined, turned = (core.sig(s) for s in ("rot_swapped", "rot_cos", "rot_sin", "rot_done"))
    with core.phase() as block:
        @block.sync
        def _(sp):
            sp.dma_start(decay[:, :, :], core.dram["decay"]).then_inc(*core.loaded.inc(16))
            sp.wait_ge(*core.loaded.ge(16))

        @block.tensor
        def _(pe):
            for j in range(2 * RET_HEADS):
                if j >= 2:
                    pe.wait_ge(*sined.ge(j - 1))
                pe.matmul(core.aux[j % 2][:, :], core.c("rot"), qk[:, j, :], start=True,
                          stop=True).then_inc(*swapped.inc())

        @block.gpsimd
        def _(pool):
            for j in range(2 * RET_HEADS):
                if j >= 2:
                    pool.wait_ge(*turned.ge(j - 1))
                pool.tensor_tensor(part[:, j % 2, :], qk[:, j, :], core.cos[:, :],
                                   ALU.mult).then_inc(*cosed.inc())

        @block.vector
        def _(dve):
            for j in range(2 * RET_HEADS):
                dve.wait_ge(*swapped.ge(j + 1))
                if j >= 2:
                    dve.wait_ge(*turned.ge(j - 1))
                dve.tensor_tensor(part2[:, j % 2, :], core.aux[j % 2][:, :], core.sin[:, :],
                                  ALU.mult).then_inc(*sined.inc())
                dve.wait_ge(*sined.ge(j + 1))
                dve.wait_ge(*cosed.ge(j + 1))
                dve.tensor_tensor(qk[:, j, :], part[:, j % 2, :], part2[:, j % 2, :],
                                  ALU.add).then_inc(*turned.inc())
    token_major(core, lambda j: v[:, j, :], RET_HEADS, v_tok)

    scored, weighted, summed, kept = (core.sig(s) for s in ("ret_scored", "ret_weighted", "ret_summed", "ret_kept"))
    units = [(h, jt) for h in range(RET_HEADS) for jt in range(NT)]
    with core.phase() as block:
        @block.tensor
        def _(pe):
            def score(u):
                h, jt = units[u]
                if u >= 2:
                    pe.wait_ge(*weighted.ge(u - 1))
                pe.matmul(core.aux[u % 2][:, 0:T - jt * P], qk[:, RET_HEADS + h, jt * P:(jt + 1) * P],
                          qk[:, h, jt * P:T], start=True, stop=True).then_inc(*scored.inc())

            score(0)
            for u, (h, jt) in enumerate(units):
                if u + 1 < len(units):
                    score(u + 1)
                pe.wait_ge(*weighted.ge(u + 1))
                if jt == 0 and h >= 2:
                    pe.wait_ge(*kept.ge(h - 1))
                mm = pe.matmul(core.aux[2 + h % 2][:, jt * P:T], v_tok[:, jt, h * P:(h + 1) * P],
                               weights[:, u % 2, 0:T - jt * P], start=(jt == 0), stop=(jt == NT - 1))
                mm.then_inc(*summed.inc())

        @block.vector
        def _(dve):
            for u, (h, jt) in enumerate(units):
                n = T - jt * P
                dve.wait_ge(*scored.ge(u + 1))
                if u >= 2:
                    dve.wait_ge(*summed.ge(u - 1))
                dve.tensor_tensor(weights[:, u % 2, 0:n], core.aux[u % 2][:, 0:n], decay[:, h, 0:n],
                                  ALU.mult).then_inc(*weighted.inc())

        @block.scalar
        def _(act):
            for h in range(RET_HEADS):
                act.wait_ge(*summed.ge(NT * (h + 1)))
                act.activation(o[:, h, :], core.aux[2 + h % 2][:, :], ACT.Copy).then_inc(*kept.inc())

    def finish(dve, j, bank):
        dve.tensor_tensor(o[:, j, :], o[:, j, :], bank, ALU.mult).then_inc(*core.dve_order.inc())
        dve.wait_ge(*core.dve_order.so_far())
        return dve.tensor_tensor(mixed[:, j, :], o[:, j, :], mixed[:, j, :], ALU.mult)
    norm(core, [o[:, h, :] for h in range(RET_HEADS)], "tile", 1.0 / P, finish)


def ssd(core, l, mixed, ctx):
    xbc = core.sb(f"ssd_in{l}", [P, NXBC, CONV_K - 1 + T], ctx=ctx)
    raw = core.sb(f"dtf{l}", [P, T], ctx=ctx)
    work = core.squares
    tiny = core.sb(f"ssd_tiny{l}", [P, 4], ctx=ctx)
    w = [work[0:NDTF, i, :] for i in range(4)]
    zeroed = core.sig("zeroed")
    with core.phase() as block:
        @block.vector
        def _(dve):
            dve.memset(xbc[:, :, 0:CONV_K - 1], 0.0).then_inc(*zeroed.inc())
    project(core, lambda k: core.xn[:, k, :], [
        (NXBC, None, copy_to(xbc, CONV_K - 1, CONV_K - 1 + T)),
        (8, None, lambda act, j, bank: act.activation(at(mixed, j + SSD_T), bank, ACT.Silu)),
        (1, None, lambda act, j, bank: act.activation(raw[:, :], bank, ACT.Copy))])

    conv, smooth, soft = core.sig("conv_acc"), core.sig("conv_done"), core.sig("soft_act")
    bias_made, z_made = core.sig("soft_bias"), core.sig("soft_z")
    acc = work[:, 4:6, :]
    out = xbc[:, :, CONV_K - 1:CONV_K - 1 + T]
    with core.phase() as block:
        @block.scalar
        def _(act):
            for j in range(NXBC):
                if j >= 2:
                    act.wait_ge(*smooth.ge(j - 1))
                    act.activation(out[:, j - 2, :], acc[:, j % 2, :], ACT.Silu
                                   ).then_inc(*core.act_order.inc())
                    act.wait_ge(*core.act_order.so_far())
                act.activation(acc[:, j % 2, :], xbc[:, j, 3:3 + T], ACT.Identity,
                               scale=core.v(f"conv_w{l}_3", j), bias=core.v(f"conv_b{l}", j)
                               ).then_inc(*conv.inc())
            for j in range(NXBC - 2, NXBC):
                act.wait_ge(*smooth.ge(j + 1))
                act.activation(out[:, j, :], acc[:, j % 2, :], ACT.Silu).then_inc(*core.act_order.inc())

        @block.vector
        def _(dve):
            order = core.dve_order
            for j in range(NXBC):
                dve.wait_ge(*conv.ge(j + 1))
                for k in (2, 1):
                    dve.scalar_tensor_tensor(out=acc[:, j % 2, :], in0=xbc[:, j, k:k + T],
                                             scalar=core.v(f"conv_w{l}_{k}", j), in1=acc[:, j % 2, :],
                                             op0=ALU.mult, op1=ALU.add).then_inc(*order.inc())
                    dve.wait_ge(*order.so_far())
                dve.scalar_tensor_tensor(out=acc[:, j % 2, :], in0=xbc[:, j, 0:T],
                                         scalar=core.v(f"conv_w{l}_0", j), in1=acc[:, j % 2, :],
                                         op0=ALU.mult, op1=ALU.add).then_inc(*smooth.inc())

    z, e, lw, d = w
    exped, dt_ready = core.sig("soft_exp"), core.sig("soft_w")
    with core.phase() as block:
        @block.scalar
        def _(act):
            act.wait_ge(*bias_made.ge(1))
            act.activation(z, raw[0:NDTF, :], ACT.Identity, scale=core.c("sign", NDTF),
                           bias=tiny[0:NDTF, 0:1]).then_inc(*soft.inc())
            act.activation(tiny[0:NDTF, 1:2], core.v(f"a_log{l}", 0, NDTF), ACT.Exp).then_inc(*soft.inc())
            act.wait_ge(*z_made.ge(1))
            act.activation(e, e, ACT.Exp, scale=-1.0).then_inc(*exped.inc())
            act.wait_ge(*dt_ready.ge(1))
            act.activation(lw, lw, ACT.Ln).then_inc(*exped.inc())

        @block.vector
        def _(dve):
            order = core.dve_order

            def step(ins):
                ins.then_inc(*order.inc())
                dve.wait_ge(*order.so_far())

            dve.tensor_tensor(tiny[0:NDTF, 0:1], core.v(f"dtf_b{l}", 0, NDTF), core.c("sign", NDTF),
                              ALU.mult).then_inc(*bias_made.inc())
            dve.memset(core.cum[:, :, :], 0.0).then_inc(*order.inc())
            dve.wait_ge(*soft.ge(2))
            dve.scalar_tensor_tensor(out=e, in0=z, scalar=-1.0, in1=z, op0=ALU.mult,
                                     op1=ALU.max).then_inc(*z_made.inc())
            step(dve.tensor_scalar(tiny[0:NDTF, 1:2], tiny[0:NDTF, 1:2], -1.0, None, ALU.mult))
            dve.wait_ge(*exped.ge(1))
            step(dve.tensor_scalar(lw, e, 1.0, None, ALU.add))
            dve.tensor_scalar(d, lw, -1.0, None, ALU.add).then_inc(*dt_ready.inc())
            dve.wait_ge(*exped.ge(2))
            step(dve.scalar_tensor_tensor(out=lw, in0=d, scalar=0.0, in1=lw, op0=ALU.is_equal, op1=ALU.add))
            step(dve.scalar_tensor_tensor(out=d, in0=d, scalar=0.0, in1=d, op0=ALU.is_equal, op1=ALU.add))
            step(dve.tensor_tensor(lw, lw, e, ALU.mult))
            step(dve.reciprocal(d, d))
            step(dve.tensor_tensor(lw, lw, d, ALU.mult))
            step(dve.scalar_tensor_tensor(out=z, in0=z, scalar=0.0, in1=lw, op0=ALU.max, op1=ALU.add))
            step(dve.tensor_scalar(d, z, tiny[0:NDTF, 1:2], None, ALU.mult))
            ones = tiled(core.c("ones"), NT)
            ones16 = core.ones_row[0:SSD_HEADS, :]
            for b in range(NT):
                dve.tensor_tensor_scan(core.cum[0:SSD_HEADS, b, b * P:T], ones16[:, b * P:T],
                                       d[0:SSD_HEADS, b * P:T], 0.0, ALU.mult, ALU.add).then_inc(*order.inc())
            dve.tensor_tensor_scan(core.cum[DTF_F:DTF_F + FOX_HEADS, 0, :],
                                   core.ones_row[DTF_F:DTF_F + FOX_HEADS, :],
                                   d[DTF_F:DTF_F + FOX_HEADS, :], 0.0, ALU.mult,
                                   ALU.add).then_inc(*order.inc())
    dt = z

    xdt = core.squares[:, :, :].rearrange("p (b k) t -> p b (k t)", b=NT)
    dt_tok = core.sb(f"ssd_dt{l}", [P, NT, NDTF], ctx=ctx)
    ncum = core.sb(f"ssd_ncum{l}", [P, NT, NDTF], ctx=ctx)
    cb_at = [0, T, 2 * T - P, 3 * T - 3 * P]
    cb = core.sb(f"ssd_cb{l}", [P, SSD_GROUPS, 4 * T - 6 * P], ctx=ctx)
    made, cols = core.sig("col_turned"), core.sig("col_stored")
    with core.phase() as block:
        @block.tensor
        def _(pe):
            for b in range(NT):
                pe.transpose(core.aux[0][:, b * NDTF:(b + 1) * NDTF], dt[:, b * P:(b + 1) * P],
                             core.c("ident", NDTF)[:, 0:NDTF])
                pe.transpose(core.aux[0][:, (NT + b) * NDTF:(NT + b + 1) * NDTF],
                             core.cum[0:NDTF, b, b * P:(b + 1) * P],
                             core.c("ident", NDTF)[:, 0:NDTF]).then_inc(*made.inc())
            u = 0
            for g in range(SSD_GROUPS):
                for b in range(NT):
                    bank = core.aux[1 + u % 3]
                    if u >= 3:
                        pe.wait_ge(*cols.ge(2 + u - 2))
                    pe.matmul(bank[:, 0:T - b * P], out[:, 8 + g, b * P:(b + 1) * P],
                              out[:, 10 + g, b * P:T], start=True, stop=True).then_inc(*made.inc())
                    u += 1

        @block.vector
        def _(dve):
            dve.wait_ge(*made.ge(NT))
            dve.tensor_copy(dt_tok[:, :, :].rearrange("p b c -> p (b c)"),
                            core.aux[0][:, 0:NT * NDTF]).then_inc(*cols.inc())
            dve.tensor_scalar(ncum[:, :, :].rearrange("p b c -> p (b c)"),
                              core.aux[0][:, NT * NDTF:2 * NT * NDTF], -1.0, None,
                              ALU.mult).then_inc(*cols.inc())
            u = 0
            for g in range(SSD_GROUPS):
                for b in range(NT):
                    dve.wait_ge(*made.ge(NT + u + 1))
                    dve.tensor_copy(cb[:, g, cb_at[b]:cb_at[b] + T - b * P],
                                    core.aux[1 + u % 3][:, 0:T - b * P]).then_inc(*cols.inc())
                    u += 1
    turned, stored = core.sig("turned"), core.sig("stored")
    units = [(b, g) for b in range(NT) for g in range(2)]
    with core.phase() as block:
        @block.tensor
        def _(pe):
            for u, (b, g) in enumerate(units):
                if u >= 4:
                    pe.wait_ge(*stored.ge(u - 3))
                for j in range(4):
                    mm = pe.transpose(core.aux[u % 4][:, j * P:(j + 1) * P],
                                      out[:, 4 * g + j, b * P:(b + 1) * P], core.c("ident"))
                mm.then_inc(*turned.inc())

        @block.vector
        def _(dve):
            for u, (b, g) in enumerate(units):
                dve.wait_ge(*turned.ge(u + 1))
                dve.tensor_tensor(
                    xdt[:, b, g * T:(g + 1) * T].rearrange("p (h d) -> p h d", d=SSD_DIM),
                    core.aux[u % 4][:, :].rearrange("p (h d) -> p h d", d=SSD_DIM),
                    rep(dt_tok[:, b, 8 * g:8 * g + 8], SSD_DIM), ALU.mult).then_inc(*stored.inc())

    spread, exps, weighted, summed, kept = (core.sig(s) for s in (
        "ssd_spread", "ssd_exp", "ssd_weighted", "ssd_summed", "ssd_kept"))
    ex = core.sb(f"ssd_ex{l}", [P, 4, T], ctx=ctx)
    y = core.sb(f"ssd_y{l}", [P, 2, T], ctx=ctx)
    units = [(h, b) for h in range(SSD_HEADS) for b in range(NT)]
    with core.phase() as block:
        @block.tensor
        def _(pe):
            def decay(u):
                h, b = units[u]
                n = T - b * P
                if u >= 4:
                    pe.wait_ge(*exps.ge(u - 3))
                bank = core.aux[u % 4]
                pe.matmul(bank[:, 0:n], column(core.c("ident")[:, h:h + 1]),
                          core.cum[:, b, b * P:T], start=True, stop=False)
                pe.matmul(bank[:, 0:P], core.c("ident"), core.c("neg_k"), start=False, stop=True
                          ).then_inc(*spread.inc())

            for u in range(2):
                decay(u)
            for u, (h, b) in enumerate(units):
                if u + 2 < len(units):
                    decay(u + 2)
                pe.wait_ge(*weighted.ge(u + 1))
                pair, half = h // 2, h % 2
                if b == 0 and half == 0 and pair >= 4:
                    pe.wait_ge(*kept.ge(pair - 3))
                mm = pe.matmul(core.acc[pair % 4][half * HD:half * HD + HD, b * P:T],
                               xdt[:, b, h * SSD_DIM:(h + 1) * SSD_DIM], ex[:, u % 4, 0:T - b * P],
                               start=(b == 0), stop=(b == NT - 1))
                mm.then_inc(*summed.inc())

        @block.scalar
        def _(act):
            for u, (h, b) in enumerate(units):
                n = T - b * P
                act.wait_ge(*spread.ge(u + 1))
                if u >= 4:
                    act.wait_ge(*summed.ge(u - 3))
                act.activation(ex[:, u % 4, 0:n], core.aux[u % 4][:, 0:n], ACT.Exp,
                               bias=ncum[:, b, h:h + 1]).then_inc(*exps.inc())

        @block.vector
        def _(dve):
            for u, (h, b) in enumerate(units):
                n = T - b * P
                dve.wait_ge(*exps.ge(u + 1))
                dve.tensor_tensor(ex[:, u % 4, 0:n], ex[:, u % 4, 0:n], cb[:, h // 8, cb_at[b]:cb_at[b] + n],
                                  ALU.mult).then_inc(*weighted.inc())
                if h % 2 == 1 and b == NT - 1:
                    pair = h // 2
                    dve.wait_ge(*summed.ge(u + 1))
                    dve.scalar_tensor_tensor(out=y[:, pair % 2, :], in0=out[:, pair, :],
                                             scalar=core.v(f"d_skip{l}", pair), in1=core.acc[pair % 4][:, :],
                                             op0=ALU.mult, op1=ALU.add).then_inc(*kept.inc())
                    dve.wait_ge(*kept.ge(pair + 1))
                    dve.tensor_tensor(mixed[:, SSD_T + pair, :], y[:, pair % 2, :], mixed[:, SSD_T + pair, :],
                                      ALU.mult).then_inc(*core.dve_order.inc())
    norm(core, [mixed[:, SSD_T + j, :] for j in range(8)], "all", 1.0 / 1024,
         gained(core, lambda j: mixed[:, SSD_T + j, :], lambda j: mixed[:, SSD_T + j, :],
                lambda j: core.v(f"ssd_g{l}", j)))


def attention_buffers(core, name, ctx):
    core.att_probs = core.sb(name + "_probs", [P, 2, T], ctx=ctx)
    core.att_probs_t = core.sb(name + "_probs_t", [P, 2, T], ctx=ctx)


def attention(core, units, out_tok):
    scored, maxed, exped, turned, copied, summed, kept = (core.sig("att_" + s) for s in (
        "scored", "maxed", "exped", "turned", "copied", "summed", "kept"))
    order = core.dve_order
    probs, probs_t = core.att_probs, core.att_probs_t
    small = core.att_small
    N = len(units)
    with core.phase() as block:
        @block.tensor
        def _(pe):
            def score(u):
                if u >= 2:
                    pe.wait_ge(*exped.ge(u - 1))
                parts = units[u]["scores"]
                for q, (lhsT, rhs, lo) in enumerate(parts):
                    n = rhs.free_size()
                    mm = pe.matmul(core.aux[u % 2][:, lo:lo + n], lhsT, rhs, start=(q == 0),
                                   stop=(q == len(parts) - 1), skip_group_check=True)
                mm.then_inc(*scored.inc())

            def turn(u):
                pe.wait_ge(*exped.ge(u + 1))
                if u >= 2:
                    pe.wait_ge(*copied.ge(u - 1))
                for b in range(units[u]["keys"] // P):
                    mm = pe.transpose(core.aux[2 + u % 2][:, b * P:(b + 1) * P],
                                      probs[:, u % 2, b * P:(b + 1) * P], core.c("ident"))
                mm.then_inc(*turned.inc())

            def values(u):
                pe.wait_ge(*copied.ge(u + 1))
                if u >= 4:
                    pe.wait_ge(*kept.ge(u - 3))
                vs = units[u]["values"]
                for b, v in enumerate(vs):
                    mm = pe.matmul(core.acc[u % 4][:, 0:HD], probs_t[:, u % 2, b * P:(b + 1) * P], v,
                                   start=(b == 0), stop=(b == len(vs) - 1))
                mm.then_inc(*summed.inc())

            for s in range(N + 2):
                if s < N:
                    score(s)
                if 1 <= s <= N:
                    turn(s - 1)
                if s >= 2:
                    values(s - 2)

        @block.scalar
        def _(act):
            def exp(u):
                n = units[u]["keys"]
                act.wait_ge(*maxed.ge(u + 1))
                if u >= 2:
                    act.wait_ge(*turned.ge(u - 1))
                if u >= 4:
                    act.wait_ge(*kept.ge(u - 3))
                total = units[u].get("sum", small[:, 4 + u % 4:5 + u % 4])
                act.activation(probs[:, u % 2, 0:n], core.aux[u % 2][:, 0:n], ACT.Exp,
                               bias=small[:, u % 4:u % 4 + 1], accum_out=total).then_inc(*exped.inc())

            def copy(u):
                n = units[u]["keys"]
                act.wait_ge(*turned.ge(u + 1))
                if u >= 2:
                    act.wait_ge(*summed.ge(u - 1))
                act.activation(probs_t[:, u % 2, 0:n], core.aux[2 + u % 2][:, 0:n],
                               ACT.Copy).then_inc(*copied.inc())

            for s in range(N + 1):
                if s < N:
                    exp(s)
                if s >= 1:
                    copy(s - 1)

        @block.vector
        def _(dve):
            def maximum(u):
                n = units[u]["keys"]
                dve.wait_ge(*scored.ge(u + 1))
                if u >= 4:
                    dve.wait_ge(*exped.ge(u - 3))
                dve.tensor_reduce(small[:, u % 4:u % 4 + 1], core.aux[u % 2][:, 0:n], AX_X, ALU.max,
                                  negate=True).then_inc(*maxed.inc())
                if "max" in units[u]:
                    dve.wait_ge(*maxed.ge(u + 1))
                    dve.tensor_scalar(units[u]["max"], small[:, u % 4:u % 4 + 1], -1.0, None,
                                      ALU.mult).then_inc(*order.inc())

            def keep(u):
                out = units[u]["out"]
                if "max" in units[u]:
                    dve.wait_ge(*summed.ge(u + 1))
                    dve.tensor_copy(out, core.acc[u % 4][:, 0:HD]).then_inc(*kept.inc())
                    return
                dve.wait_ge(*exped.ge(u + 1))
                dve.reciprocal(small[:, 8 + u % 4:9 + u % 4], small[:, 4 + u % 4:5 + u % 4]
                               ).then_inc(*order.inc())
                dve.wait_ge(*order.so_far())
                dve.wait_ge(*summed.ge(u + 1))
                dve.tensor_scalar(out, core.acc[u % 4][:, 0:HD], small[:, 8 + u % 4:9 + u % 4], None,
                                  ALU.mult).then_inc(*kept.inc())

            for s in range(N + 3):
                if s < N:
                    maximum(s)
                if s >= 3:
                    keep(s - 3)


def fox(core, l, mixed, ctx):
    def one_head_each(act, q, j, bank):
        act.activation(at(q, j * 2), bank, ACT.Copy, scale=core.c("head2_scaled")[:, 0:1])
        return act.activation(at(q, j * 2 + 1), bank, ACT.Copy, scale=core.c("head2_scaled")[:, 1:2])

    q = core.sb(f"fox_q{l}", [P, FOX_HEADS, T], ctx=ctx)
    k = core.sb(f"fox_k{l}", [P, 4, T], ctx=ctx)
    v = core.sb(f"fox_v{l}", [P, 4, T], ctx=ctx)
    v_tok = core.sb(f"fox_vtok{l}", [P, NT, T], ctx=ctx)
    o_tok = v
    ncum = core.sb(f"fox_ncum{l}", [P, T], ctx=ctx)
    attention_buffers(core, f"fox{l}", ctx)
    project(core, lambda k: core.xn[:, k, :], [
        (4, None, lambda act, j, bank: one_head_each(act, q, j, bank)),
        (4, None, copy_to(k)),
        (4, None, copy_to(v)),
        (4, None, lambda act, j, bank: act.activation(at(mixed, j + FOX_T), bank, ACT.Silu))])
    with core.phase() as block:
        @block.vector
        def _(dve):
            dve.tensor_scalar(ncum[:, :], core.cum[:, 0, :], -1.0, None,
                              ALU.mult).then_inc(*core.dve_order.inc())
    token_major(core, lambda j: v[:, j, :], 4, v_tok)
    units = []
    for h in range(FOX_HEADS):
        pick = core.c("ident")[:, DTF_F + h:DTF_F + h + 1]
        for t in range(NT):
            n = (t + 1) * P
            units.append({
                "keys": n,
                "scores": [(q[:, h, t * P:n], k[:, h // 2, 0:n], 0),
                           (column(pick), ncum[:, 0:n], 0),
                           (core.cum[:, 0, t * P:n], column(pick, n), 0),
                           (core.c("ident"), core.c("neg_q"), t * P)],
                "values": [v_tok[:, b, h * HD:(h + 1) * HD] for b in range(t + 1)],
                "out": o_tok[:, t, h * HD:(h + 1) * HD]})
    attention(core, units, o_tok)
    feature_major(core, o_tok, 4, None, after=lambda dve, j, bank: dve.tensor_tensor(
        mixed[:, FOX_T + j, :], bank, mixed[:, FOX_T + j, :], ALU.mult))


def add_to_x(core, moving, scale, dst=None):
    with core.phase() as block:
        @block.sync
        def _(sp):
            core.stream_ahead(sp, KD)

        @block.tensor
        def _(pe):
            core.linear(pe, 0, KD, moving)

        @block.vector
        def _(dve):
            core.read_out(dve, 0, KD, lambda j, bank: dve.scalar_tensor_tensor(
                out=at(core.x, j), in0=bank[:, :], scalar=scale(j), in1=at(core.x, j),
                op0=ALU.mult, op1=ALU.add))
    core.end_linear(KD)


def rotary_tables(core, ctx):
    pos_i = core.sb("pos_i", [P, T], I32, ctx=ctx)
    ang, k, r = (core.sb(n, [P, T], ctx=ctx) for n in ("ang", "ang_k", "ang_r"))
    wrapped = core.sig("wrapped")
    sined = core.sig("sin_made")
    with core.phase() as block:
        @block.sync
        def _(sp):
            sp.dma_start(pos_i[:, :], core.dram["positions"].partition_broadcast(P)
                         ).then_inc(*core.loaded.inc(16))

        @block.vector
        def _(dve):
            order = core.dve_order

            def step(ins):
                ins.then_inc(*order.inc())
                dve.wait_ge(*order.so_far())

            step(dve.memset(core.ones_row[:, :], 1.0))
            dve.wait_ge(*core.loaded.ge(16))
            step(dve.tensor_copy(ang[:, :], pos_i[:, :]))
            step(dve.tensor_scalar(ang[:, :], ang[:, :], core.c("freq"), None, ALU.mult))
            for which in range(2):
                shift = 0.25 * which
                step(dve.tensor_scalar(k[:, :], ang[:, :], float(1 / TWO_PI), shift, ALU.mult, ALU.add))
                step(dve.tensor_scalar(k[:, :], k[:, :], ROUND, None, ALU.add))
                step(dve.tensor_scalar(k[:, :], k[:, :], -ROUND, None, ALU.add))
                if which:
                    dve.wait_ge(*sined.ge(1))
                step(dve.scalar_tensor_tensor(out=r[:, :], in0=k[:, :], scalar=-C1, in1=ang[:, :],
                                              op0=ALU.mult, op1=ALU.add))
                step(dve.scalar_tensor_tensor(out=r[:, :], in0=k[:, :], scalar=-C2, in1=r[:, :],
                                              op0=ALU.mult, op1=ALU.add))
                step(dve.scalar_tensor_tensor(out=r[:, :], in0=k[:, :], scalar=-C3, in1=r[:, :],
                                              op0=ALU.mult, op1=ALU.add))
                step(dve.tensor_scalar(r[:, :], r[:, :], float(np.pi / 2 * which), 3.1415925, ALU.add, ALU.min))
                dve.tensor_scalar(r[:, :], r[:, :], -3.1415925, None, ALU.max).then_inc(*wrapped.inc())
                if not which:
                    dve.wait_ge(*wrapped.ge(1))

        @block.scalar
        def _(act):
            act.wait_ge(*wrapped.ge(1))
            act.activation(core.sin[:, :], r[:, :], ACT.Sin).then_inc(*sined.inc())
            act.wait_ge(*wrapped.ge(2))
            act.activation(core.cos[:, :], r[:, :], ACT.Sin).then_inc(*sined.inc())


def first_block(core):
    with ExitStack() as ctx:
        core.cos, core.sin = (core.sb(n, [P, T], ctx=ctx) for n in ("cos", "sin"))
        core.cum = core.sb("cum", [P, NT, T], ctx=ctx)
        with ExitStack() as inner:
            rotary_tables(core, inner)
        modulation(core)
        for l in range(DEPTH):
            with ExitStack() as layer:
                mixed = core.sb(f"mixed{l}", [P, MIX, T], ctx=layer)
                layer_norm_in(core, l)
                for branch in (retention, ssd, fox):
                    with ExitStack() as inner:
                        branch(core, l, mixed, inner)
                add_to_x(core, lambda k: mixed[:, k, :],
                         lambda j: core.mod[:, l, 2 * KD + j:2 * KD + j + 1] if isinstance(j, int)
                         else core.mod[:, l, bass.ds(j + 2 * KD, 1)])
    norm(core, [core.x[:, k, :] for k in range(KD)], "all", 1.0 / D,
         gained(core, lambda j: core.x[:, j, :], lambda j: core.x[:, j, :], lambda j: core.v("final_g", j)))


def swiglu(core, gain, name):
    rms_all(core, gain)
    gated = core.sig("ffn_gated")
    count = 2 * KF
    with ExitStack() as ctx:
        h = core.sb(f"ffn_h_{name}", [P, KF, T], ctx=ctx)
        gate = core.sb(f"ffn_gate_{name}", [P, 2, T], ctx=ctx)
        with core.phase() as block:
            @block.sync
            def _(sp):
                core.stream_ahead(sp, count)

            @block.tensor
            def _(pe):
                core.linear(pe, 0, count, lambda k: core.xn[:, k, :])

            @block.scalar
            def _(act):
                slot = [0]

                def body(j, g_bank, u_bank):
                    slot[0] += 1
                    return act.activation(gate[:, (slot[0] - 1) % 2, :], g_bank[:, :], ACT.Silu
                                          ).then_inc(gated.handle, 1)
                core.read_out(act, 0, count, body, per_piece=2, free=False)

            @block.vector
            def _(dve):
                slot = [0]

                def body(j, g_bank, u_bank):
                    slot[0] += 1
                    dve.wait_ge(gated.handle, j + (gated.base + 1))
                    return dve.tensor_tensor(at(h, j), gate[:, (slot[0] - 1) % 2, :], u_bank[:, :],
                                             ALU.mult)
                core.read_out(dve, 0, count, body, per_piece=2)
            gated.total += KF
        core.end_linear(count)
        add_to_x(core, lambda k: h[:, k, :], lambda j: 0.5)


def masked_gains(core, dst, gain):
    with core.phase() as block:
        @block.vector
        def _(dve):
            dve.tensor_scalar(dst, core.c("head2_scaled"), core.v(gain), None,
                              ALU.mult).then_inc(*core.dve_order.inc())


def split_heads(dst, src, gains):
    def finish(dve, j, bank):
        for e in range(2):
            ins = dve.scalar_tensor_tensor(out=dst(2 * j + e), in0=src(j), scalar=gains[:, e:e + 1],
                                           in1=bank, op0=ALU.mult, op1=ALU.mult)
        return ins
    return finish


def memory_keys(core, l, k, v_tok, ctx):
    mem = core.sb(f"mem{l}", [P, KD, MEM], ctx=ctx)
    v = core.sb(f"mem_v{l}", [P, 2, MEM], ctx=ctx)
    with core.phase() as block:
        @block.sync
        def _(sp):
            sp.dma_start(mem[:, :, :], core.dram["mem"]).then_inc(*core.loaded.inc(16))
            sp.wait_ge(*core.loaded.ge(16))
    norm(core, [mem[:, j, :] for j in range(KD)], "all", 1.0 / D,
         gained(core, lambda j: mem[:, j, :], lambda j: mem[:, j, :], lambda j: core.v(f"mem_g{l}", j)),
         n=MEM)
    project(core, lambda j: mem[:, j, :], [(2, None, copy_to(k, hi=MEM)), (2, None, copy_to(v, hi=MEM))],
            n=MEM)
    norm(core, [k[:, j, :] for j in range(2)], "half", 1.0 / HD,
         gained(core, lambda j: k[:, j, :], lambda j: k[:, j, :], lambda j: core.v(f"memk_g{l}")), n=MEM)
    token_major(core, lambda j: v[:, j, :], 2, v_tok, n=MEM)


def memory_attention(core, l, q_raw, k, v_tok, out, ctx):
    q = core.sb(f"mem_q{l}", [P, MEM_HEADS, T], ctx=ctx)
    gains = core.sb(f"mem_gains{l}", [P, 2], ctx=ctx)
    o_tok = core.sb(f"mem_o{l}", [P, NT, MEM], ctx=ctx)
    attention_buffers(core, f"mem{l}", ctx)
    masked_gains(core, gains[:, :], f"memq_g{l}")
    norm(core, [q_raw(j) for j in range(2)], "half", 1.0 / HD,
         split_heads(lambda h: q[:, h, :], q_raw, gains))
    units = [{"keys": MEM,
              "scores": [(q[:, h, t * P:(t + 1) * P], k[:, h // 2, :], 0)],
              "values": [v_tok[:, b, h * HD:(h + 1) * HD] for b in range(MEM // P)],
              "out": o_tok[:, t, h * HD:(h + 1) * HD]}
             for h in range(MEM_HEADS) for t in range(NT)]
    attention(core, units, o_tok)
    feature_major(core, o_tok, 2, None, after=lambda dve, j, bank: dve.tensor_copy(out(j), bank))


def rwkv(core, p, ctx):
    kk = core.sb("kk", [P, RW, T], ctx=ctx)
    lora = core.sb("lora", [P, 2 * RW, P], ctx=ctx)
    gate_up = core.sb("gate_up", [P, RW, P], ctx=ctx)
    extra = core.sb("rwkv_work", [P, 9, T], ctx=ctx)
    state = core.sb("state", [P, P], ctx=ctx)
    joined = core.sb("state_joined", [P, P], ctx=ctx)
    ec = core.sb("exp_center", [P, NT], ctx=ctx)
    carry = core.sb("state_carry", [P, NT], ctx=ctx)
    tile = lambda j: p[:, j, 1:1 + T]

    def work(i):
        return core.xn[:, i, :] if i < 8 else core.squares[:, i - 8, :] if i < 16 else extra[:, i - 16, :]

    def chunks(ap):
        return ap.rearrange("p (n t) -> p n t", n=NT)

    def chunk(ap, n):
        return ap[:, n * P:(n + 1) * P]

    def pred(name):
        return tiled(core.c(name).bitcast(U32), NT)

    diffed, shifted = core.sig("shift_diff"), core.sig("shift_done")
    with core.phase() as block:
        @block.sync
        def _(sp):
            sp.dma_start(lora[:, :, :].rearrange("p k m -> p (k m)"), core.dram["lora"]
                         ).then_inc(*core.loaded.inc(16))
            sp.dma_start(gate_up[:, :, :].rearrange("p k m -> p (k m)"), core.dram["gate_up"]
                         ).then_inc(*core.loaded.inc(16))
            sp.wait_ge(*core.loaded.ge(32))

        @block.gpsimd
        def _(pool):
            for j in range(NSHIFT):
                if j >= 8:
                    pool.wait_ge(*shifted.ge(j - 7))
                pool.tensor_tensor(core.squares[:, j % 8, :], p[:, j, 0:T], tile(j),
                                   ALU.subtract).then_inc(*diffed.inc())

        @block.vector
        def _(dve):
            for j in range(NSHIFT):
                dve.wait_ge(*diffed.ge(j + 1))
                dve.scalar_tensor_tensor(out=tile(j), in0=core.squares[:, j % 8, :], scalar=core.v("mu", j),
                                         in1=tile(j), op0=ALU.mult, op1=ALU.add).then_inc(*shifted.inc())
    with core.phase() as block:
        @block.scalar
        def _(act):
            act.activation(tile(18)[0:HD, :], tile(18)[0:HD, :], ACT.Tanh).then_inc(*core.act_order.inc())
            act.activation(tile(19), tile(19), ACT.Sigmoid).then_inc(*core.act_order.inc())

        @block.vector
        def _(dve):
            for m in range(RW):
                dve.tensor_scalar(kk[:, m, :], tile(RW + m), core.v("kk_scale", m), None,
                                  ALU.mult).then_inc(*core.dve_order.inc())

        @block.gpsimd
        def _(pool):
            for i in (15, 16, 17, 18, 19, 20, 21, 22, 23, 24):
                if i >= 16:
                    pool.memset(work(i), 0.0).then_inc(*core.pool_order.inc())
    norm(core, [kk[:, m, :] for m in range(RW)], "half", 1.0,
         lambda dve, j, bank: dve.tensor_tensor(kk[:, j, :], kk[:, j, :], bank, ALU.mult), floor=1e-12)
    with core.phase() as block:
        @block.gpsimd
        def _(pool):
            pool.memset(work(15), 0.0).then_inc(*core.pool_order.inc())
    for m in range(RW):
        rwkv_heads(core, m, tile, kk, lora, work, state, joined, ec, carry, chunks, chunk, pred)

    centered, meaned = core.sig("ln_centered"), core.sig("ln_mean")
    with core.phase() as block:
        @block.tensor
        def _(pe):
            for m in range(RW):
                if m >= 4:
                    pe.wait_ge(*centered.ge(m - 3))
                pe.matmul(core.aux[m % 4][:, :], core.c("blkmean"), tile(m), start=True,
                          stop=True).then_inc(*meaned.inc())

        @block.vector
        def _(dve):
            for m in range(RW):
                dve.wait_ge(*meaned.ge(m + 1))
                dve.tensor_tensor(tile(m), tile(m), core.aux[m % 4][:, :],
                                  ALU.subtract).then_inc(*centered.inc())

    def finish(dve, m, bank):
        order = core.dve_order
        dve.scalar_tensor_tensor(out=tile(m), in0=tile(m), scalar=core.v("lnx_g", m), in1=bank,
                                 op0=ALU.mult, op1=ALU.mult).then_inc(*order.inc())
        dve.wait_ge(*order.so_far())
        return dve.scalar_tensor_tensor(out=tile(m), in0=tile(m), scalar=core.v("lnx_b", m),
                                        in1=tile(RW + m), op0=ALU.add, op1=ALU.add)
    norm(core, [tile(m) for m in range(RW)], "half", 1.0 / HD, finish, eps=LNX_EPS)
    gate_made, gated = core.sig("gate_made"), core.sig("gate_used")
    with core.phase() as block:
        @block.tensor
        def _(pe):
            for m in range(RW):
                if m >= 4:
                    pe.wait_ge(*gated.ge(m - 3))
                pe.matmul(core.aux[m % 4][:, :], gate_up[:, m, :], tile(19), start=True,
                          stop=True).then_inc(*gate_made.inc())

        @block.vector
        def _(dve):
            for m in range(RW):
                dve.wait_ge(*gate_made.ge(m + 1))
                dve.tensor_tensor(tile(m), tile(m), core.aux[m % 4][:, :], ALU.mult).then_inc(*gated.inc())


def rwkv_heads(core, m, tile, kk, lora, work, state, joined, ec, carry, chunks, chunk, pred):
    r, k, v = tile(m), tile(RW + m), tile(2 * RW + m)
    lw, a, kmod, lc, ex, e1, e2 = (work(i) for i in range(7))
    kkq, rq, bh, kh = (work(i) for i in range(7, 11))
    kkq_e, rq_e = (work(3), work(4)), (work(5), work(6))
    kkq_t, bh_t, kh_t, v_t = (work(i) for i in range(11, 15))
    A, ak, rb, rk, a0 = ((work(15 + 2 * i), work(16 + 2 * i)) for i in range(5))
    X, Dm, C, G = (work(3), work(4)), (work(5), work(6)), (work(0), work(1)), (work(2), work(7))
    wt, z, u0, sa = work(9), work(10), work(0), work(1)
    order = core.dve_order

    def stepper(dve):
        def step(ins):
            ins.then_inc(*order.inc())
            dve.wait_ge(*order.so_far())
        return step

    lora_done, squashed, centered = core.sig("lora_done"), core.sig("lora_act"), core.sig("decay_sums")
    exped, bonus_in, bonus_sum = core.sig("decay_exp"), core.sig("bonus_in"), core.sig("bonus_sum")
    with core.phase() as block:
        @block.tensor
        def _(pe):
            pe.matmul(core.aux[0][:, :], lora[:, m, :], tile(18), start=True, stop=True
                      ).then_inc(*lora_done.inc())
            pe.matmul(core.aux[1][:, :], lora[:, RW + m, :], tile(18), start=True, stop=True
                      ).then_inc(*lora_done.inc())
            pe.wait_ge(*bonus_in.ge(1))
            pe.matmul(core.aux[2][:, :], core.c("blk"), kkq_t, start=True, stop=True
                      ).then_inc(*bonus_sum.inc())

        @block.scalar
        def _(act):
            act.wait_ge(*lora_done.ge(1))
            act.activation(lw, core.aux[0][:, :], ACT.Sigmoid, bias=core.v("w0", m)).then_inc(*squashed.inc())
            act.wait_ge(*lora_done.ge(2))
            act.activation(a, core.aux[1][:, :], ACT.Sigmoid, bias=core.v("a0", m)).then_inc(*squashed.inc())
            act.wait_ge(*centered.ge(1))
            act.activation(ex, ex, ACT.Exp).then_inc(*exped.inc())
            act.activation(e1, lc, ACT.Exp).then_inc(*exped.inc())
            act.activation(e2, lc, ACT.Exp, scale=-1.0).then_inc(*exped.inc())
            act.activation(ec[:, :], ec[:, :], ACT.Exp).then_inc(*exped.inc())

        @block.vector
        def _(dve):
            step = stepper(dve)
            dve.wait_ge(*squashed.ge(1))
            step(dve.tensor_scalar(lw, lw, DECAY_SCALE, None, ALU.mult))
            for n in range(NT):
                dve.tensor_tensor_scan(chunk(e1, n), core.c("ones"), chunk(lw, n), 0.0, ALU.mult,
                                       ALU.add).then_inc(*order.inc())
            dve.wait_ge(*order.so_far())
            middle = chunks(e1)[:, :, P // 2 - 1:P // 2]
            dve.tensor_copy(ec[:, :], middle.rearrange("p n a -> p (n a)")).then_inc(*order.inc())
            spread = bass.AP(middle.tensor, middle.offset, [*[list(d) for d in middle.ap[:2]], [0, P]])
            step(dve.tensor_tensor(chunks(lc), chunks(e1), spread, ALU.subtract))
            dve.tensor_tensor(ex, lc, lw, ALU.subtract).then_inc(*centered.inc())
            dve.wait_ge(*squashed.ge(2))
            step(dve.tensor_scalar(kmod, a, -1.0, core.v("k_a", m), ALU.add, ALU.mult))
            step(dve.scalar_tensor_tensor(out=kmod, in0=kmod, scalar=1.0, in1=k, op0=ALU.add, op1=ALU.mult))
            dve.scalar_tensor_tensor(out=kkq_t, in0=r, scalar=core.v("r_k", m), in1=kmod, op0=ALU.mult,
                                     op1=ALU.mult).then_inc(*bonus_in.inc())
            step(dve.tensor_tensor(a, kk[:, m, :], a, ALU.mult))
            dve.wait_ge(*exped.ge(4))
            dve.tensor_tensor(kkq, kk[:, m, :], ex, ALU.mult).then_inc(*order.inc())
            dve.tensor_tensor(rq, r, e1, ALU.mult).then_inc(*order.inc())
            dve.tensor_tensor(bh, a, e2, ALU.mult).then_inc(*order.inc())
            dve.tensor_tensor(kh, kmod, e2, ALU.mult).then_inc(*order.inc())
            last = chunks(e1)[:, 0:NT - 1, P - 1:P].rearrange("p n a -> p (n a)")
            dve.tensor_tensor(carry[:, 0:NT - 1], last, ec[:, 1:NT], ALU.mult).then_inc(*order.inc())
            dve.wait_ge(*bonus_sum.ge(1))
            dve.tensor_tensor(k, core.aux[2][:, :], v, ALU.mult).then_inc(*order.inc())
            dve.wait_ge(*order.so_far())
            for e in range(2):
                mask = core.c("head2")[:, e:e + 1]
                dve.tensor_scalar(kkq_e[e], kkq, mask, None, ALU.mult).then_inc(*order.inc())
                dve.tensor_scalar(rq_e[e], rq, mask, None, ALU.mult).then_inc(*order.inc())

    turned, kept = core.sig("rwkv_turned"), core.sig("rwkv_kept")
    pairs = ((kkq, kkq_t), (bh, bh_t), (kh, kh_t), (v, v_t))
    products = [(out[e], lhsT[e], rhs[e], mask) for out, lhsT, rhs, mask in (
        (A, kkq_e, (bh, bh), "strict"), (a0, (bh, bh), kkq_e, "level0_t"),
        (ak, (kh, kh), kkq_e, "strict_t"), (rb, (bh, bh), rq_e, "incl"),
        (rk, (kh, kh), rq_e, "incl")) for e in range(2)]
    with core.phase() as block:
        @block.tensor
        def _(pe):
            for i, (src, _) in enumerate(pairs):
                for n in range(NT):
                    mm = pe.transpose(chunk(core.aux[i], n), chunk(src, n), core.c("ident"))
                mm.then_inc(*turned.inc())
            for i, (_, lhsT, rhs, _) in enumerate(products):
                if i >= 4:
                    pe.wait_ge(*kept.ge(i - 3))
                for n in range(NT):
                    mm = pe.matmul(chunk(core.acc[i % 4], n), chunk(lhsT, n), chunk(rhs, n),
                                   start=True, stop=True)
                mm.then_inc(*turned.inc())

        @block.scalar
        def _(act):
            for i, (_, dst) in enumerate(pairs):
                act.wait_ge(*turned.ge(i + 1))
                act.activation(dst, core.aux[i][:, :], ACT.Copy).then_inc(*core.act_order.inc())

        @block.vector
        def _(dve):
            for i, (dst, _, _, mask) in enumerate(products):
                dve.wait_ge(*turned.ge(len(pairs) + i + 1))
                dve.copy_predicated(chunks(dst), pred(mask), chunks(core.acc[i % 4][:, :])
                                    ).then_inc(*kept.inc())

    started, picked, first, copied = (core.sig(s) for s in ("inv_start", "inv_pick", "inv_first", "inv_copied"))
    second, third, x_new, d_new = (core.sig(s) for s in ("inv_second", "inv_third", "inv_x", "inv_d"))
    ident = tiled(core.c("ident"), NT)
    with core.phase() as block:
        @block.gpsimd
        def _(pool):
            for level in range(7):
                for e in range(2):
                    if level == 1:
                        pool.wait_ge(*started.ge(2 * e + 2))
                    elif level > 1:
                        pool.wait_ge(*first.ge(2 * (level - 2) + e + 1))
                    pool.tensor_tensor(chunks(C[e]), chunks(A[e]), tiled(core.c(f"level{level}"), NT),
                                       ALU.mult).then_inc(*picked.inc())

        @block.tensor
        def _(pe):
            for level in range(1, 7):
                i = 2 * (level - 1)
                for e in range(2):
                    pe.wait_ge(*picked.ge(2 * level + e + 1))
                    if level == 1:
                        pe.wait_ge(*started.ge(2 * e + 2))
                    else:
                        pe.wait_ge(*x_new.ge(i - 2 + e + 1))
                    for n in range(NT):
                        mm = pe.matmul(chunk(core.aux[e], n), chunk(C[e], n), chunk(X[e], n),
                                       start=True, stop=True)
                    mm.then_inc(*first.inc())
                for e in range(2):
                    pe.wait_ge(*copied.ge(i + e + 1))
                    if level > 1:
                        pe.wait_ge(*d_new.ge(i - 2 + e + 1))
                    for n in range(NT):
                        mm = pe.matmul(chunk(core.aux[2 + e], n), chunk(Dm[e], n), chunk(G[e], n),
                                       start=True, stop=True)
                    mm.then_inc(*second.inc())
                    if level < 6:
                        for n in range(NT):
                            mm = pe.matmul(chunk(core.acc[e], n), chunk(G[e], n), chunk(Dm[e], n),
                                           start=True, stop=True)
                        mm.then_inc(*third.inc())

        @block.scalar
        def _(act):
            for level in range(1, 7):
                for e in range(2):
                    i = 2 * (level - 1) + e
                    act.wait_ge(*first.ge(i + 1))
                    if level > 1:
                        act.wait_ge(*third.ge(i - 1))
                    act.activation(G[e], core.aux[e][:, :], ACT.Copy).then_inc(*copied.inc())

        @block.vector
        def _(dve):
            for e in range(2):
                dve.tensor_tensor(chunks(X[e]), ident, chunks(a0[e]), ALU.subtract).then_inc(*started.inc())
                dve.wait_ge(*picked.ge(e + 1))
                dve.tensor_tensor(chunks(Dm[e]), ident, chunks(C[e]), ALU.subtract).then_inc(*started.inc())
            for level in range(1, 7):
                for e in range(2):
                    i = 2 * (level - 1) + e
                    dve.wait_ge(*second.ge(i + 1))
                    dve.tensor_tensor(X[e], X[e], core.aux[2 + e][:, :], ALU.subtract).then_inc(*x_new.inc())
                    if level < 6:
                        dve.wait_ge(*third.ge(i + 1))
                        dve.tensor_tensor(Dm[e], Dm[e], core.acc[e][:, :], ALU.subtract
                                          ).then_inc(*d_new.inc())

    half = lambda ap, n, e: ap[:, n * P + e * HD:n * P + (e + 1) * HD]
    done, stored = core.sig("solve_done"), core.sig("solve_kept")
    with core.phase() as block:
        @block.tensor
        def _(pe):
            for n in range(NT):
                for e in range(2):
                    mm = pe.matmul(half(core.aux[0], n, e), chunk(ak[e], n), half(v_t, n, e), start=True,
                                   stop=True)
            mm.then_inc(*done.inc())
            for n in range(NT):
                for e in range(2):
                    mm = pe.matmul(chunk(core.aux[1][e * HD:(e + 1) * HD, :], n), half(kkq_t, n, e),
                                   chunk(X[e], n), start=True, stop=True)
            mm.then_inc(*done.inc())
            pe.wait_ge(*stored.ge(1))
            for n in range(NT):
                for e in range(2):
                    mm = pe.matmul(half(core.aux[2], n, e), chunk(X[e], n), half(z, n, e), start=True,
                                   stop=True)
            mm.then_inc(*done.inc())

        @block.scalar
        def _(act):
            for i, dst in enumerate((z, wt, u0)):
                act.wait_ge(*done.ge(i + 1))
                act.activation(dst, core.aux[i][:, :], ACT.Copy).then_inc(*stored.inc())

    from_state, corrected, added, moved, out_done = (core.sig(s) for s in (
        "seq_from_state", "seq_corrected", "seq_added", "seq_state", "seq_out"))
    y = core.aux[2]
    with core.phase() as block:
        @block.tensor
        def _(pe):
            for n in range(NT):
                if n:
                    pe.wait_ge(*moved.ge(n))
                    pe.matmul(core.aux[0][:, 0:P], chunk(wt, n), state[:, :], start=True, stop=True
                              ).then_inc(*from_state.inc())
                    pe.matmul(chunk(y, n), state[:, :], chunk(rq, n), start=True, stop=False,
                              skip_group_check=True)
                for e in range(2):
                    pe.matmul(chunk(y[e * HD:(e + 1) * HD, :], n), half(v_t, n, e), chunk(rk[e], n),
                              start=(n == 0), stop=False, skip_group_check=True)
                pe.wait_ge(*corrected.ge(n + 1))
                if n < NT - 1:
                    pe.matmul(core.aux[1][:, 0:P], chunk(bh_t, n), chunk(sa, n), start=True, stop=False)
                    pe.matmul(core.aux[1][:, 0:P], chunk(kh_t, n), chunk(v_t, n), start=False, stop=True
                              ).then_inc(*added.inc())
                for e in range(2):
                    mm = pe.matmul(chunk(y[e * HD:(e + 1) * HD, :], n), half(sa, n, e), chunk(rb[e], n),
                                   start=False, stop=True, skip_group_check=True)
            mm.then_inc(*out_done.inc())

        @block.vector
        def _(dve):
            step = stepper(dve)
            for n in range(NT):
                if n:
                    dve.wait_ge(*from_state.ge(n))
                    dve.scalar_tensor_tensor(out=chunk(sa, n), in0=core.aux[0][:, 0:P], scalar=-1.0,
                                             in1=chunk(u0, n), op0=ALU.mult,
                                             op1=ALU.subtract).then_inc(*corrected.inc())
                else:
                    dve.tensor_scalar(chunk(sa, n), chunk(u0, n), -1.0, None, ALU.mult
                                      ).then_inc(*corrected.inc())
                if n < NT - 1:
                    dve.wait_ge(*added.ge(n + 1))
                    if n:
                        step(dve.tensor_tensor(joined[:, :], core.aux[1][:, 0:P], state[:, :], ALU.add))
                    else:
                        step(dve.tensor_copy(joined[:, :], core.aux[1][:, 0:P]))
                    dve.scalar_tensor_tensor(out=state[:, :], in0=joined[:, :], scalar=carry[:, n:n + 1],
                                             in1=core.c("blk"), op0=ALU.mult,
                                             op1=ALU.mult).then_inc(*moved.inc())

        @block.scalar
        def _(act):
            act.wait_ge(*out_done.ge(1))
            act.activation(r, y[:, :], ACT.Copy).then_inc(*core.act_order.inc())


def shared_keys(core, k, v_tok):
    rms_all(core, "kv_g")
    with ExitStack() as ctx:
        v = core.sb("dil_v", [P, 2 * DIL, T], ctx=ctx)
        project(core, lambda j: core.xn[:, j, :], [(2 * DIL, None, copy_to(k)), (2 * DIL, None, copy_to(v))])
        norm(core, [k[:, j, :] for j in range(2 * DIL)], "half", 1.0 / HD,
             gained(core, lambda j: k[:, j, :], lambda j: k[:, j, :], lambda j: core.v("kvk_g")))
        turned, stored = core.sig("turned"), core.sig("stored")
        units = [(g, t) for g in range(DIL) for t in range(NT)]
        with core.phase() as block:
            @block.tensor
            def _(pe):
                for u, (g, t) in enumerate(units):
                    if u >= 4:
                        pe.wait_ge(*stored.ge(u - 3))
                    for j in range(2):
                        mm = pe.transpose(core.aux[u % 4][:, j * P:(j + 1) * P],
                                          tokens(v[:, 2 * g + j, :], g, t), core.c("ident"))
                    mm.then_inc(*turned.inc())

            @block.vector
            def _(dve):
                for u, (g, t) in enumerate(units):
                    dve.wait_ge(*turned.ge(u + 1))
                    dve.tensor_copy(v_tok[:, t, g * 2 * P:(g + 1) * 2 * P], core.aux[u % 4][:, 0:2 * P]
                                    ).then_inc(*stored.inc())


def tokens(ap, g, t):
    return ap[:, t * P:(t + 1) * P] if g == 0 else ap.rearrange("p (a r) -> p r a", r=NT)[:, t, :]


def relative_bias(core, bias, ctx):
    table = core.sb("rel_table", [P, 12], ctx=ctx)
    buckets = core.sb("buckets", [P, DIL, NREL], ctx=ctx)
    rows = core.sb("rel_rows", [P, 12, NREL], ctx=ctx)
    cleared, spread, kept = core.sig("rel_cleared"), core.sig("rel_spread"), core.sig("rel_kept")
    written, read = core.sig("rel_written"), core.sig("rel_read")
    skew = core.dram["skew"]
    with core.phase() as block:
        @block.sync
        def _(sp):
            sp.dma_start(buckets[:, :, :], core.dram["buckets"]).then_inc(*core.loaded.inc(16))
            sp.wait_ge(*cleared.ge(2))
            sp.dma_start(table[0:BUCKETS, :], core.dram["rel"]).then_inc(*core.loaded.inc(16))
            for h in range(12):
                sp.wait_ge(*kept.ge(h + 1))
                sp.dma_start(skew[h], rows[:, h, :]).then_inc(*written.inc(16))
            sp.wait_ge(*written.ge(12 * 16))
            for h in range(12):
                first, n = (P - 1, 2 * P) if h < DIL_HEADS else (2 * P - 1, P)
                src = bass.AP(skew.tensor, skew.offset + h * P * NREL + first, [[NREL - 1, P], [1, n]])
                sp.dma_start(bias[:, h, 0:n], src).then_inc(*read.inc(16))
            sp.wait_ge(*read.ge(12 * 16))

        @block.vector
        def _(dve):
            dve.memset(table[:, :], 0.0).then_inc(*cleared.inc())
            dve.wait_ge(*cleared.ge(1))
            dve.memset(table[BUCKETS:BUCKETS + 1, :], NEG).then_inc(*cleared.inc())
            for h in range(12):
                dve.wait_ge(*spread.ge(h + 1))
                dve.tensor_copy(rows[:, h, :], core.aux[h % 4][:, 0:NREL]).then_inc(*kept.inc())

        @block.tensor
        def _(pe):
            pe.wait_ge(*core.loaded.ge(32))
            for h in range(12):
                if h >= 4:
                    pe.wait_ge(*kept.ge(h - 3))
                pe.matmul(core.aux[h % 4][:, 0:NREL], column(table[:, h:h + 1]),
                          buckets[:, h // DIL_HEADS, :], start=True, stop=True).then_inc(*spread.inc())


def dilated(core, k, v_tok, out, q_raw):
    with ExitStack() as ctx:
        bias = core.sb("rel_bias", [P, 12, 2 * P], ctx=ctx)
        with ExitStack() as inner:
            relative_bias(core, bias, inner)
        q = core.sb("dil_q", [P, 12, T], ctx=ctx)
        gains = core.sb("dil_gains", [P, 2], ctx=ctx)
        masked_gains(core, gains[:, :], "bq_g")
        norm(core, [q_raw(j) for j in range(2 * DIL)], "half", 1.0 / HD,
             split_heads(lambda h: q[:, h, :], q_raw, gains))
        attention_buffers(core, "dil", ctx)
        o_tok = core.xn[:, 0:6, :].rearrange("p a t -> p (a t)").rearrange("p (n c) -> p n c", n=NT)
        top = core.sb("dil_max", [P, DIL, NT, DIL_HEADS], ctx=ctx)
        total = core.sb("dil_sum", [P, DIL, NT, DIL_HEADS], ctx=ctx)
        units = []
        for g in range(DIL):
            for h in range(DIL_HEADS):
                head = g * DIL_HEADS + h
                for t in range(NT):
                    if g == 0:
                        t0 = max(t - 1, 0)
                        keys = k[:, head // 2, t0 * P:(t + 1) * P]
                        b = bias[:, head, (P if t == 0 else 0):2 * P]
                        vs = [v_tok[:, x, head * HD:(head + 1) * HD] for x in range(t0, t + 1)]
                    else:
                        keys = tokens(k[:, head // 2, :], g, t)
                        b = bias[:, head, 0:P]
                        vs = [v_tok[:, t, head * HD:(head + 1) * HD]]
                    units.append({"keys": len(vs) * P, "values": vs,
                                  "scores": [(tokens(q[:, head, :], g, t), keys, 0),
                                             (core.c("ident"), b, 0)],
                                  "out": o_tok[:, t, head * HD:(head + 1) * HD],
                                  "max": top[:, g, t, h:h + 1], "sum": total[:, g, t, h:h + 1]})
        attention(core, units, o_tok)

        peak = core.squares[0:DIL_HEADS, 7, :]
        weight = [core.squares[:, g, :] for g in range(DIL)]
        sums = [core.squares[0:DIL_HEADS, 3 + g, :] for g in range(DIL)]
        norm_sum = core.squares[0:DIL_HEADS, 6, :]
        o = [q_raw(i) for i in range(2 * DIL)]
        turned, cleared, less, exped = (core.sig(s) for s in ("mix_turned", "mix_cleared", "mix_less", "mix_exp"))
        with core.phase() as block:
            @block.tensor
            def _(pe):
                for g in range(DIL):
                    for src, bank in ((top, core.aux[g]), (total, core.acc[g])):
                        for t in range(NT):
                            mm = pe.transpose(tokens(bank[0:DIL_HEADS, :], g, t), src[:, g, t, :],
                                              core.c("ident"))
                        mm.then_inc(*turned.inc())

            @block.vector
            def _(dve):
                order = core.dve_order

                def step(ins):
                    ins.then_inc(*order.inc())
                    dve.wait_ge(*order.so_far())

                for g in range(DIL):
                    dve.memset(weight[g], 0.0).then_inc(*order.inc())
                dve.wait_ge(*order.so_far())
                dve.wait_ge(*turned.ge(2 * DIL))
                w = [x[0:DIL_HEADS, :] for x in weight]
                for g in range(DIL):
                    dve.tensor_copy(w[g], core.aux[g][0:DIL_HEADS, :]).then_inc(*order.inc())
                    dve.tensor_copy(sums[g], core.acc[g][0:DIL_HEADS, :]).then_inc(*order.inc())
                dve.wait_ge(*order.so_far())
                step(dve.tensor_tensor(peak, w[0], w[1], ALU.max))
                step(dve.tensor_tensor(peak, peak, w[2], ALU.max))
                for g in range(DIL):
                    dve.tensor_tensor(w[g], w[g], peak, ALU.subtract).then_inc(*less.inc())
                dve.wait_ge(*exped.ge(DIL))
                for g in range(DIL):
                    step(dve.tensor_tensor(sums[g], sums[g], w[g], ALU.mult))
                step(dve.tensor_tensor(norm_sum, sums[0], sums[1], ALU.add))
                step(dve.tensor_tensor(norm_sum, norm_sum, sums[2], ALU.add))
                step(dve.reciprocal(norm_sum, norm_sum))
                for g in range(DIL):
                    step(dve.tensor_tensor(w[g], w[g], norm_sum, ALU.mult))

            @block.scalar
            def _(act):
                for g in range(DIL):
                    act.wait_ge(*less.ge(g + 1))
                    act.activation(weight[g][0:DIL_HEADS, :], weight[g][0:DIL_HEADS, :], ACT.Exp
                                   ).then_inc(*exped.inc())

        fm, fm_kept, spread, used = (core.sig(s) for s in ("mix_fm", "mix_fm_kept", "mix_spread", "mix_used"))
        with core.phase() as block:
            @block.tensor
            def _(pe):
                for g in range(DIL):
                    for j in range(2):
                        i = 2 * g + j
                        if i >= 4:
                            pe.wait_ge(*fm_kept.ge(i - 3))
                        for t in range(NT):
                            mm = pe.transpose(tokens(core.aux[i % 4][:, :], g, t),
                                              o_tok[:, t, i * P:(i + 1) * P], core.c("ident"))
                        mm.then_inc(*fm.inc())
                        if i >= 4:
                            pe.wait_ge(*used.ge(i - 3))
                        for e in range(2):
                            mm = pe.matmul(core.acc[i % 4][e * HD:(e + 1) * HD, :],
                                           column(core.c("ident")[:, 2 * j + e:2 * j + e + 1], HD),
                                           weight[g], start=True, stop=True)
                        mm.then_inc(*spread.inc())

            @block.vector
            def _(dve):
                order = core.dve_order
                for g in range(DIL):
                    for j in range(2):
                        i = 2 * g + j
                        dve.wait_ge(*fm.ge(i + 1))
                        dve.tensor_copy(o[i], core.aux[i % 4][:, :]).then_inc(*fm_kept.inc())
                        dve.wait_ge(*fm_kept.ge(i + 1))
                        dve.wait_ge(*spread.ge(i + 1))
                        dve.tensor_tensor(o[i], o[i], core.acc[i % 4][:, :], ALU.mult
                                          ).then_inc(*used.inc())
                dve.wait_ge(*used.ge(2 * DIL))
                for j in range(2):
                    dve.tensor_tensor(o[j], o[j], o[2 + j], ALU.add).then_inc(*order.inc())
                dve.wait_ge(*order.so_far())
                for j in range(2):
                    dve.tensor_tensor(out(j), o[j], o[4 + j], ALU.add).then_inc(*order.inc())


def second_block(core):
    swiglu(core, "pre_g0", "pre0")
    with ExitStack() as ctx:
        p = core.sb("rwkv_p", [P, A_TILES, 1 + T], ctx=ctx)
        tile = lambda j: p[:, j, 1:1 + T]
        with ExitStack() as inner:
            k = core.sb("mem_k0", [P, 2, MEM], ctx=inner)
            v_tok = core.sb("mem_vt0", [P, 2, MEM], ctx=inner)
            with ExitStack() as keys:
                memory_keys(core, 0, k, v_tok, keys)
            rms_all(core, "mix_g0")
            with core.phase() as block:
                @block.vector
                def _(dve):
                    dve.memset(p[:, :, 0:1], 0.0).then_inc(*core.dve_order.inc())
            project(core, lambda j: core.xn[:, j, :], [(A_TILES, None, copy_to(p, 1, 1 + T))])
            memory_attention(core, 0, lambda j: tile(NSHIFT + j), k, v_tok, lambda j: tile(NSHIFT + j), inner)
        with ExitStack() as inner:
            rwkv(core, p, inner)
        add_to_x(core, lambda j: tile(j if j < RW else NSHIFT + j - RW), lambda j: 1.0)
    swiglu(core, "post_g0", "post0")

    with ExitStack() as ctx:
        k = core.sb("dil_k", [P, 2 * DIL, T], ctx=ctx)
        v_tok = core.sb("dil_vt", [P, NT, 12 * HD], ctx=ctx)
        shared_keys(core, k, v_tok)
        swiglu(core, "pre_g1", "pre1")
        y = core.sb("mix_y", [P, 4, T], ctx=ctx)
        with ExitStack() as inner:
            mk = core.sb("mem_k1", [P, 2, MEM], ctx=inner)
            mv_tok = core.sb("mem_vt1", [P, 2, MEM], ctx=inner)
            with ExitStack() as keys:
                memory_keys(core, 1, mk, mv_tok, keys)
            rms_all(core, "mix_g1")
            raw = core.sb("b_q", [P, 2 * DIL + 2, T], ctx=inner)
            project(core, lambda j: core.xn[:, j, :], [(2 * DIL + 2, None, copy_to(raw))])
            with ExitStack() as mem_ctx:
                memory_attention(core, 1, lambda j: raw[:, 2 * DIL + j, :], mk, mv_tok,
                                 lambda j: y[:, 2 + j, :], mem_ctx)
            dilated(core, k, v_tok, lambda j: y[:, j, :], lambda j: raw[:, j, :])
        add_to_x(core, lambda j: y[:, j, :], lambda j: 1.0)
    swiglu(core, "post_g1", "post1")


def store(core):
    stored = core.sig("out_stored")
    with core.phase() as block:
        @block.sync
        def _(sp):
            sp.dma_start(core.dram["out"], core.x[:, :, :]).then_inc(*stored.inc(16))
            sp.wait_ge(*stored.ge(16))


def build(nc, dram):
    with ExitStack() as ctx:
        core = Core(nc, ctx, dram)
        core.cond = core.sb("cond", [P, KD])
        core.mod = core.sb("mod", [P, DEPTH, 3 * KD])
        core.gs = core.sb("gs", [P, KD])
        core.sums = core.sb("sums", [P, 64])
        core.roots = core.sb("roots", [P, 64])
        core.squares = core.sb("squares", [P, KD, T])
        core.ones_row = core.sb("ones_row", [NDTF, T])
        core.att_small = core.sb("att_small", [P, 12])
        setup(core)
        first_block(core)
        second_block(core)
        store(core)


def weight_stream(a):
    used, stream = {}, []

    def add(w):
        k, n = w.shape
        name = f"w{k // P}"
        at = sum(x.shape[1] // P for x in used.setdefault(name, []))
        used[name].append(w)
        stream.extend((name, at + i, k // P) for i in range(n // P))

    def swiglu(w_in, w_out):
        for i in range(KF):
            add(w_in[:, i * P:(i + 1) * P])
            add(w_in[:, FF + i * P:FF + (i + 1) * P])
        add(w_out)

    for l in range(DEPTH):
        add(a["w_ada"][l])
    for l in range(DEPTH):
        w = a["w_in"][l]
        n = 2048 + 1536
        add(w[:, :n])
        add(w[:, n + 16:n + 16 + 1024])
        dtf = np.zeros((D, P), w.dtype)
        dtf[:, 0:SSD_HEADS] = w[:, n:n + 16]
        dtf[:, DTF_F:DTF_F + FOX_HEADS] = w[:, -FOX_HEADS:]
        add(dtf)
        add(w[:, n + 16 + 1024:-FOX_HEADS])
        add(a["w_out"][l])
    if SECOND:
        for l in range(DEPTH):
            swiglu(a["ffn_pre_w_in_2"][l], a["ffn_pre_w_out_2"][l])
            add(a["mem_w_kv_2"][l])
            if l == 0:
                add(a["a_w_in_2"][0])
                add(a["a_w_out_2"][0])
            else:
                add(a["b_w_q_2"][0])
                add(a["b_w_out_2"][0])
            swiglu(a["ffn_post_w_in_2"][l], a["ffn_post_w_out_2"][l])
            if l == 0:
                add(a["kv_w_2"])
    arrays = {}
    for name, ws in used.items():
        k = ws[0].shape[0]
        out = arrays[name] = np.empty((sum(w.shape[1] for w in ws) // P, P, k // P, P), np.float32)
        at = 0
        for w in ws:
            n = w.shape[1] // P
            out[at:at + n] = w.reshape(k // P, P, n, P).transpose(2, 1, 0, 3)
            at += n
        arrays[name] = out.reshape(-1, P, k)
    return arrays, stream


def feature_columns(v):
    return v.reshape(-1, P).T


def packed_vectors(a):
    out = np.zeros((P, NVEC), np.float32)

    def put(name, v):
        at, n = VEC[name]
        out[:, at:at + n] = feature_columns(v)

    for l in range(DEPTH):
        put(f"norm_g{l}", a["norm_g"][l])
        put(f"b_ada{l}", a["b_ada"][l])
        for k in range(CONV_K):
            put(f"conv_w{l}_{k}", a["conv_w"][l, k])
        put(f"conv_b{l}", a["conv_b"][l])
        put(f"d_skip{l}", np.repeat(a["d_skip"][l], SSD_DIM))
        put(f"ssd_g{l}", a["ssd_norm_g"][l])
        at = VEC[f"dtf_b{l}"][0]
        out[0:SSD_HEADS, at] = a["dt_bias"][l]
        out[DTF_F:DTF_F + FOX_HEADS, at] = a["b_forget"][l]
        out[0:SSD_HEADS, VEC[f"a_log{l}"][0]] = a["a_log"][l]
        for name, key in (("pre_g", "ffn_pre_norm_2"), ("mix_g", "mix_norm_2"),
                          ("post_g", "ffn_post_norm_2"), ("mem_g", "mem_norm_2")):
            put(f"{name}{l}", a[key][l])
        put(f"memq_g{l}", np.tile(a["mem_q_norm_2"][l], 2))
        put(f"memk_g{l}", np.tile(a["mem_k_norm_2"][l], 2))
    put("final_g", a["final_g"])
    put("mu", a["a_shift_mu_2"][0])
    for name, key in (("w0", "a_w0_2"), ("a0", "a_a0_2"), ("kk_scale", "a_kk_scale_2"),
                      ("k_a", "a_k_a_2"), ("r_k", "a_r_k_2"), ("lnx_g", "a_lnx_g_2"),
                      ("lnx_b", "a_lnx_b_2")):
        put(name, a[key][0].reshape(-1))
    put("bq_g", np.tile(a["b_q_norm_2"][0], 2))
    put("kv_g", a["kv_norm_2"])
    put("kvk_g", np.tile(a["kv_k_norm_2"], 2))
    return out


def token_columns(x):
    return np.ascontiguousarray(x.T.reshape(-1, P, x.shape[0]).transpose(1, 0, 2))


def kernel(**inputs):
    import concourse.bacc as bacc
    from concourse.bass_utils import run_bass_kernel_spmd

    a = {name: np.asarray(v) for name, v in inputs.items()}
    weights, stream = weight_stream(a)
    lora = np.zeros((P, 2 * RW * P), np.float32)
    lora[0:HD, 0:RW * P] = a["a_w_up_2"][0]
    lora[HD:P, RW * P:] = a["a_a_up_2"][0]
    arrays = {
        "const": CONST_ARRAY, "decay": decay_table(), "buckets": bucket_table(),
        "vec": packed_vectors(a),
        "x": token_columns(a["x"][0]), "c": np.ascontiguousarray(feature_columns(a["c"][0])),
        "positions": a["positions"].reshape(T),
        "mem": token_columns(a["mem_2"][0]),
        "lora": lora,
        "gate_up": a["a_g_up_2"][0],
        "rel": a["rel_bias_2"], **weights}
    arrays = {n: np.ascontiguousarray(v) for n, v in arrays.items()}
    nc = bacc.Bacc("TRN2", target_bir_lowering=False, num_devices=1)
    dram = {n: nc.dram_tensor(f"in_{n}", v.shape, mybir.dt.from_np(v.dtype), kind="ExternalInput").ap()
            for n, v in arrays.items()}
    dram["out"] = nc.dram_tensor("out", (P, KD, T), F32, kind="ExternalOutput").ap()
    dram["skew"] = nc.dram_tensor("skew", (12, P, NREL), F32, kind="Internal").ap()
    dram["stream"] = stream
    build(nc, dram)
    run = run_bass_kernel_spmd(nc, [{f"in_{n}": v for n, v in arrays.items()}], core_ids=[0])
    out = run.results[0]["out"]
    return np.ascontiguousarray(out.transpose(1, 0, 2).reshape(D, T).T)[None]
```

```python
from contextlib import ExitStack, contextmanager

import numpy as np

import concourse.bass as bass
from concourse import mybir

F32 = mybir.dt.float32
F32R = mybir.dt.float32r
U32 = mybir.dt.uint32
I32 = mybir.dt.int32
ALU = mybir.AluOpType
ACT = mybir.ActivationFunctionType
AX_X = mybir.AxisListType.X

P = 128
T = 512
NT = T // P
D = 1024
KD = D // P
DEPTH = 2
KC = 8
RING = 4
ADA_RUN = 4
ADA_RUNS = DEPTH * 3 * KD // ADA_RUN
ADA_SLOTS = 4

RET_HEADS = 4
SSD_HEADS, SSD_DIM = 16, 64
SSD_GROUPS = 2
FOX_HEADS, FOX_DIM = 8, 64
CONV_K = 4
NXBC = 12
MIX = 16
RET_T, SSD_T, FOX_T = 0, 4, 12
DTF_F = 32
NDTF = 64

FF = 2816
KF = FF // P
FF_CHUNKS = (8, 8, KF - 16)
FF_ORDER = (("pairs", 0), ("pairs", 1), ("sum", 0), ("pairs", 2), ("sum", 1), ("sum", 2))
RW = 6
RW_HEADS = 12
NSHIFT = 20
A_TILES = 22
MEM = 256
MEM_HEADS = 4
HD = 64
DIL = 3
DIL_HEADS = 4
NREL = 384
BUCKETS = 32

EPS = 1e-6
LNX_EPS = 64e-5
NEG = -1e30
TWO_PI = 2 * np.pi
C1 = 6.28125
C2 = float(np.float32(np.round((TWO_PI - C1) * 2 ** 22) / 2 ** 22))
C3 = float(np.float32(TWO_PI - C1 - C2))
ROUND = 1.5 * 2.0 ** 23
DECAY_SCALE = -float(np.exp(-0.5))

RET_TILES = 16
SSD_TILES = NXBC + 8 + 1
FOX_TILES = 16


def vec_columns():
    at, out = 0, {}

    def add(name, count):
        nonlocal at
        out[name] = (at, count)
        at += count

    for l in range(DEPTH):
        add(f"norm_g{l}", KD)
        add(f"b_ada{l}", 3 * KD)
        for k in range(CONV_K):
            add(f"conv_w{l}_{k}", NXBC)
        add(f"conv_b{l}", NXBC)
        add(f"d_skip{l}", 8)
        add(f"ssd_g{l}", 8)
        add(f"dtf_b{l}", 1)
        add(f"a_log{l}", 1)
    add("final_g", KD)
    for l in range(DEPTH):
        for name in ("pre_g", "mix_g", "post_g", "mem_g"):
            add(f"{name}{l}", KD)
        add(f"memq_g{l}", 1)
        add(f"memk_g{l}", 1)
    add("mu", NSHIFT)
    for name in ("w0", "a0", "kk_scale", "k_a", "r_k", "lnx_g", "lnx_b"):
        add(name, RW)
    add("bq_g", 1)
    add("kv_g", KD)
    add("kvk_g", 1)
    return out, at


VEC, NVEC = vec_columns()


def const_tables():
    i = np.arange(P)
    row, col = i[:, None], i[None, :]
    pick = (row % NDTF == np.arange(NDTF)).astype(float)
    parts = {"r_ident": np.eye(P), "r_neg_k": np.where(row <= col, 0.0, NEG),
             "r_neg_q": np.where(col <= row, 0.0, NEG), "pick": pick, "unpick": -pick,
             "ident": np.eye(P), "ones": np.ones((P, P)),
             "mean": np.full((P, 1), 1.0),
             "head2": np.stack([i < HD, i >= HD], 1),
             "head2_scaled": np.stack([i < HD, i >= HD], 1) * HD ** -0.5,
             "blk": row // HD == col // HD,
             "blkmean": (row // HD == col // HD) / HD}
    rot = np.zeros((P, P))
    rot[i[:HD] + HD, i[:HD]] = -1.0
    rot[i[:HD], i[:HD] + HD] = 1.0
    parts["rot"] = rot
    parts["incl"] = row <= col
    parts["strict_t"] = row < col
    parts["strict"] = row > col
    for level in range(7):
        b = 1 << level
        m = (row // (2 * b) == col // (2 * b)) & (row % (2 * b) >= b) & (col % (2 * b) < b)
        parts[f"level{level}"] = m
        if level == 0:
            parts["level0_t"] = m.T
    half = HD
    parts["freq"] = (10000.0 ** (-(i % half).astype(np.float64) / half))[:, None]
    parts["sign"] = np.where(i < DTF_F, 1.0, -1.0)[:, None]
    at, where, arrays = 0, {}, []
    for name, a in parts.items():
        where[name] = (at, a.shape[1])
        at += a.shape[1]
        arrays.append(np.asarray(a, np.float32))
    return where, np.concatenate(arrays, 1)


CONST, CONST_ARRAY = const_tables()
N_ROUNDED = CONST["ident"][0]


def decay_table():
    out = np.zeros((P, RET_HEADS, T), np.float64)
    d = np.arange(T)[None, :] - np.arange(P)[:, None]
    for h in range(RET_HEADS):
        out[:, h] = np.where(d >= 0, (1.0 - 2.0 ** (-5.0 - h)) ** np.maximum(d, 0), 0.0) * P ** -0.5
    return out.astype(np.float32)


def bucket_table():
    out = np.zeros((P, DIL, NREL), np.float32)
    e = 255 - np.arange(NREL)
    exact = BUCKETS // 2
    for g, (window, dil) in enumerate(((128, 1), (512, 4), (2048, 16))):
        dist = e * (1 if g == 0 else 4)
        ok = (dist >= 0) & (dist % dil == 0) & (dist // dil <= window // dil)
        f = np.maximum(dist, 1).astype(np.float32)
        large = exact + (np.log(f / np.float32(exact)) / np.float32(np.log(2048 / exact))
                         * np.float32(BUCKETS - exact)).astype(np.int32)
        bucket = np.where(dist < exact, dist, np.minimum(large, BUCKETS - 1))
        for x in range(NREL):
            out[bucket[x] if ok[x] else BUCKETS, g, x] = 1.0
    return out


class Signal:

    def __init__(self, handle):
        self.handle, self.total, self.base = handle, 0, 0

    def inc(self, k=1):
        self.total += k
        return self.handle, k

    def ge(self, n):
        return self.handle, self.base + n

    def so_far(self):
        return self.handle, self.total


def rep(ap, n):
    return bass.AP(ap.tensor, ap.offset, [*[list(d) for d in ap.ap], [0, n]])


def tiled(ap, n):
    first, *rest = [list(d) for d in ap.ap]
    return bass.AP(ap.tensor, ap.offset, [first, [0, n], *rest])


class Core:

    def __init__(self, nc, ctx, dram):
        self.nc, self.dram, self.ctx = nc, dram, ctx
        self.signals, self.joint = {}, None
        self.operand_ready = {}
        self.stream = dram["stream"]
        self.piece = 0
        self.raw = [self.sb(f"raw{s}", [P, KC, P]) for s in range(RING)]
        self.w_hi = [self.sb(f"w_hi{s}", [P, KC, P], F32R) for s in range(2)]
        self.w_lo = [self.sb(f"w_lo{s}", [P, KC, P], F32R) for s in range(2)]
        self.op = tuple(self.sb(n, [P, KC, T], F32R) for n in ("op_hi", "op_lo"))
        self.const = self.sb("const", [P, CONST_ARRAY.shape[1]])
        self.vec = self.sb("vec", [P, NVEC])
        self.x = self.sb("x", [P, KD, T])
        self.squares = self.sb("squares", [P, KD, T])
        self.acc = [ctx.enter_context(nc.psum_tensor(f"acc{s}", [P, T], F32)) for s in range(RING)]
        self.aux = [ctx.enter_context(nc.psum_tensor(f"aux{s}", [P, T], F32)) for s in range(4)]
        self.weights_ready = [self.sig(f"weights_ready{s}") for s in range(RING)]
        self.split_hi = self.sig("split_hi")
        self.split_done = self.sig("split_done")
        self.tile_done = self.sig("tile_done")
        self.bank_free = self.sig("bank_free")
        self.dve_order = self.sig("dve_order")
        self.act_order = self.sig("act_order")
        self.pool_order = self.sig("pool_order")
        self.loaded = self.sig("loaded")

    def sb(self, name, shape, dtype=F32, ctx=None):
        return (ctx or self.ctx).enter_context(self.nc.sbuf_tensor(name, shape, dtype))

    def sig(self, name):
        if name not in self.signals:
            self.signals[name] = Signal(self.ctx.enter_context(self.nc.semaphore(name)))
        return self.signals[name]

    def c(self, name, rows=P):
        at, n = CONST[name]
        return self.const[0:rows, at:at + n]

    def r(self, name):
        at, n = CONST[name]
        return self.rounded[:, at:at + n]

    def v(self, name, j=0, rows=P):
        at, _ = VEC[name]
        return self.vec[0:rows, at + j:at + j + 1]

    @contextmanager
    def together(self):
        with self.phase() as block:
            self.joint = block
            yield
            self.joint = None

    @contextmanager
    def phase(self):
        if self.joint:
            yield self.joint
            return
        for s in self.signals.values():
            s.base = s.total
        with self.nc.Block() as block:
            yield block

    def load_piece(self, sp, g, index=None):
        tensor, at, k = self.stream[g]
        src = self.dram[tensor][at] if index is None else \
            self.dram[tensor][bass.ds(index, 1)].rearrange("a p n -> (a p) n")
        dst = self.raw[g % RING][:, 0:k, :].rearrange("p k m -> p (k m)")
        sp.dma_start(dst, src).then_inc(self.weights_ready[g % RING].handle, 16)

    def load_behind(self, sp, g, end):
        free, lead, last = self.split_done, RING, len(self.stream)
        end = min(end, last - lead)
        while g < end:
            tensor, at, k = self.stream[g + lead]
            run = 0
            while g + run < end and self.stream[g + run + lead] == (tensor, at + run, k):
                run += 1
            loops = run // RING
            if loops >= 2:
                with sp.Fori(0, loops) as i:
                    for u in range(RING):
                        sp.wait_ge(free.handle, i * RING + (g + u + 1))
                        self.load_piece(sp, g + u + lead, i * RING + (at + u))
                g += loops * RING
            else:
                for u in range(min(run, RING)):
                    sp.wait_ge(free.handle, g + u + 1)
                    self.load_piece(sp, g + u + lead)
                g += min(run, RING)

    def split_piece_hi(self, act, g, i=0):
        s = g % RING
        act.wait_ge(self.weights_ready[s].handle, i * 16 + 16 * (g // RING + 1))
        act.activation(self.w_hi[g % 2][:, :, :], self.raw[s][:, :, :], ACT.Copy
                       ).then_inc(self.split_hi.handle, 1)

    def split_piece_lo(self, dve, g, i=0):
        dve.wait_ge(self.split_hi.handle, i * RING + (g + 1))
        dve.tensor_tensor(self.w_lo[g % 2][:, :, :], self.raw[g % RING][:, :, :],
                          self.w_hi[g % 2][:, :, :].bitcast(F32), ALU.subtract
                          ).then_inc(self.split_done.handle, 1)


def each(eng, count, body, unroll=False, first=0):
    loops = count // RING
    if loops >= first + 2 and not unroll:
        for u in range(first * RING):
            body(u, 0)
        with eng.Fori(first, loops) as i:
            for u in range(RING):
                body(u, i)
    else:
        loops = 0
    for u in range(loops * RING, count):
        body(u, 0)


def at(buf, j, lo=0, hi=T):
    if isinstance(j, int):
        return buf[:, j, lo:hi]
    return buf[:, bass.ds(j, 1), lo:hi].rearrange("p a t -> p (a t)")


class Segment:

    def __init__(self, count, moving, reader, body=None, n=T, product=None, after=0, ready=None):
        self.count, self.moving, self.reader, self.body = count, moving, reader, body
        self.ready = ready
        self.n, self.product, self.after = n, product, after


def linear(core, segments):
    g0, starts, g = core.piece, [], core.piece
    for s in segments:
        starts.append(g)
        g += s.count
    end, last = g, len(core.stream)
    gated, h_hi, h_lo = core.sig("ffn_gated"), core.sig("ffn_h_hi"), core.sig("ffn_h_lo")
    conv_summed, conv_done, _ = core.sig("conv_summed"), core.sig("conv_done"), core.sig("conv_tap")

    def bank_of(s, g):
        return core.acc[g % RING][:, 0:s.n]

    with core.phase() as block:
        @block.sync
        def _(sp):
            core.load_behind(sp, g0 + 2, end + 2)

        @block.tensor
        def _(pe):
            for s, start in zip(segments, starts):
                if s.after:
                    pe.wait_ge(*h_lo.ge(s.after))

                def one(u, i):
                    g = start + u
                    k_tiles = core.stream[g][2]
                    pe.wait_ge(core.split_done.handle, i * RING + (g + 1))
                    pe.wait_ge(core.bank_free.handle, i * RING + (g + 1))
                    hi, lo = s.moving
                    w_hi, w_lo = core.w_hi[g % 2], core.w_lo[g % 2]
                    for k in range(k_tiles):
                        if s.ready and u == 0 and isinstance(i, int):
                            pe.wait_ge(*s.ready[k])
                        for q, (w, a) in enumerate(((w_hi, hi), (w_hi, lo), (w_lo, hi))):
                            mm = pe.matmul(bank_of(s, g), w[:, k, :], a[:, k, 0:s.n],
                                           start=(k == 0 and q == 0), stop=(k == k_tiles - 1 and q == 2))
                    mm.then_inc(core.tile_done.handle, 1)
                each(pe, s.count, one, start + s.count + 2 > last, first=1 if s.ready else 0)

        @block.scalar
        def _(act):
            for s, start in zip(segments, starts):
                def one(u, i):
                    g = start + u
                    act.wait_ge(core.tile_done.handle, i * RING + (g + 1))
                    if g + 2 < last:
                        core.split_piece_hi(act, g + 2, i)
                    if s.reader == "conv":
                        s.body.keep(act, u, bank_of(s, g))
                        if u >= 2:
                            act.wait_ge(*conv_done.ge(u - 1))
                        s.body.begin(act, u, bank_of(s, g)).then_inc(core.bank_free.handle, 1)
                        act.wait_ge(*conv_summed.ge(u + 1))
                        s.body.end(act, u).then_inc(conv_done.handle, 1)
                    if s.reader == "act":
                        s.body(act, i * RING + u, bank_of(s, g)).then_inc(core.bank_free.handle, 1)
                    if s.reader == "swiglu":
                        j = i * (RING // 2) + u // 2
                        if u % 2 == 0:
                            act.activation(core.gate[:, u // 2 % 2, :], bank_of(s, g), ACT.Silu
                                           ).then_inc(gated.handle, 1)
                        else:
                            act.wait_ge(core.bank_free.handle, i * RING + (g + 1 + RING))
                            act.activation(at(s.product[0], j), core.product[:, u // 2 % 2, :], ACT.Copy
                                           ).then_inc(h_hi.handle, 1)
                each(act, s.count, one, start + s.count + 2 > last or s.reader == "conv")

        @block.vector
        def _(dve):
            pairs = 0
            for s, start in zip(segments, starts):
                def one(u, i):
                    g = start + u
                    if s.reader == "swiglu" and u % 2:
                        j = i * (RING // 2) + (u // 2 + 1 + pairs)
                        slot = u // 2 % 2
                        dve.wait_ge(gated.handle, j + gated.base)
                        dve.wait_ge(core.tile_done.handle, i * RING + (g + 1))
                        dve.tensor_tensor(core.product[:, slot, :], core.gate[:, slot, :],
                                          bank_of(s, g), ALU.mult).then_inc(core.bank_free.handle, 2)
                    if g + 2 < last:
                        core.split_piece_lo(dve, g + 2, i)
                    if s.reader == "swiglu" and u % 2:
                        dve.wait_ge(h_hi.handle, j + h_hi.base)
                        dve.tensor_tensor(at(s.product[1], i * (RING // 2) + u // 2),
                                          core.product[:, slot, :],
                                          at(s.product[0], i * (RING // 2) + u // 2).bitcast(F32),
                                          ALU.subtract).then_inc(h_lo.handle, 1)
                    if s.reader == "conv":
                        dve.wait_ge(core.bank_free.handle, g + 1 + RING)
                        s.body.taps(dve, u).then_inc(conv_summed.handle, 1)
                    if s.reader == "dve":
                        dve.wait_ge(core.tile_done.handle, i * RING + (g + 1))
                        s.body(dve, i * RING + u, bank_of(s, g)).then_inc(core.bank_free.handle, 1)
                each(dve, s.count, one, start + s.count + 2 > last or s.reader == "conv")
                if s.reader == "swiglu":
                    pairs += s.count // 2
        for signal in (conv_summed, conv_done):
            signal.total += sum(s.count for s in segments if s.reader == "conv")
        for signal in (gated, h_hi, h_lo):
            signal.total += sum(s.count for s in segments if s.reader == "swiglu") // 2
    core.piece = end

SECOND = True


def column(ap, n=P):
    return bass.AP(ap.tensor, ap.offset, [list(ap.ap[0]), [0, n]])


def split_tiles(core, act, dve, pool, srcs, pair, ready, bias=None, n=T):
    which = "" if pair is core.op else "2"
    hi_done, lo_dve, lo_pool = (core.sig(f"operand{which}_{s}") for s in ("hi", "lo_dve", "lo_pool"))
    hi, lo = pair
    if act:
        for j, src in enumerate(srcs):
            act.wait_ge(*ready(j))
            act.activation(hi[:, j, 0:n], src, ACT.Identity, bias=bias(j) if bias else 0.0
                           ).then_inc(*hi_done.inc())
    for eng, js in ((pool, [0, 2, 4]), (dve, [1, 3, 5, 6, 7])):
        if eng:
            if bias:
                js = [] if eng is pool else range(KC)
            for j in js:
                if j >= len(srcs):
                    continue
                eng.wait_ge(*hi_done.ge(j + 1))
                if bias:
                    eng.scalar_tensor_tensor(out=lo[:, j, 0:n], in0=srcs[j], scalar=bias(j),
                                             in1=hi[:, j, 0:n].bitcast(F32), op0=ALU.add,
                                             op1=ALU.subtract).then_inc(*lo_dve.inc())
                    core.operand_ready[lo.name, j] = lo_dve.so_far()
                else:
                    made = lo_dve if eng is dve else lo_pool
                    eng.tensor_tensor(lo[:, j, 0:n], srcs[j], hi[:, j, 0:n].bitcast(F32),
                                      ALU.subtract).then_inc(*made.inc())
                    core.operand_ready[lo.name, j] = made.so_far()


def operand(core, srcs, pair, n=T):
    with core.phase() as block:
        start = core.sig("operand_start")

        @block.vector
        def _(dve):
            dve.sem_inc(*start.inc())
            split_tiles(core, None, dve, None, srcs, pair, None, n=n)

        @block.scalar
        def _(act):
            split_tiles(core, act, None, None, srcs, pair, lambda j: start.ge(1), n=n)

        @block.gpsimd
        def _(pool):
            split_tiles(core, None, None, pool, srcs, pair, None, n=n)


def made_now(core, pair, count=KC):
    return [core.operand_ready[pair[1].name, j] for j in range(count)]


def norm(core, tiles, kind, scale, finish, eps=EPS, floor=None, n=T, result=None, bias=None):
    nj, nt = len(tiles), n // P
    per = {"all": 0, "tile": 1, "half": 2}[kind]
    cols = max(1, per * nj)
    squares, sums, roots = core.squares, core.sums, core.roots
    sq_act, sq_dve = core.sig("squares_act"), core.sig("squares_dve")
    summed, eps_added, rooted = core.sig("summed"), core.sig("eps_added"), core.sig("rooted")
    inverse, spread, applied = core.sig("inverse"), core.sig("spread"), core.sig("applied")
    stats = core.aux[0]
    banks = core.aux[1:4]
    n_spread = 1 if kind == "all" else nj

    with core.phase() as block:
        @block.scalar
        def _(act):
            for j in range(0, nj, 2):
                act.activation(squares[:, j, 0:n], tiles[j], ACT.Square).then_inc(*sq_act.inc())
            act.wait_ge(*eps_added.ge(1))
            act.activation(roots[:, 0:nt * cols], sums[:, 0:nt * cols], ACT.Sqrt).then_inc(*rooted.inc())
            if result:
                split_tiles(core, act, None, None, result, core.op, lambda j: applied.ge(j + 1), bias, n)

        if result and not bias:
            @block.gpsimd
            def _(pool):
                split_tiles(core, None, None, pool, result, core.op, None, bias, n)

        @block.tensor
        def _(pe):
            pe.wait_ge(*sq_act.ge((nj + 1) // 2))
            if nj > 1:
                pe.wait_ge(*sq_dve.ge(nj // 2))
            for t in range(nt):
                for j in range(nj):
                    w = max(1, per)
                    c0 = t * cols + (j * per if per else 0)
                    rhs = core.c("head2") if kind == "half" else core.c("mean")
                    mm = pe.matmul(stats[:, c0:c0 + w], squares[:, j, t * P:(t + 1) * P], rhs,
                                   start=(j == 0 or per > 0), stop=(j == nj - 1 or per > 0))
            mm.then_inc(*summed.inc())
            pe.wait_ge(*inverse.ge(1))
            for j in range(n_spread):
                if j >= 3:
                    pe.wait_ge(*applied.ge(j - 2))
                for t in range(nt):
                    c0 = t * cols + j * per
                    parts = max(1, per)
                    for e in range(parts):
                        rows = slice(e * P // parts, (e + 1) * P // parts)
                        mm = pe.matmul(banks[j % 3][rows, t * P:(t + 1) * P],
                                       column(sums[:, c0 + e:c0 + e + 1], P // parts),
                                       core.c("ident"), start=True, stop=True)
                mm.then_inc(*spread.inc())

        @block.vector
        def _(dve):
            for j in range(1, nj, 2):
                dve.tensor_tensor(squares[:, j, 0:n], tiles[j], tiles[j], ALU.mult).then_inc(*sq_dve.inc())
            dve.wait_ge(*summed.ge(1))
            dve.tensor_scalar(sums[:, 0:nt * cols], stats[:, 0:nt * cols], 1.0 if floor else scale,
                              0.0 if floor else eps, ALU.mult, ALU.add).then_inc(*eps_added.inc())
            dve.wait_ge(*rooted.ge(1))
            if floor:
                dve.tensor_scalar(roots[:, 0:nt * cols], roots[:, 0:nt * cols], floor, None,
                                  ALU.max).then_inc(*core.dve_order.inc())
                dve.wait_ge(*core.dve_order.so_far())
            dve.reciprocal(sums[:, 0:nt * cols], roots[:, 0:nt * cols]).then_inc(*inverse.inc())
            for j in range(nj):
                dve.wait_ge(*spread.ge(1 if kind == "all" else j + 1))
                bank = banks[0 if kind == "all" else j % 3]
                finish(dve, j, bank[:, 0:n]).then_inc(*applied.inc())
            if result:
                split_tiles(core, None, dve, None, result, core.op, None, bias, n)


def gained(core, dst, src, gain):
    def finish(dve, j, bank):
        return dve.scalar_tensor_tensor(out=dst(j), in0=src(j), scalar=gain(j), in1=bank,
                                        op0=ALU.mult, op1=ALU.mult)
    return finish


def rms_all(core, gain):
    norm(core, [core.x[:, k, :] for k in range(KD)], "all", 1.0 / D,
         gained(core, lambda j: core.squares[:, j, :], lambda j: core.x[:, j, :], lambda j: core.v(gain, j)),
         result=[core.squares[:, j, :] for j in range(KD)])


def load_ada(core, eng, run):
    eng.dma_start(core.ada[:, run % ADA_SLOTS, :, :, :].rearrange("p u k m -> p (u k m)"),
                 core.dram["ada"][run]).then_inc(*core.sig(f"ada_ready{run % ADA_SLOTS}").inc(16))


def setup(core):
    dram = core.dram
    cond = core.sig("cond_ready")
    with core.phase() as block:
        @block.sync
        def _(sp):
            for dst, src in ((core.const[:, :], dram["const"]), (core.cond[:, :], dram["c"]),
                             (core.vec[:, :], dram["vec"])):
                sp.dma_start(dst, src).then_inc(*core.loaded.inc(16))
            sp.dma_start(core.pos_i[:, :], dram["positions"].partition_broadcast(P)
                         ).then_inc(*core.loaded.inc(16))
            for run in range(0, ADA_SLOTS, 2):
                load_ada(core, sp, run)
            sp.wait_ge(*core.loaded.ge(64))

        @block.vector
        def _(dve):
            dve.sem_inc(core.bank_free.handle, RING)

        @block.scalar
        def _(act):
            for run in range(1, ADA_SLOTS, 2):
                load_ada(core, act, run)
            act.wait_ge(*core.loaded.ge(64))
            act.activation(core.cond[:, :], core.cond[:, :], ACT.Silu).then_inc(*cond.inc())
            act.activation(core.rounded[:, :], core.const[:, 0:N_ROUNDED], ACT.Copy).then_inc(*cond.inc())
            act.wait_ge(*cond.ge(2))


def modulation(core, ctx):
    ang, k, r = (core.sb(n, [P, T], ctx=ctx) for n in ("ang", "ang_k", "ang_r"))
    wrapped, sined = core.sig("wrapped"), core.sig("sin_made")
    ready, used = [core.sig(f"ada_ready{s}") for s in range(ADA_SLOTS)], core.sig("ada_used")
    with core.phase() as block:
        @block.sync
        def _(sp):
            for run in range(ADA_SLOTS, ADA_RUNS, 2):
                sp.wait_ge(*used.ge(run - ADA_SLOTS + 1))
                load_ada(core, sp, run)
            for g in range(RING):
                core.load_piece(sp, g)
            core.load_behind(sp, 0, 2)

        @block.tensor
        def _(pe):
            with pe.Fori(0, ADA_RUNS // ADA_SLOTS) as i:
                for slot in range(ADA_SLOTS):
                    pe.wait_ge(ready[slot].handle, i * 16 + 16)
                    for u in range(ADA_RUN):
                        j = i * (ADA_SLOTS * ADA_RUN) + (slot * ADA_RUN + u)
                        for k_tile in range(KD):
                            mm = pe.matmul(core.aux[0][:, bass.ds(j, 1)],
                                           core.ada[:, slot, u, k_tile, :],
                                           core.cond[:, k_tile:k_tile + 1], start=(k_tile == 0),
                                           stop=(k_tile == KD - 1))
                    mm.then_inc(used.handle, 1)

        used.total += ADA_RUNS

        @block.vector
        def _(dve):
            order = core.dve_order

            def step(ins):
                ins.then_inc(*order.inc())
                dve.wait_ge(*order.so_far())

            step(dve.memset(core.ones_row[:, :], 1.0))
            step(dve.tensor_copy(ang[:, :], core.pos_i[:, :]))
            step(dve.tensor_scalar(ang[:, :], ang[:, :], core.c("freq"), None, ALU.mult))
            for which in range(2):
                shift = 0.25 * which
                step(dve.tensor_scalar(k[:, :], ang[:, :], float(1 / TWO_PI), shift, ALU.mult, ALU.add))
                step(dve.tensor_scalar(k[:, :], k[:, :], ROUND, None, ALU.add))
                step(dve.tensor_scalar(k[:, :], k[:, :], -ROUND, None, ALU.add))
                if which:
                    dve.wait_ge(*sined.ge(1))
                step(dve.scalar_tensor_tensor(out=r[:, :], in0=k[:, :], scalar=-C1, in1=ang[:, :],
                                              op0=ALU.mult, op1=ALU.add))
                step(dve.scalar_tensor_tensor(out=r[:, :], in0=k[:, :], scalar=-C2, in1=r[:, :],
                                              op0=ALU.mult, op1=ALU.add))
                step(dve.scalar_tensor_tensor(out=r[:, :], in0=k[:, :], scalar=-C3, in1=r[:, :],
                                              op0=ALU.mult, op1=ALU.add))
                step(dve.tensor_scalar(r[:, :], r[:, :], float(np.pi / 2 * which), 3.1415925, ALU.add, ALU.min))
                dve.tensor_scalar(r[:, :], r[:, :], -3.1415925, None, ALU.max).then_inc(*wrapped.inc())
                if not which:
                    dve.wait_ge(*wrapped.ge(1))
            dve.wait_ge(*used.ge(ADA_RUNS))
            for l in range(DEPTH):
                b0 = VEC[f"b_ada{l}"][0]
                dve.tensor_tensor(core.mod[:, l, :], core.aux[0][:, l * 3 * KD:(l + 1) * 3 * KD],
                                  core.vec[:, b0:b0 + 3 * KD], ALU.add).then_inc(*order.inc())
            for g in range(2):
                core.split_piece_lo(dve, g)

        @block.scalar
        def _(act):
            act.wait_ge(*wrapped.ge(1))
            act.activation(core.sin[:, :], r[:, :], ACT.Sin).then_inc(*sined.inc())
            act.wait_ge(*wrapped.ge(2))
            act.activation(core.cos[:, :], r[:, :], ACT.Sin).then_inc(*sined.inc())
            for run in range(ADA_SLOTS + 1, ADA_RUNS, 2):
                act.wait_ge(*used.ge(run - ADA_SLOTS + 1))
                load_ada(core, act, run)
            act.dma_start(core.x[:, :, :], core.dram["x"]).then_inc(*core.loaded.inc(16))
            for g in range(2):
                core.split_piece_hi(act, g)
            act.wait_ge(*core.loaded.ge(16))


def gained_scale(core, l):
    gs = core.gs
    made = core.sig("gs_made")
    with core.phase() as block:
        @block.vector
        def _(dve):
            g0 = VEC[f"norm_g{l}"][0]
            dve.scalar_tensor_tensor(out=gs[:, :], in0=core.mod[:, l, KD:2 * KD], scalar=1.0,
                                     in1=core.vec[:, g0:g0 + KD], op0=ALU.add,
                                     op1=ALU.mult).then_inc(*made.inc())


def layer_norm_in(core, l):
    gs = core.gs
    norm(core, [core.x[:, k, :] for k in range(KD)], "all", 1.0 / D,
         gained(core, lambda j: core.squares[:, j, :], lambda j: core.x[:, j, :],
                lambda j: gs[:, j:j + 1]),
         result=[core.squares[:, j, :] for j in range(KD)], bias=lambda j: core.mod[:, l, j:j + 1])


def project(core, segments, n=T, ready=None):
    linear(core, [Segment(count, core.op, "act", body, n=n, ready=ready if i == 0 else None)
                  for i, (count, body) in enumerate(segments)])


def copy_to(buf, lo=0, hi=T, scale=1.0, func=ACT.Copy):
    return lambda act, j, bank: act.activation(at(buf, j, lo, hi), bank, func, scale=scale)


def token_major(core, src, count, dst, n=T, tag="v"):
    turned, stored = core.sig("turned"), core.sig("stored")
    units = [(t, j0) for t in range(n // P) for j0 in range(0, count, 4)]
    with core.phase() as block:
        @block.tensor
        def _(pe):
            for u, (t, j0) in enumerate(units):
                if u >= 4:
                    pe.wait_ge(*stored.ge(u - 3))
                for j in range(j0, min(j0 + 4, count)):
                    mm = pe.transpose(core.aux[u % 4][:, (j - j0) * P:(j - j0 + 1) * P],
                                      src(j)[:, t * P:(t + 1) * P], core.c("ident"))
                mm.then_inc(*turned.inc())

        @block.vector
        def _(dve):
            for u, (t, j0) in enumerate(units):
                w = (min(j0 + 4, count) - j0) * P
                dve.wait_ge(*turned.ge(u + 1))
                dve.tensor_copy(dst[:, t, j0 * P:j0 * P + w],
                                core.aux[u % 4][:, 0:w]).then_inc(*stored.inc())


def feature_major(core, src, count, dst, order=None, after=None):
    turned, stored = core.sig("turned"), core.sig("stored")
    with core.phase() as block:
        @block.tensor
        def _(pe):
            for j in range(count):
                if j >= 4:
                    pe.wait_ge(*stored.ge(j - 3))
                for t in range(NT):
                    out = core.aux[j % 4][:, t * P:(t + 1) * P]
                    mm = pe.transpose(out, src[:, t, j * P:(j + 1) * P], core.c("ident"))
                mm.then_inc(*turned.inc())

        @block.vector
        def _(dve):
            for j in range(count):
                dve.wait_ge(*turned.ge(j + 1))
                after(dve, j, core.aux[j % 4][:, :]).then_inc(*stored.inc())


def retention(core, l, mixed, ctx):
    qk = core.squares
    v = core.sb(f"ret_v{l}", [P, RET_HEADS, T], ctx=ctx)
    v_tok = core.sb(f"ret_vtok{l}", [P, NT, RET_HEADS * P], ctx=ctx)
    o = v
    decay = core.sb(f"ret_decay{l}", [P, RET_HEADS, T], ctx=ctx)
    part = core.sb(f"ret_part{l}", [P, 2, T], ctx=ctx)
    part2 = core.sb(f"ret_part2{l}", [P, 2, T], ctx=ctx)
    weights = core.sb(f"ret_w{l}", [P, 2, T], ctx=ctx)
    gained_scale(core, l)
    with core.together():
        layer_norm_in(core, l)
        project(core, [
            (2 * RET_HEADS, copy_to(qk)),
            (RET_HEADS, copy_to(v)),
            (RET_HEADS, copy_to(mixed, func=ACT.Silu))], ready=made_now(core, core.op))

    swapped, cosed, sined, turned = (core.sig(s) for s in ("rot_swapped", "rot_cos", "rot_sin", "rot_done"))
    with core.phase() as block:
        @block.sync
        def _(sp):
            sp.dma_start(decay[:, :, :], core.dram["decay"]).then_inc(*core.loaded.inc(16))
            sp.wait_ge(*core.loaded.ge(16))

        @block.tensor
        def _(pe):
            for j in range(2 * RET_HEADS):
                if j >= 2:
                    pe.wait_ge(*sined.ge(j - 1))
                pe.matmul(core.aux[j % 2][:, :], core.c("rot"), qk[:, j, :], start=True,
                          stop=True).then_inc(*swapped.inc())

        @block.gpsimd
        def _(pool):
            for j in range(2 * RET_HEADS):
                if j >= 2:
                    pool.wait_ge(*turned.ge(j - 1))
                pool.tensor_tensor(part[:, j % 2, :], qk[:, j, :], core.cos[:, :],
                                   ALU.mult).then_inc(*cosed.inc())

        @block.vector
        def _(dve):
            for j in range(2 * RET_HEADS):
                dve.wait_ge(*swapped.ge(j + 1))
                if j >= 2:
                    dve.wait_ge(*turned.ge(j - 1))
                dve.tensor_tensor(part2[:, j % 2, :], core.aux[j % 2][:, :], core.sin[:, :],
                                  ALU.mult).then_inc(*sined.inc())
                dve.wait_ge(*sined.ge(j + 1))
                dve.wait_ge(*cosed.ge(j + 1))
                dve.tensor_tensor(qk[:, j, :], part[:, j % 2, :], part2[:, j % 2, :],
                                  ALU.add).then_inc(*turned.inc())
    token_major(core, lambda j: v[:, j, :], RET_HEADS, v_tok)

    scored, weighted, summed, kept = (core.sig(s) for s in ("ret_scored", "ret_weighted", "ret_summed", "ret_kept"))
    units = [(h, jt) for h in range(RET_HEADS) for jt in range(NT)]
    with core.phase() as block:
        @block.tensor
        def _(pe):
            def score(u):
                h, jt = units[u]
                if u >= 2:
                    pe.wait_ge(*weighted.ge(u - 1))
                pe.matmul(core.aux[u % 2][:, 0:T - jt * P], qk[:, RET_HEADS + h, jt * P:(jt + 1) * P],
                          qk[:, h, jt * P:T], start=True, stop=True).then_inc(*scored.inc())

            score(0)
            for u, (h, jt) in enumerate(units):
                if u + 1 < len(units):
                    score(u + 1)
                pe.wait_ge(*weighted.ge(u + 1))
                if jt == 0 and h >= 2:
                    pe.wait_ge(*kept.ge(h - 1))
                mm = pe.matmul(core.aux[2 + h % 2][:, jt * P:T], v_tok[:, jt, h * P:(h + 1) * P],
                               weights[:, u % 2, 0:T - jt * P], start=(jt == 0), stop=(jt == NT - 1))
                mm.then_inc(*summed.inc())

        @block.vector
        def _(dve):
            for u, (h, jt) in enumerate(units):
                n = T - jt * P
                dve.wait_ge(*scored.ge(u + 1))
                if u >= 2:
                    dve.wait_ge(*summed.ge(u - 1))
                dve.tensor_tensor(weights[:, u % 2, 0:n], core.aux[u % 2][:, 0:n], decay[:, h, 0:n],
                                  ALU.mult).then_inc(*weighted.inc())

        @block.scalar
        def _(act):
            for h in range(RET_HEADS):
                act.wait_ge(*summed.ge(NT * (h + 1)))
                act.activation(o[:, h, :], core.aux[2 + h % 2][:, :], ACT.Copy).then_inc(*kept.inc())

    def finish(dve, j, bank):
        dve.tensor_tensor(o[:, j, :], o[:, j, :], bank, ALU.mult).then_inc(*core.dve_order.inc())
        dve.wait_ge(*core.dve_order.so_far())
        return dve.tensor_tensor(mixed[:, j, :], o[:, j, :], mixed[:, j, :], ALU.mult)
    norm(core, [o[:, h, :] for h in range(RET_HEADS)], "tile", 1.0 / P, finish)


class Convolution:

    def __init__(self, core, l, xbc, acc):
        self.core, self.l, self.xbc, self.acc = core, l, xbc, acc

    def weight(self, k, j):
        return self.core.v(f"conv_w{self.l}_{k}", j)

    def keep(self, act, j, bank):
        act.activation(self.xbc[:, j, CONV_K - 1:CONV_K - 1 + T], bank, ACT.Copy)

    def begin(self, act, j, bank):
        return act.activation(self.acc[:, j % 2, :], bank, ACT.Identity, scale=self.weight(3, j),
                              bias=self.core.v(f"conv_b{self.l}", j))

    def taps(self, dve, j):
        acc, tap = self.acc[:, j % 2, :], self.core.sig("conv_tap")
        for k in (2, 1, 0):
            if k < 2:
                dve.wait_ge(*tap.so_far())
            ins = dve.scalar_tensor_tensor(out=acc, in0=self.xbc[:, j, k:k + T], scalar=self.weight(k, j),
                                           in1=acc, op0=ALU.mult, op1=ALU.add)
            if k:
                ins.then_inc(*tap.inc())
        return ins

    def end(self, act, j):
        return act.activation(self.xbc[:, j, CONV_K - 1:CONV_K - 1 + T], self.acc[:, j % 2, :], ACT.Silu)


def ssd(core, l, mixed, ctx):
    xbc = core.sb(f"ssd_in{l}", [P, NXBC, CONV_K - 1 + T], ctx=ctx)
    work = core.squares
    raw = work[:, 6, :]
    tiny = core.sb(f"ssd_tiny{l}", [P, 4], ctx=ctx)
    w = [work[0:NDTF, i, :] for i in range(4)]
    zeroed = core.sig("zeroed")
    with core.phase() as block:
        @block.vector
        def _(dve):
            dve.memset(xbc[:, :, 0:CONV_K - 1], 0.0).then_inc(*zeroed.inc())
    linear(core, [
        Segment(NXBC, core.op, "conv", Convolution(core, l, xbc, work[:, 4:6, :])),
        Segment(8, core.op, "act", lambda act, j, bank: act.activation(at(mixed, j + SSD_T), bank, ACT.Silu)),
        Segment(1, core.op, "act", lambda act, j, bank: act.activation(raw, bank, ACT.Copy))])
    out = xbc[:, :, CONV_K - 1:CONV_K - 1 + T]

    soft = core.sig("soft_act")
    bias_made, z_made = core.sig("soft_bias"), core.sig("soft_z")
    z, e, lw, d = w
    cum = work[0:NDTF, 4:8, :]
    exped, dt_ready = core.sig("soft_exp"), core.sig("soft_w")
    with core.phase() as block:
        @block.scalar
        def _(act):
            act.wait_ge(*bias_made.ge(1))
            act.activation(z, raw[0:NDTF, :], ACT.Identity, scale=core.c("sign", NDTF),
                           bias=tiny[0:NDTF, 0:1]).then_inc(*soft.inc())
            act.activation(tiny[0:NDTF, 1:2], core.v(f"a_log{l}", 0, NDTF), ACT.Exp).then_inc(*soft.inc())
            act.wait_ge(*z_made.ge(1))
            act.activation(e, e, ACT.Exp, scale=-1.0).then_inc(*exped.inc())
            act.wait_ge(*dt_ready.ge(1))
            act.activation(lw, lw, ACT.Ln).then_inc(*exped.inc())

        @block.vector
        def _(dve):
            order = core.dve_order

            def step(ins):
                ins.then_inc(*order.inc())
                dve.wait_ge(*order.so_far())

            dve.tensor_tensor(tiny[0:NDTF, 0:1], core.v(f"dtf_b{l}", 0, NDTF), core.c("sign", NDTF),
                              ALU.mult).then_inc(*bias_made.inc())
            dve.wait_ge(*soft.ge(2))
            dve.memset(cum, 0.0).then_inc(*order.inc())
            dve.scalar_tensor_tensor(out=e, in0=z, scalar=-1.0, in1=z, op0=ALU.mult,
                                     op1=ALU.max).then_inc(*z_made.inc())
            step(dve.tensor_scalar(tiny[0:NDTF, 1:2], tiny[0:NDTF, 1:2], -1.0, None, ALU.mult))
            dve.wait_ge(*exped.ge(1))
            step(dve.tensor_scalar(lw, e, 1.0, None, ALU.add))
            dve.tensor_scalar(d, lw, -1.0, None, ALU.add).then_inc(*dt_ready.inc())
            dve.wait_ge(*exped.ge(2))
            step(dve.scalar_tensor_tensor(out=lw, in0=d, scalar=0.0, in1=lw, op0=ALU.is_equal, op1=ALU.add))
            step(dve.scalar_tensor_tensor(out=d, in0=d, scalar=0.0, in1=d, op0=ALU.is_equal, op1=ALU.add))
            step(dve.tensor_tensor(lw, lw, e, ALU.mult))
            step(dve.reciprocal(d, d))
            step(dve.tensor_tensor(lw, lw, d, ALU.mult))
            step(dve.scalar_tensor_tensor(out=z, in0=z, scalar=0.0, in1=lw, op0=ALU.max, op1=ALU.add))
            step(dve.tensor_scalar(d, z, tiny[0:NDTF, 1:2], None, ALU.mult))
            ones16 = core.ones_row[0:SSD_HEADS, :]
            for b in range(NT):
                dve.tensor_tensor_scan(cum[0:SSD_HEADS, b, b * P:T], ones16[:, b * P:T],
                                       d[0:SSD_HEADS, b * P:T], 0.0, ALU.mult, ALU.add).then_inc(*order.inc())
            dve.tensor_tensor_scan(cum[DTF_F:DTF_F + FOX_HEADS, 0, :],
                                   core.ones_row[DTF_F:DTF_F + FOX_HEADS, :],
                                   d[DTF_F:DTF_F + FOX_HEADS, :], 0.0, ALU.mult,
                                   ALU.add).then_inc(*order.inc())
    dt = z

    xdt = core.squares[:, :, :].rearrange("p (b k) t -> p b (k t)", b=NT)
    dt_tok = core.sb(f"ssd_dt{l}", [P, NT, NDTF], ctx=ctx)
    ncum = core.sb(f"ssd_ncum{l}", [P, NT, NDTF], ctx=ctx)
    cb_at = [0, T, 2 * T - P, 3 * T - 3 * P]
    cb = core.sb(f"ssd_cb{l}", [P, SSD_GROUPS, 4 * T - 6 * P], ctx=ctx)
    made, cols, cum_hi = core.sig("col_turned"), core.sig("col_stored"), core.sig("cum_hi")
    with core.phase() as block:
        @block.tensor
        def _(pe):
            for b in range(NT):
                pe.transpose(core.aux[0][:, b * NDTF:(b + 1) * NDTF], dt[:, b * P:(b + 1) * P],
                             core.c("ident", NDTF)[:, 0:NDTF])
                pe.transpose(core.aux[0][:, (NT + b) * NDTF:(NT + b + 1) * NDTF],
                             cum[:, b, b * P:(b + 1) * P],
                             core.c("ident", NDTF)[:, 0:NDTF]).then_inc(*made.inc())
            u = 0
            for g in range(SSD_GROUPS):
                for b in range(NT):
                    bank = core.aux[1 + u % 3]
                    if u >= 3:
                        pe.wait_ge(*cols.ge(2 + u - 2))
                    pe.matmul(bank[:, 0:T - b * P], out[:, 8 + g, b * P:(b + 1) * P],
                              out[:, 10 + g, b * P:T], start=True, stop=True).then_inc(*made.inc())
                    u += 1

        @block.scalar
        def _(act):
            act.activation(core.cum[0:NDTF, :, :], cum, ACT.Copy).then_inc(*cum_hi.inc())

        @block.vector
        def _(dve):
            dve.wait_ge(*cum_hi.ge(1))
            dve.tensor_tensor(core.cum[NDTF:P, :, :], cum, core.cum[0:NDTF, :, :].bitcast(F32),
                              ALU.subtract).then_inc(*core.dve_order.inc())
            dve.wait_ge(*made.ge(NT))
            dve.tensor_copy(dt_tok[:, :, :].rearrange("p b c -> p (b c)"),
                            core.aux[0][:, 0:NT * NDTF]).then_inc(*cols.inc())
            dve.tensor_scalar(ncum[:, :, :].rearrange("p b c -> p (b c)"),
                              core.aux[0][:, NT * NDTF:2 * NT * NDTF], -1.0, None,
                              ALU.mult).then_inc(*cols.inc())
            u = 0
            for g in range(SSD_GROUPS):
                for b in range(NT):
                    dve.wait_ge(*made.ge(NT + u + 1))
                    dve.tensor_copy(cb[:, g, cb_at[b]:cb_at[b] + T - b * P],
                                    core.aux[1 + u % 3][:, 0:T - b * P]).then_inc(*cols.inc())
                    u += 1
    turned, stored = core.sig("turned"), core.sig("stored")
    units = [(b, g) for b in range(NT) for g in range(2)]
    with core.phase() as block:
        @block.tensor
        def _(pe):
            for u, (b, g) in enumerate(units):
                if u >= 4:
                    pe.wait_ge(*stored.ge(u - 3))
                for j in range(4):
                    mm = pe.transpose(core.aux[u % 4][:, j * P:(j + 1) * P],
                                      out[:, 4 * g + j, b * P:(b + 1) * P], core.c("ident"))
                mm.then_inc(*turned.inc())

        @block.vector
        def _(dve):
            for u, (b, g) in enumerate(units):
                dve.wait_ge(*turned.ge(u + 1))
                dve.tensor_tensor(
                    xdt[:, b, g * T:(g + 1) * T].rearrange("p (h d) -> p h d", d=SSD_DIM),
                    core.aux[u % 4][:, :].rearrange("p (h d) -> p h d", d=SSD_DIM),
                    rep(dt_tok[:, b, 8 * g:8 * g + 8], SSD_DIM), ALU.mult).then_inc(*stored.inc())

    spread, exps, weighted, summed, kept = (core.sig(s) for s in (
        "ssd_spread", "ssd_exp", "ssd_weighted", "ssd_summed", "ssd_kept"))
    EX = 4
    ex = core.sb(f"ssd_ex{l}", [P, EX, T], ctx=ctx)
    y = core.sb(f"ssd_y{l}", [P, 2, T], ctx=ctx)
    units = [(h, b) for h in range(SSD_HEADS) for b in range(NT)]
    with core.phase() as block:
        @block.tensor
        def _(pe):
            def decay(u):
                h, b = units[u]
                n = T - b * P
                if u >= 4:
                    pe.wait_ge(*exps.ge(u - 3))
                bank = core.aux[u % 4]
                pe.matmul(bank[:, 0:n], column(core.r("pick")[:, h:h + 1]),
                          core.cum[:, b, b * P:T], start=True, stop=False)
                pe.matmul(bank[:, 0:P], core.r("r_ident"), core.r("r_neg_k"), start=False, stop=True
                          ).then_inc(*spread.inc())

            for u in range(3):
                decay(u)
            for u, (h, b) in enumerate(units):
                if u + 3 < len(units):
                    decay(u + 3)
                pe.wait_ge(*weighted.ge(u + 1))
                pair, half = h // 2, h % 2
                if b == 0 and half == 0 and pair >= 4:
                    pe.wait_ge(*kept.ge(pair - 3))
                mm = pe.matmul(core.acc[pair % 4][half * HD:half * HD + HD, b * P:T],
                               xdt[:, b, h * SSD_DIM:(h + 1) * SSD_DIM], ex[:, u % EX, 0:T - b * P],
                               start=(b == 0), stop=(b == NT - 1))
                mm.then_inc(*summed.inc())

        @block.scalar
        def _(act):
            for u, (h, b) in enumerate(units):
                n = T - b * P
                act.wait_ge(*spread.ge(u + 1))
                if u >= EX:
                    act.wait_ge(*summed.ge(u - EX + 1))
                act.activation(ex[:, u % EX, 0:n], core.aux[u % 4][:, 0:n], ACT.Exp,
                               bias=ncum[:, b, h:h + 1]).then_inc(*exps.inc())

        @block.vector
        def _(dve):
            for u, (h, b) in enumerate(units):
                n = T - b * P
                dve.wait_ge(*exps.ge(u + 1))
                dve.tensor_tensor(ex[:, u % EX, 0:n], ex[:, u % EX, 0:n], cb[:, h // 8, cb_at[b]:cb_at[b] + n],
                                  ALU.mult).then_inc(*weighted.inc())
                if h % 2 == 1 and b == NT - 1:
                    pair = h // 2
                    dve.wait_ge(*summed.ge(u + 1))
                    dve.scalar_tensor_tensor(out=y[:, pair % 2, :], in0=out[:, pair, :],
                                             scalar=core.v(f"d_skip{l}", pair), in1=core.acc[pair % 4][:, :],
                                             op0=ALU.mult, op1=ALU.add).then_inc(*kept.inc())
                    dve.wait_ge(*kept.ge(pair + 1))
                    dve.tensor_tensor(mixed[:, SSD_T + pair, :], y[:, pair % 2, :], mixed[:, SSD_T + pair, :],
                                      ALU.mult).then_inc(*core.dve_order.inc())
    norm(core, [mixed[:, SSD_T + j, :] for j in range(8)], "all", 1.0 / 1024,
         gained(core, lambda j: mixed[:, SSD_T + j, :], lambda j: mixed[:, SSD_T + j, :],
                lambda j: core.v(f"ssd_g{l}", j)))


def attention_buffers(core, name, ctx):
    core.att_probs = core.sb(name + "_probs", [P, 2, T], ctx=ctx)
    core.att_probs_t = core.sb(name + "_probs_t", [P, 2, T], ctx=ctx)


def attention(core, units, out_tok):
    scored, maxed, exped, turned, copied, summed, kept = (core.sig("att_" + s) for s in (
        "scored", "maxed", "exped", "turned", "copied", "summed", "kept"))
    order = core.dve_order
    probs, probs_t = core.att_probs, core.att_probs_t
    small = core.att_small
    N = len(units)
    with core.phase() as block:
        @block.tensor
        def _(pe):
            def score(u):
                if u >= 2:
                    pe.wait_ge(*exped.ge(u - 1))
                parts = units[u]["scores"]
                for q, (lhsT, rhs, lo) in enumerate(parts):
                    n = rhs.free_size()
                    mm = pe.matmul(core.aux[u % 2][:, lo:lo + n], lhsT, rhs, start=(q == 0),
                                   stop=(q == len(parts) - 1), skip_group_check=True)
                mm.then_inc(*scored.inc())

            def turn(u):
                pe.wait_ge(*exped.ge(u + 1))
                if u >= 2:
                    pe.wait_ge(*copied.ge(u - 1))
                for b in range(units[u]["keys"] // P):
                    mm = pe.transpose(core.aux[2 + u % 2][:, b * P:(b + 1) * P],
                                      probs[:, u % 2, b * P:(b + 1) * P], core.c("ident"))
                mm.then_inc(*turned.inc())

            def values(u):
                pe.wait_ge(*copied.ge(u + 1))
                if u >= 4:
                    pe.wait_ge(*kept.ge(u - 3))
                vs = units[u]["values"]
                for b, v in enumerate(vs):
                    mm = pe.matmul(core.acc[u % 4][:, 0:HD], probs_t[:, u % 2, b * P:(b + 1) * P], v,
                                   start=(b == 0), stop=(b == len(vs) - 1))
                mm.then_inc(*summed.inc())

            for s in range(N + 2):
                if s < N:
                    score(s)
                if 1 <= s <= N:
                    turn(s - 1)
                if s >= 2:
                    values(s - 2)

        @block.scalar
        def _(act):
            def exp(u):
                n = units[u]["keys"]
                act.wait_ge(*maxed.ge(u + 1))
                if u >= 2:
                    act.wait_ge(*turned.ge(u - 1))
                if u >= 4:
                    act.wait_ge(*kept.ge(u - 3))
                total = units[u].get("sum", small[:, 4 + u % 4:5 + u % 4])
                act.activation(probs[:, u % 2, 0:n], core.aux[u % 2][:, 0:n], ACT.Exp,
                               bias=small[:, u % 4:u % 4 + 1], accum_out=total).then_inc(*exped.inc())

            def copy(u):
                n = units[u]["keys"]
                act.wait_ge(*turned.ge(u + 1))
                if u >= 2:
                    act.wait_ge(*summed.ge(u - 1))
                act.activation(probs_t[:, u % 2, 0:n], core.aux[2 + u % 2][:, 0:n],
                               ACT.Copy).then_inc(*copied.inc())

            for s in range(N + 1):
                if s < N:
                    exp(s)
                if s >= 1:
                    copy(s - 1)

        @block.vector
        def _(dve):
            def maximum(u):
                n = units[u]["keys"]
                dve.wait_ge(*scored.ge(u + 1))
                if u >= 4:
                    dve.wait_ge(*exped.ge(u - 3))
                dve.tensor_reduce(small[:, u % 4:u % 4 + 1], core.aux[u % 2][:, 0:n], AX_X, ALU.max,
                                  negate=True).then_inc(*maxed.inc())
                if "max" in units[u]:
                    dve.wait_ge(*maxed.ge(u + 1))
                    dve.tensor_scalar(units[u]["max"], small[:, u % 4:u % 4 + 1], -1.0, None,
                                      ALU.mult).then_inc(*order.inc())

            def keep(u):
                out = units[u]["out"]
                if "max" in units[u]:
                    dve.wait_ge(*summed.ge(u + 1))
                    dve.tensor_copy(out, core.acc[u % 4][:, 0:HD]).then_inc(*kept.inc())
                    return
                dve.wait_ge(*exped.ge(u + 1))
                dve.reciprocal(small[:, 8 + u % 4:9 + u % 4], small[:, 4 + u % 4:5 + u % 4]
                               ).then_inc(*order.inc())
                dve.wait_ge(*order.so_far())
                dve.wait_ge(*summed.ge(u + 1))
                dve.tensor_scalar(out, core.acc[u % 4][:, 0:HD], small[:, 8 + u % 4:9 + u % 4], None,
                                  ALU.mult).then_inc(*kept.inc())

            for s in range(N + 3):
                if s < N:
                    maximum(s)
                if s >= 3:
                    keep(s - 3)


def fox(core, l, mixed, ctx):
    def one_head_each(act, q, j, bank):
        act.activation(at(q, j * 2), bank, ACT.Copy, scale=core.c("head2_scaled")[:, 0:1])
        return act.activation(at(q, j * 2 + 1), bank, ACT.Copy, scale=core.c("head2_scaled")[:, 1:2])

    q = core.sb(f"fox_q{l}", [P, FOX_HEADS, T], ctx=ctx)
    k = core.sb(f"fox_k{l}", [P, 4, T], ctx=ctx)
    v = core.squares[:, 0:4, :]
    v_tok = core.sb(f"fox_vtok{l}", [P, NT, T], ctx=ctx)
    o_tok = v
    attention_buffers(core, f"fox{l}", ctx)
    project(core, [
        (4, lambda act, j, bank: one_head_each(act, q, j, bank)),
        (4, copy_to(k)),
        (4, copy_to(v)),
        (4, lambda act, j, bank: act.activation(at(mixed, j + FOX_T), bank, ACT.Silu))])
    token_major(core, lambda j: v[:, j, :], 4, v_tok)
    units = []
    for h in range(FOX_HEADS):
        pick, unpick = (core.r(n)[:, DTF_F + h:DTF_F + h + 1] for n in ("pick", "unpick"))
        for t in range(NT):
            n = (t + 1) * P
            units.append({
                "keys": n,
                "scores": [(q[:, h, t * P:n], k[:, h // 2, 0:n], 0),
                           (column(unpick), core.cum[:, 0, 0:n], 0),
                           (core.cum[:, 0, t * P:n], column(pick, n), 0),
                           (core.r("r_ident"), core.r("r_neg_q"), t * P)],
                "values": [v_tok[:, b, h * HD:(h + 1) * HD] for b in range(t + 1)],
                "out": o_tok[:, t, h * HD:(h + 1) * HD]})
    attention(core, units, o_tok)
    feature_major(core, o_tok, 4, None, after=lambda dve, j, bank: dve.tensor_tensor(
        mixed[:, FOX_T + j, :], bank, mixed[:, FOX_T + j, :], ALU.mult))


def add_to_x(core, scale):
    return lambda dve, j, bank: dve.scalar_tensor_tensor(
        out=at(core.x, j), in0=bank, scalar=scale(j), in1=at(core.x, j), op0=ALU.mult, op1=ALU.add)


def first_block(core):
    with ExitStack() as ctx:
        core.cos, core.sin = (core.sb(n, [P, T], ctx=ctx) for n in ("cos", "sin"))
        core.cum = core.sb("cum", [P, NT, T], F32R, ctx=ctx)
        core.rounded = core.sb("rounded", [P, N_ROUNDED], F32R, ctx=ctx)
        with ExitStack() as inner:
            core.ada = core.sb("ada", [P, ADA_SLOTS, ADA_RUN, KD, P], ctx=inner)
            core.pos_i = core.sb("pos_i", [P, T], I32, ctx=inner)
            setup(core)
            modulation(core, inner)
        for l in range(DEPTH):
            with ExitStack() as layer:
                mixed = core.sb(f"mixed{l}", [P, MIX, T], ctx=layer)
                for branch in (retention, ssd, fox):
                    with ExitStack() as inner:
                        branch(core, l, mixed, inner)
                gate = lambda j: core.mod[:, l, 2 * KD + j:2 * KD + j + 1] if isinstance(j, int) \
                    else core.mod[:, l, bass.ds(j + 2 * KD, 1)]
                second = tuple(core.sb(f"op2_{part}{l}", [P, KC, T], F32R, ctx=layer) for part in "hl")
                with core.together():
                    operand(core, [mixed[:, k, :] for k in range(KC)], core.op)
                    operand(core, [mixed[:, KC + k, :] for k in range(KC)], second)
                    linear(core, [Segment(KD, pair, "dve", add_to_x(core, gate), ready=made_now(core, pair))
                                  for pair in (core.op, second)])
    norm(core, [core.x[:, k, :] for k in range(KD)], "all", 1.0 / D,
         gained(core, lambda j: core.x[:, j, :], lambda j: core.x[:, j, :], lambda j: core.v("final_g", j)))


def swiglu(core, gain, name):
    with ExitStack() as ctx:
        core.gate = core.sb(f"ffn_gate_{name}", [P, 2, T], ctx=ctx)
        core.product = core.sb(f"ffn_product_{name}", [P, 2, T], ctx=ctx)
        h = [tuple(core.sb(f"ffn_{part}{i}_{name}", [P, KC, T], F32R, ctx=ctx) for part in "hl")
             for i in range(2)]
        segments = []
        with core.together():
            rms_all(core, gain)
            for kind, c in FF_ORDER:
                if kind == "pairs":
                    segments.append(Segment(2 * FF_CHUNKS[c], core.op, "swiglu", product=h[c % 2],
                                            ready=None if c else made_now(core, core.op)))
                else:
                    segments.append(Segment(KD, h[c % 2], "dve", add_to_x(core, lambda j: 0.5),
                                            after=sum(FF_CHUNKS[:c + 1])))
            linear(core, segments)


def masked_gains(core, dst, gain):
    with core.phase() as block:
        @block.vector
        def _(dve):
            dve.tensor_scalar(dst, core.c("head2_scaled"), core.v(gain), None,
                              ALU.mult).then_inc(*core.dve_order.inc())


def split_heads(dst, src, gains):
    def finish(dve, j, bank):
        for e in range(2):
            ins = dve.scalar_tensor_tensor(out=dst(2 * j + e), in0=src(j), scalar=gains[:, e:e + 1],
                                           in1=bank, op0=ALU.mult, op1=ALU.mult)
        return ins
    return finish


def memory_keys(core, l, k, v_tok, ctx):
    mem = core.sb(f"mem{l}", [P, KD, MEM], ctx=ctx)
    v = core.sb(f"mem_v{l}", [P, 2, MEM], ctx=ctx)
    with core.phase() as block:
        @block.sync
        def _(sp):
            sp.dma_start(mem[:, :, :], core.dram["mem"]).then_inc(*core.loaded.inc(16))
            sp.wait_ge(*core.loaded.ge(16))
    with core.together():
        norm(core, [mem[:, j, :] for j in range(KD)], "all", 1.0 / D,
             gained(core, lambda j: mem[:, j, :], lambda j: mem[:, j, :], lambda j: core.v(f"mem_g{l}", j)),
             n=MEM, result=[mem[:, j, :] for j in range(KD)])
        project(core, [(2, copy_to(k, hi=MEM)), (2, copy_to(v, hi=MEM))], n=MEM, ready=made_now(core, core.op))
    norm(core, [k[:, j, :] for j in range(2)], "half", 1.0 / HD,
         gained(core, lambda j: k[:, j, :], lambda j: k[:, j, :], lambda j: core.v(f"memk_g{l}")), n=MEM)
    token_major(core, lambda j: v[:, j, :], 2, v_tok, n=MEM)


def memory_attention(core, l, q_raw, k, v_tok, out, ctx):
    q = core.sb(f"mem_q{l}", [P, MEM_HEADS, T], ctx=ctx)
    gains = core.sb(f"mem_gains{l}", [P, 2], ctx=ctx)
    o_tok = core.sb(f"mem_o{l}", [P, NT, MEM], ctx=ctx)
    attention_buffers(core, f"mem{l}", ctx)
    masked_gains(core, gains[:, :], f"memq_g{l}")
    norm(core, [q_raw(j) for j in range(2)], "half", 1.0 / HD,
         split_heads(lambda h: q[:, h, :], q_raw, gains))
    units = [{"keys": MEM,
              "scores": [(q[:, h, t * P:(t + 1) * P], k[:, h // 2, :], 0)],
              "values": [v_tok[:, b, h * HD:(h + 1) * HD] for b in range(MEM // P)],
              "out": o_tok[:, t, h * HD:(h + 1) * HD]}
             for h in range(MEM_HEADS) for t in range(NT)]
    attention(core, units, o_tok)
    feature_major(core, o_tok, 2, None, after=lambda dve, j, bank: dve.tensor_copy(out(j), bank))


def rwkv(core, p, ctx):
    kk = core.sb("kk", [P, RW, T], ctx=ctx)
    lora = core.sb("lora", [P, 2 * RW, P], ctx=ctx)
    extra = core.sb("rwkv_work", [P, 17, T], ctx=ctx)
    state = core.sb("state", [P, P], ctx=ctx)
    joined = core.sb("state_joined", [P, P], ctx=ctx)
    ec = core.sb("exp_center", [P, NT], ctx=ctx)
    carry = core.sb("state_carry", [P, NT], ctx=ctx)
    tile = lambda j: p[:, j, 1:1 + T]

    def work(i):
        return core.squares[:, i, :] if i < 8 else extra[:, i - 8, :]

    def chunks(ap):
        return ap.rearrange("p (n t) -> p n t", n=NT)

    def chunk(ap, n):
        return ap[:, n * P:(n + 1) * P]

    def pred(name):
        return tiled(core.c(name).bitcast(U32), NT)

    diffed, own, shifted = (core.sig("shift_" + s) for s in ("diff", "own_diff", "done"))
    by_pool = [j for j in range(NSHIFT) if j % 3 != 2]
    with core.phase() as block:
        @block.sync
        def _(sp):
            sp.dma_start(lora[:, :, :].rearrange("p k m -> p (k m)"), core.dram["lora"]
                         ).then_inc(*core.loaded.inc(16))
            sp.wait_ge(*core.loaded.ge(16))

        @block.gpsimd
        def _(pool):
            for j in by_pool:
                if j >= 8:
                    pool.wait_ge(*shifted.ge(j - 7))
                pool.tensor_tensor(core.squares[:, j % 8, :], p[:, j, 0:T], tile(j),
                                   ALU.subtract).then_inc(*diffed.inc())

        @block.vector
        def _(dve):
            for j in range(NSHIFT):
                if j in by_pool:
                    dve.wait_ge(*diffed.ge(by_pool.index(j) + 1))
                else:
                    dve.tensor_tensor(core.squares[:, j % 8, :], p[:, j, 0:T], tile(j),
                                      ALU.subtract).then_inc(*own.inc())
                    dve.wait_ge(*own.so_far())
                dve.scalar_tensor_tensor(out=tile(j), in0=core.squares[:, j % 8, :], scalar=core.v("mu", j),
                                         in1=tile(j), op0=ALU.mult, op1=ALU.add).then_inc(*shifted.inc())
    with core.phase() as block:
        @block.scalar
        def _(act):
            act.activation(tile(18)[0:HD, :], tile(18)[0:HD, :], ACT.Tanh).then_inc(*core.act_order.inc())
            act.activation(tile(19), tile(19), ACT.Sigmoid).then_inc(*core.act_order.inc())

        @block.vector
        def _(dve):
            for m in range(RW):
                dve.tensor_scalar(kk[:, m, :], tile(RW + m), core.v("kk_scale", m), None,
                                  ALU.mult).then_inc(*core.dve_order.inc())

        @block.gpsimd
        def _(pool):
            for i in range(15, 25):
                pool.memset(work(i), 0.0).then_inc(*core.pool_order.inc())
    norm(core, [kk[:, m, :] for m in range(RW)], "half", 1.0,
         lambda dve, j, bank: dve.tensor_tensor(kk[:, j, :], kk[:, j, :], bank, ALU.mult), floor=1e-12)
    for m in range(RW):
        rwkv_heads(core, m, tile, kk, lora, work, state, joined, ec, carry, chunks, chunk, pred)

    centered, meaned = core.sig("ln_centered"), core.sig("ln_mean")
    gate_up = extra[:, 0:2, :].rearrange("p a t -> p (a t)")[:, 0:RW * P]
    with core.phase() as block:
        @block.sync
        def _(sp):
            sp.dma_start(gate_up, core.dram["gate_up"]).then_inc(*core.loaded.inc(16))
            sp.wait_ge(*core.loaded.ge(16))

        @block.tensor
        def _(pe):
            for m in range(RW):
                if m >= 4:
                    pe.wait_ge(*centered.ge(m - 3))
                pe.matmul(core.aux[m % 4][:, :], core.c("blkmean"), tile(m), start=True,
                          stop=True).then_inc(*meaned.inc())

        @block.vector
        def _(dve):
            for m in range(RW):
                dve.wait_ge(*meaned.ge(m + 1))
                dve.tensor_tensor(tile(m), tile(m), core.aux[m % 4][:, :],
                                  ALU.subtract).then_inc(*centered.inc())

    def finish(dve, m, bank):
        order = core.dve_order
        dve.scalar_tensor_tensor(out=tile(m), in0=tile(m), scalar=core.v("lnx_g", m), in1=bank,
                                 op0=ALU.mult, op1=ALU.mult).then_inc(*order.inc())
        dve.wait_ge(*order.so_far())
        return dve.scalar_tensor_tensor(out=tile(m), in0=tile(m), scalar=core.v("lnx_b", m),
                                        in1=tile(RW + m), op0=ALU.add, op1=ALU.add)
    norm(core, [tile(m) for m in range(RW)], "half", 1.0 / HD, finish, eps=LNX_EPS)
    gate_made, gated = core.sig("gate_made"), core.sig("gate_used")
    with core.phase() as block:
        @block.tensor
        def _(pe):
            for m in range(RW):
                if m >= 4:
                    pe.wait_ge(*gated.ge(m - 3))
                pe.matmul(core.aux[m % 4][:, :], gate_up[:, m * P:(m + 1) * P], tile(19), start=True,
                          stop=True).then_inc(*gate_made.inc())

        @block.vector
        def _(dve):
            for m in range(RW):
                dve.wait_ge(*gate_made.ge(m + 1))
                dve.tensor_tensor(tile(m), tile(m), core.aux[m % 4][:, :], ALU.mult).then_inc(*gated.inc())


def rwkv_heads(core, m, tile, kk, lora, work, state, joined, ec, carry, chunks, chunk, pred):
    r, k, v = tile(m), tile(RW + m), tile(2 * RW + m)
    lw, a, kmod, lc, ex, e1, e2 = (work(i) for i in range(7))
    kkq, rq, bh, kh = (work(i) for i in range(7, 11))
    kkq_e, rq_e = (work(3), work(4)), (work(5), work(6))
    kkq_t, bh_t, kh_t, v_t = (work(i) for i in range(11, 15))
    A, ak, rb, rk, a0 = ((work(15 + 2 * i), work(16 + 2 * i)) for i in range(5))
    X, Dm, C, G = (work(3), work(4)), (work(5), work(6)), (work(0), work(1)), (work(2), work(7))
    wt, z, u0, sa = work(9), work(10), work(0), work(1)
    order = core.dve_order

    def stepper(dve):
        def step(ins):
            ins.then_inc(*order.inc())
            dve.wait_ge(*order.so_far())
        return step

    lora_done, squashed, centered = core.sig("lora_done"), core.sig("lora_act"), core.sig("decay_sums")
    factored = core.sig("factored")
    exped, bonus_in, bonus_sum = core.sig("decay_exp"), core.sig("bonus_in"), core.sig("bonus_sum")
    with core.phase() as block:
        @block.tensor
        def _(pe):
            pe.matmul(core.aux[0][:, :], lora[:, m, :], tile(18), start=True, stop=True
                      ).then_inc(*lora_done.inc())
            pe.matmul(core.aux[1][:, :], lora[:, RW + m, :], tile(18), start=True, stop=True
                      ).then_inc(*lora_done.inc())
            pe.wait_ge(*bonus_in.ge(1))
            pe.matmul(core.aux[2][:, :], core.c("blk"), kkq_t, start=True, stop=True
                      ).then_inc(*bonus_sum.inc())

        @block.scalar
        def _(act):
            act.wait_ge(*lora_done.ge(1))
            act.activation(lw, core.aux[0][:, :], ACT.Sigmoid, bias=core.v("w0", m)).then_inc(*squashed.inc())
            act.wait_ge(*lora_done.ge(2))
            act.activation(a, core.aux[1][:, :], ACT.Sigmoid, bias=core.v("a0", m)).then_inc(*squashed.inc())
            act.wait_ge(*centered.ge(1))
            act.activation(ex, ex, ACT.Exp).then_inc(*exped.inc())
            act.activation(e1, lc, ACT.Exp).then_inc(*exped.inc())
            act.activation(e2, lc, ACT.Exp, scale=-1.0).then_inc(*exped.inc())
            act.activation(ec[:, :], ec[:, :], ACT.Exp).then_inc(*exped.inc())
            for made, src, dsts in ((1, kkq, kkq_e), (5, rq, rq_e)):
                act.wait_ge(*factored.ge(made))
                for e in range(2):
                    act.activation(dsts[e], src, ACT.Copy, scale=core.c("head2")[:, e:e + 1]
                                   ).then_inc(*core.act_order.inc())

        @block.vector
        def _(dve):
            step = stepper(dve)
            dve.wait_ge(*squashed.ge(1))
            step(dve.tensor_scalar(lw, lw, DECAY_SCALE, None, ALU.mult))
            for n in range(NT):
                dve.tensor_tensor_scan(chunk(e1, n), core.c("ones"), chunk(lw, n), 0.0, ALU.mult,
                                       ALU.add).then_inc(*order.inc())
            dve.wait_ge(*order.so_far())
            middle = chunks(e1)[:, :, P // 2 - 1:P // 2]
            dve.tensor_copy(ec[:, :], middle.rearrange("p n a -> p (n a)")).then_inc(*order.inc())
            spread = bass.AP(middle.tensor, middle.offset, [*[list(d) for d in middle.ap[:2]], [0, P]])
            step(dve.tensor_tensor(chunks(lc), chunks(e1), spread, ALU.subtract))
            dve.tensor_tensor(ex, lc, lw, ALU.subtract).then_inc(*centered.inc())
            dve.wait_ge(*squashed.ge(2))
            step(dve.tensor_scalar(kmod, a, -1.0, core.v("k_a", m), ALU.add, ALU.mult))
            step(dve.scalar_tensor_tensor(out=kmod, in0=kmod, scalar=1.0, in1=k, op0=ALU.add, op1=ALU.mult))
            dve.scalar_tensor_tensor(out=kkq_t, in0=r, scalar=core.v("r_k", m), in1=kmod, op0=ALU.mult,
                                     op1=ALU.mult).then_inc(*bonus_in.inc())
            step(dve.tensor_tensor(a, kk[:, m, :], a, ALU.mult))
            dve.wait_ge(*exped.ge(4))
            dve.tensor_tensor(kkq, kk[:, m, :], ex, ALU.mult).then_inc(*factored.inc())
            dve.tensor_tensor(rq, r, e1, ALU.mult).then_inc(*factored.inc())
            dve.tensor_tensor(bh, a, e2, ALU.mult).then_inc(*factored.inc())
            dve.tensor_tensor(kh, kmod, e2, ALU.mult).then_inc(*factored.inc())
            last = chunks(e1)[:, 0:NT - 1, P - 1:P].rearrange("p n a -> p (n a)")
            dve.tensor_tensor(carry[:, 0:NT - 1], last, ec[:, 1:NT], ALU.mult).then_inc(*factored.inc())
            dve.wait_ge(*bonus_sum.ge(1))
            dve.tensor_tensor(k, core.aux[2][:, :], v, ALU.mult).then_inc(*order.inc())

    turned, kept = core.sig("rwkv_turned"), core.sig("rwkv_kept")
    pairs = ((kkq, kkq_t), (bh, bh_t), (kh, kh_t), (v, v_t))
    products = [(out[e], lhsT[e], rhs[e], mask) for out, lhsT, rhs, mask in (
        (A, kkq_e, (bh, bh), "strict"), (a0, (bh, bh), kkq_e, "level0_t"),
        (ak, (kh, kh), kkq_e, "strict_t"), (rb, (bh, bh), rq_e, "incl"),
        (rk, (kh, kh), rq_e, "incl")) for e in range(2)]
    with core.phase() as block:
        @block.tensor
        def _(pe):
            for i, (src, _) in enumerate(pairs):
                for n in range(NT):
                    mm = pe.transpose(chunk(core.aux[i], n), chunk(src, n), core.c("ident"))
                mm.then_inc(*turned.inc())
            for i, (_, lhsT, rhs, _) in enumerate(products):
                if i >= 4:
                    pe.wait_ge(*kept.ge(i - 3))
                for n in range(NT):
                    mm = pe.matmul(chunk(core.acc[i % 4], n), chunk(lhsT, n), chunk(rhs, n),
                                   start=True, stop=True)
                mm.then_inc(*turned.inc())

        @block.scalar
        def _(act):
            for i, (_, dst) in enumerate(pairs):
                act.wait_ge(*turned.ge(i + 1))
                act.activation(dst, core.aux[i][:, :], ACT.Copy).then_inc(*core.act_order.inc())

        @block.vector
        def _(dve):
            for i, (dst, _, _, mask) in enumerate(products):
                dve.wait_ge(*turned.ge(len(pairs) + i + 1))
                dve.copy_predicated(chunks(dst), pred(mask), chunks(core.acc[i % 4][:, :])
                                    ).then_inc(*kept.inc())

    def columns_of(ap, level, which):
        b = 1 << level
        return ap.rearrange("p (k c) -> p k c", c=2 * b)[:, :, which * b:(which + 1) * b]

    started, picked, first, copied = (core.sig(s) for s in ("inv_start", "inv_pick", "inv_first", "inv_copied"))
    second, third, x_new, d_new = (core.sig(s) for s in ("inv_second", "inv_third", "inv_x", "inv_d"))
    ident = tiled(core.c("ident"), NT)
    with core.phase() as block:
        @block.gpsimd
        def _(pool):
            for level in range(7):
                for e in range(2):
                    if level == 1:
                        pool.wait_ge(*started.ge(2 * e + 2))
                    elif level > 1:
                        pool.wait_ge(*first.ge(2 * (level - 2) + e + 1))
                    pool.tensor_tensor(chunks(C[e]), chunks(A[e]), tiled(core.c(f"level{level}"), NT),
                                       ALU.mult).then_inc(*picked.inc())

        @block.tensor
        def _(pe):
            for level in range(1, 7):
                i = 2 * (level - 1)
                for e in range(2):
                    pe.wait_ge(*picked.ge(2 * level + e + 1))
                    if level == 1:
                        pe.wait_ge(*started.ge(2 * e + 2))
                    else:
                        pe.wait_ge(*x_new.ge(i - 2 + e + 1))
                    for n in range(NT):
                        mm = pe.matmul(chunk(core.aux[e], n), chunk(C[e], n), chunk(X[e], n),
                                       start=True, stop=True)
                    mm.then_inc(*first.inc())
                for e in range(2):
                    pe.wait_ge(*copied.ge(i + e + 1))
                    if level > 1:
                        pe.wait_ge(*d_new.ge(i - 2 + e + 1))
                    for n in range(NT):
                        mm = pe.matmul(columns_of(chunk(core.aux[2 + e], n), level, 1), chunk(Dm[e], n),
                                       columns_of(chunk(G[e], n), level, 1), start=True, stop=True)
                    mm.then_inc(*second.inc())
                    if level < 6:
                        for n in range(NT):
                            mm = pe.matmul(columns_of(chunk(core.acc[e], n), level, 0), chunk(G[e], n),
                                           columns_of(chunk(Dm[e], n), level, 0), start=True, stop=True)
                        mm.then_inc(*third.inc())

        @block.scalar
        def _(act):
            for level in range(1, 7):
                for e in range(2):
                    i = 2 * (level - 1) + e
                    act.wait_ge(*first.ge(i + 1))
                    if level > 1:
                        act.wait_ge(*third.ge(i - 1))
                    act.activation(G[e], core.aux[e][:, :], ACT.Copy).then_inc(*copied.inc())

        @block.vector
        def _(dve):
            for e in range(2):
                dve.tensor_tensor(chunks(X[e]), ident, chunks(a0[e]), ALU.subtract).then_inc(*started.inc())
                dve.wait_ge(*picked.ge(e + 1))
                dve.tensor_tensor(chunks(Dm[e]), ident, chunks(C[e]), ALU.subtract).then_inc(*started.inc())
            for level in range(1, 7):
                for e in range(2):
                    i = 2 * (level - 1) + e
                    dve.wait_ge(*second.ge(i + 1))
                    x = columns_of(X[e], level, 1)
                    dve.tensor_tensor(x, x, columns_of(core.aux[2 + e][:, :], level, 1), ALU.subtract
                                      ).then_inc(*x_new.inc())
                    if level < 6:
                        dve.wait_ge(*third.ge(i + 1))
                        d = columns_of(Dm[e], level, 0)
                        dve.tensor_tensor(d, d, columns_of(core.acc[e][:, :], level, 0), ALU.subtract
                                          ).then_inc(*d_new.inc())

    half = lambda ap, n, e: ap[:, n * P + e * HD:n * P + (e + 1) * HD]
    done, stored = core.sig("solve_done"), core.sig("solve_kept")
    with core.phase() as block:
        @block.tensor
        def _(pe):
            for n in range(NT):
                for e in range(2):
                    mm = pe.matmul(half(core.aux[0], n, e), chunk(ak[e], n), half(v_t, n, e), start=True,
                                   stop=True)
            mm.then_inc(*done.inc())
            for n in range(NT):
                for e in range(2):
                    mm = pe.matmul(chunk(core.aux[1][e * HD:(e + 1) * HD, :], n), half(kkq_t, n, e),
                                   chunk(X[e], n), start=True, stop=True)
            mm.then_inc(*done.inc())
            pe.wait_ge(*stored.ge(1))
            for n in range(NT):
                for e in range(2):
                    mm = pe.matmul(half(core.aux[2], n, e), chunk(X[e], n), half(z, n, e), start=True,
                                   stop=True)
            mm.then_inc(*done.inc())

        @block.scalar
        def _(act):
            for i, dst in enumerate((z, wt, u0)):
                act.wait_ge(*done.ge(i + 1))
                act.activation(dst, core.aux[i][:, :], ACT.Copy).then_inc(*stored.inc())

    from_state, corrected, added, moved, out_done = (core.sig(s) for s in (
        "seq_from_state", "seq_corrected", "seq_added", "seq_state", "seq_out"))
    y = core.aux[2]
    with core.phase() as block:
        @block.tensor
        def _(pe):
            for n in range(NT):
                if n:
                    pe.wait_ge(*moved.ge(n))
                    pe.matmul(core.aux[0][:, 0:P], chunk(wt, n), state[:, :], start=True, stop=True
                              ).then_inc(*from_state.inc())
                    pe.matmul(chunk(y, n), state[:, :], chunk(rq, n), start=True, stop=False,
                              skip_group_check=True)
                for e in range(2):
                    pe.matmul(chunk(y[e * HD:(e + 1) * HD, :], n), half(v_t, n, e), chunk(rk[e], n),
                              start=(n == 0), stop=False, skip_group_check=True)
                pe.wait_ge(*corrected.ge(n + 1))
                if n < NT - 1:
                    pe.matmul(core.aux[1][:, 0:P], chunk(bh_t, n), chunk(sa, n), start=True, stop=False)
                    pe.matmul(core.aux[1][:, 0:P], chunk(kh_t, n), chunk(v_t, n), start=False, stop=True
                              ).then_inc(*added.inc())
                for e in range(2):
                    mm = pe.matmul(chunk(y[e * HD:(e + 1) * HD, :], n), half(sa, n, e), chunk(rb[e], n),
                                   start=False, stop=True, skip_group_check=True)
            mm.then_inc(*out_done.inc())

        @block.vector
        def _(dve):
            step = stepper(dve)
            for n in range(NT):
                if n:
                    dve.wait_ge(*from_state.ge(n))
                    dve.scalar_tensor_tensor(out=chunk(sa, n), in0=core.aux[0][:, 0:P], scalar=-1.0,
                                             in1=chunk(u0, n), op0=ALU.mult,
                                             op1=ALU.subtract).then_inc(*corrected.inc())
                else:
                    dve.tensor_scalar(chunk(sa, n), chunk(u0, n), -1.0, None, ALU.mult
                                      ).then_inc(*corrected.inc())
                if n < NT - 1:
                    dve.wait_ge(*added.ge(n + 1))
                    if n:
                        step(dve.tensor_tensor(joined[:, :], core.aux[1][:, 0:P], state[:, :], ALU.add))
                    else:
                        step(dve.tensor_copy(joined[:, :], core.aux[1][:, 0:P]))
                    dve.scalar_tensor_tensor(out=state[:, :], in0=joined[:, :], scalar=carry[:, n:n + 1],
                                             in1=core.c("blk"), op0=ALU.mult,
                                             op1=ALU.mult).then_inc(*moved.inc())

        @block.scalar
        def _(act):
            act.wait_ge(*out_done.ge(1))
            act.activation(r, y[:, :], ACT.Copy).then_inc(*core.act_order.inc())


def shared_keys(core, k, v_tok):
    with ExitStack() as ctx:
        v = core.sb("dil_v", [P, 2 * DIL, T], ctx=ctx)
        with core.together():
            rms_all(core, "kv_g")
            project(core, [(2 * DIL, copy_to(k)), (2 * DIL, copy_to(v))], ready=made_now(core, core.op))
        norm(core, [k[:, j, :] for j in range(2 * DIL)], "half", 1.0 / HD,
             gained(core, lambda j: k[:, j, :], lambda j: k[:, j, :], lambda j: core.v("kvk_g")))
        turned, stored = core.sig("turned"), core.sig("stored")
        units = [(g, t) for g in range(DIL) for t in range(NT)]
        with core.phase() as block:
            @block.tensor
            def _(pe):
                for u, (g, t) in enumerate(units):
                    if u >= 4:
                        pe.wait_ge(*stored.ge(u - 3))
                    for j in range(2):
                        mm = pe.transpose(core.aux[u % 4][:, j * P:(j + 1) * P],
                                          tokens(v[:, 2 * g + j, :], g, t), core.c("ident"))
                    mm.then_inc(*turned.inc())

            @block.vector
            def _(dve):
                for u, (g, t) in enumerate(units):
                    dve.wait_ge(*turned.ge(u + 1))
                    dve.tensor_copy(v_tok[:, t, g * 2 * P:(g + 1) * 2 * P], core.aux[u % 4][:, 0:2 * P]
                                    ).then_inc(*stored.inc())


def tokens(ap, g, t):
    return ap[:, t * P:(t + 1) * P] if g == 0 else ap.rearrange("p (a r) -> p r a", r=NT)[:, t, :]


def relative_bias(core, bias, ctx):
    table = core.sb("rel_table", [P, 12], ctx=ctx)
    buckets = core.sb("buckets", [P, DIL, NREL], ctx=ctx)
    rows = core.sb("rel_rows", [P, 12, NREL], ctx=ctx)
    cleared, spread, kept = core.sig("rel_cleared"), core.sig("rel_spread"), core.sig("rel_kept")
    written, read = core.sig("rel_written"), core.sig("rel_read")
    skew = core.dram["skew"]
    with core.phase() as block:
        @block.sync
        def _(sp):
            sp.dma_start(buckets[:, :, :], core.dram["buckets"]).then_inc(*core.loaded.inc(16))
            sp.wait_ge(*cleared.ge(2))
            sp.dma_start(table[0:BUCKETS, :], core.dram["rel"]).then_inc(*core.loaded.inc(16))
            for h in range(12):
                sp.wait_ge(*kept.ge(h + 1))
                sp.dma_start(skew[h], rows[:, h, :]).then_inc(*written.inc(16))
            sp.wait_ge(*written.ge(12 * 16))
            for h in range(12):
                first, n = (P - 1, 2 * P) if h < DIL_HEADS else (2 * P - 1, P)
                src = bass.AP(skew.tensor, skew.offset + h * P * NREL + first, [[NREL - 1, P], [1, n]])
                sp.dma_start(bias[:, h, 0:n], src).then_inc(*read.inc(16))
            sp.wait_ge(*read.ge(12 * 16))

        @block.vector
        def _(dve):
            dve.memset(table[:, :], 0.0).then_inc(*cleared.inc())
            dve.wait_ge(*cleared.ge(1))
            dve.memset(table[BUCKETS:BUCKETS + 1, :], NEG).then_inc(*cleared.inc())
            for h in range(12):
                dve.wait_ge(*spread.ge(h + 1))
                dve.tensor_copy(rows[:, h, :], core.aux[h % 4][:, 0:NREL]).then_inc(*kept.inc())

        @block.tensor
        def _(pe):
            pe.wait_ge(*core.loaded.ge(32))
            for h in range(12):
                if h >= 4:
                    pe.wait_ge(*kept.ge(h - 3))
                pe.matmul(core.aux[h % 4][:, 0:NREL], column(table[:, h:h + 1]),
                          buckets[:, h // DIL_HEADS, :], start=True, stop=True).then_inc(*spread.inc())


def dilated(core, k, v_tok, out, q_raw):
    with ExitStack() as ctx:
        bias = core.sb("rel_bias", [P, 12, 2 * P], ctx=ctx)
        with ExitStack() as inner:
            relative_bias(core, bias, inner)
        q = core.sb("dil_q", [P, 12, T], ctx=ctx)
        gains = core.sb("dil_gains", [P, 2], ctx=ctx)
        masked_gains(core, gains[:, :], "bq_g")
        norm(core, [q_raw(j) for j in range(2 * DIL)], "half", 1.0 / HD,
             split_heads(lambda h: q[:, h, :], q_raw, gains))
        attention_buffers(core, "dil", ctx)
        o_tok = core.squares[:, 0:6, :].rearrange("p a t -> p (a t)").rearrange("p (n c) -> p n c", n=NT)
        top = core.sb("dil_max", [P, DIL, NT, DIL_HEADS], ctx=ctx)
        total = core.sb("dil_sum", [P, DIL, NT, DIL_HEADS], ctx=ctx)
        units = []
        for g in range(DIL):
            for h in range(DIL_HEADS):
                head = g * DIL_HEADS + h
                for t in range(NT):
                    if g == 0:
                        t0 = max(t - 1, 0)
                        keys = k[:, head // 2, t0 * P:(t + 1) * P]
                        b = bias[:, head, (P if t == 0 else 0):2 * P]
                        vs = [v_tok[:, x, head * HD:(head + 1) * HD] for x in range(t0, t + 1)]
                    else:
                        keys = tokens(k[:, head // 2, :], g, t)
                        b = bias[:, head, 0:P]
                        vs = [v_tok[:, t, head * HD:(head + 1) * HD]]
                    units.append({"keys": len(vs) * P, "values": vs,
                                  "scores": [(tokens(q[:, head, :], g, t), keys, 0),
                                             (core.c("ident"), b, 0)],
                                  "out": o_tok[:, t, head * HD:(head + 1) * HD],
                                  "max": top[:, g, t, h:h + 1], "sum": total[:, g, t, h:h + 1]})
        attention(core, units, o_tok)

        peak = q[0:DIL_HEADS, 7, :]
        weight = [q[:, g, :] for g in range(DIL)]
        sums = [q[0:DIL_HEADS, 3 + g, :] for g in range(DIL)]
        norm_sum = q[0:DIL_HEADS, 6, :]
        o = [q_raw(i) for i in range(2 * DIL)]
        turned, cleared, less, exped = (core.sig(s) for s in ("mix_turned", "mix_cleared", "mix_less", "mix_exp"))
        with core.phase() as block:
            @block.tensor
            def _(pe):
                for g in range(DIL):
                    for src, bank in ((top, core.aux[g]), (total, core.acc[g])):
                        for t in range(NT):
                            mm = pe.transpose(tokens(bank[0:DIL_HEADS, :], g, t), src[:, g, t, :],
                                              core.c("ident"))
                        mm.then_inc(*turned.inc())

            @block.vector
            def _(dve):
                order = core.dve_order

                def step(ins):
                    ins.then_inc(*order.inc())
                    dve.wait_ge(*order.so_far())

                for g in range(DIL):
                    dve.memset(weight[g], 0.0).then_inc(*order.inc())
                dve.wait_ge(*order.so_far())
                dve.wait_ge(*turned.ge(2 * DIL))
                w = [x[0:DIL_HEADS, :] for x in weight]
                for g in range(DIL):
                    dve.tensor_copy(w[g], core.aux[g][0:DIL_HEADS, :]).then_inc(*order.inc())
                    dve.tensor_copy(sums[g], core.acc[g][0:DIL_HEADS, :]).then_inc(*order.inc())
                dve.wait_ge(*order.so_far())
                step(dve.tensor_tensor(peak, w[0], w[1], ALU.max))
                step(dve.tensor_tensor(peak, peak, w[2], ALU.max))
                for g in range(DIL):
                    dve.tensor_tensor(w[g], w[g], peak, ALU.subtract).then_inc(*less.inc())
                dve.wait_ge(*exped.ge(DIL))
                for g in range(DIL):
                    step(dve.tensor_tensor(sums[g], sums[g], w[g], ALU.mult))
                step(dve.tensor_tensor(norm_sum, sums[0], sums[1], ALU.add))
                step(dve.tensor_tensor(norm_sum, norm_sum, sums[2], ALU.add))
                step(dve.reciprocal(norm_sum, norm_sum))
                for g in range(DIL):
                    step(dve.tensor_tensor(w[g], w[g], norm_sum, ALU.mult))

            @block.scalar
            def _(act):
                for g in range(DIL):
                    act.wait_ge(*less.ge(g + 1))
                    act.activation(weight[g][0:DIL_HEADS, :], weight[g][0:DIL_HEADS, :], ACT.Exp
                                   ).then_inc(*exped.inc())

        fm, fm_kept, spread, used = (core.sig(s) for s in ("mix_fm", "mix_fm_kept", "mix_spread", "mix_used"))
        with core.phase() as block:
            @block.tensor
            def _(pe):
                for g in range(DIL):
                    for j in range(2):
                        i = 2 * g + j
                        if i >= 4:
                            pe.wait_ge(*fm_kept.ge(i - 3))
                        for t in range(NT):
                            mm = pe.transpose(tokens(core.aux[i % 4][:, :], g, t),
                                              o_tok[:, t, i * P:(i + 1) * P], core.c("ident"))
                        mm.then_inc(*fm.inc())
                        if i >= 4:
                            pe.wait_ge(*used.ge(i - 3))
                        for e in range(2):
                            mm = pe.matmul(core.acc[i % 4][e * HD:(e + 1) * HD, :],
                                           column(core.c("ident")[:, 2 * j + e:2 * j + e + 1], HD),
                                           weight[g], start=True, stop=True)
                        mm.then_inc(*spread.inc())

            @block.vector
            def _(dve):
                order = core.dve_order
                for g in range(DIL):
                    for j in range(2):
                        i = 2 * g + j
                        dve.wait_ge(*fm.ge(i + 1))
                        dve.tensor_copy(o[i], core.aux[i % 4][:, :]).then_inc(*fm_kept.inc())
                        dve.wait_ge(*fm_kept.ge(i + 1))
                        dve.wait_ge(*spread.ge(i + 1))
                        dve.tensor_tensor(o[i], o[i], core.acc[i % 4][:, :], ALU.mult
                                          ).then_inc(*used.inc())
                dve.wait_ge(*used.ge(2 * DIL))
                for j in range(2):
                    dve.tensor_tensor(o[j], o[j], o[2 + j], ALU.add).then_inc(*order.inc())
                dve.wait_ge(*order.so_far())
                for j in range(2):
                    dve.tensor_tensor(out(j), o[j], o[4 + j], ALU.add).then_inc(*order.inc())


def second_block(core):
    swiglu(core, "pre_g0", "pre0")
    with ExitStack() as ctx:
        p = core.sb("rwkv_p", [P, A_TILES, 1 + T], ctx=ctx)
        tile = lambda j: p[:, j, 1:1 + T]
        with ExitStack() as inner:
            k = core.sb("mem_k0", [P, 2, MEM], ctx=inner)
            v_tok = core.sb("mem_vt0", [P, 2, MEM], ctx=inner)
            with ExitStack() as keys:
                memory_keys(core, 0, k, v_tok, keys)
            with core.phase() as block:
                @block.vector
                def _(dve):
                    dve.memset(p[:, :, 0:1], 0.0).then_inc(*core.dve_order.inc())
            with core.together():
                rms_all(core, "mix_g0")
                project(core, [(A_TILES, copy_to(p, 1, 1 + T))], ready=made_now(core, core.op))
            memory_attention(core, 0, lambda j: tile(NSHIFT + j), k, v_tok, lambda j: tile(NSHIFT + j), inner)
        with ExitStack() as inner:
            rwkv(core, p, inner)
        with core.together():
            operand(core, [tile(j if j < RW else NSHIFT + j - RW) for j in range(KD)], core.op)
            linear(core, [Segment(KD, core.op, "dve", add_to_x(core, lambda j: 1.0),
                                  ready=made_now(core, core.op))])
    swiglu(core, "post_g0", "post0")

    with ExitStack() as ctx:
        k = core.sb("dil_k", [P, 2 * DIL, T], ctx=ctx)
        v_tok = core.sb("dil_vt", [P, NT, 12 * HD], ctx=ctx)
        shared_keys(core, k, v_tok)
        swiglu(core, "pre_g1", "pre1")
        y = core.sb("mix_y", [P, 4, T], ctx=ctx)
        with ExitStack() as inner:
            mk = core.sb("mem_k1", [P, 2, MEM], ctx=inner)
            mv_tok = core.sb("mem_vt1", [P, 2, MEM], ctx=inner)
            with ExitStack() as keys:
                memory_keys(core, 1, mk, mv_tok, keys)
            raw = core.sb("b_q", [P, 2 * DIL + 2, T], ctx=inner)
            with core.together():
                rms_all(core, "mix_g1")
                project(core, [(2 * DIL + 2, copy_to(raw))], ready=made_now(core, core.op))
            with ExitStack() as mem_ctx:
                memory_attention(core, 1, lambda j: raw[:, 2 * DIL + j, :], mk, mv_tok,
                                 lambda j: y[:, 2 + j, :], mem_ctx)
            dilated(core, k, v_tok, lambda j: y[:, j, :], lambda j: raw[:, j, :])
        with core.together():
            operand(core, [y[:, j, :] for j in range(4)], core.op)
            linear(core, [Segment(KD, core.op, "dve", add_to_x(core, lambda j: 1.0),
                                  ready=made_now(core, core.op, 4))])
    swiglu(core, "post_g1", "post1")


def store(core):
    stored = core.sig("out_stored")
    with core.phase() as block:
        @block.sync
        def _(sp):
            sp.dma_start(core.dram["out"], core.x[:, :, :]).then_inc(*stored.inc(16))
            sp.wait_ge(*stored.ge(16))


def build(nc, dram):
    with ExitStack() as ctx:
        core = Core(nc, ctx, dram)
        core.cond = core.sb("cond", [P, KD])
        core.mod = core.sb("mod", [P, DEPTH, 3 * KD])
        core.gs = core.sb("gs", [P, KD])
        core.sums = core.sb("sums", [P, 64])
        core.roots = core.sb("roots", [P, 64])
        core.ones_row = core.sb("ones_row", [NDTF, T])
        core.att_small = core.sb("att_small", [P, 12])
        first_block(core)
        second_block(core)
        store(core)


def weight_stream(a):
    used, stream = {}, []

    def add(w):
        k, n = w.shape
        name = f"w{k // P}"
        at = sum(x.shape[1] // P for x in used.setdefault(name, []))
        used[name].append(w)
        stream.extend((name, at + i, k // P) for i in range(n // P))

    def swiglu(w_in, w_out):
        for kind, c in FF_ORDER:
            first, last = sum(FF_CHUNKS[:c]), sum(FF_CHUNKS[:c + 1])
            if kind == "sum":
                add(w_out[first * P:last * P])
                continue
            for i in range(first, last):
                add(w_in[:, i * P:(i + 1) * P])
                add(w_in[:, FF + i * P:FF + (i + 1) * P])

    for l in range(DEPTH):
        w = a["w_in"][l]
        n = 2048 + 1536
        add(w[:, :n])
        add(w[:, n + 16:n + 16 + 1024])
        dtf = np.zeros((D, P), w.dtype)
        dtf[:, 0:SSD_HEADS] = w[:, n:n + 16]
        dtf[:, DTF_F:DTF_F + FOX_HEADS] = w[:, -FOX_HEADS:]
        add(dtf)
        add(w[:, n + 16 + 1024:-FOX_HEADS])
        for half in range(2):
            add(a["w_out"][l][half * D:(half + 1) * D])
    if SECOND:
        for l in range(DEPTH):
            swiglu(a["ffn_pre_w_in_2"][l], a["ffn_pre_w_out_2"][l])
            add(a["mem_w_kv_2"][l])
            if l == 0:
                add(a["a_w_in_2"][0])
                add(a["a_w_out_2"][0])
            else:
                add(a["b_w_q_2"][0])
                add(a["b_w_out_2"][0])
            swiglu(a["ffn_post_w_in_2"][l], a["ffn_post_w_out_2"][l])
            if l == 0:
                add(a["kv_w_2"])
    arrays = {}
    for name, ws in used.items():
        k = ws[0].shape[0]
        out = arrays[name] = np.empty((sum(w.shape[1] for w in ws) // P, P, k // P, P), np.float32)
        at = 0
        for w in ws:
            n = w.shape[1] // P
            out[at:at + n] = w.reshape(k // P, P, n, P).transpose(2, 1, 0, 3)
            at += n
        arrays[name] = out.reshape(-1, P, k)
    return arrays, stream


def feature_columns(v):
    return v.reshape(-1, P).T


def packed_vectors(a):
    out = np.zeros((P, NVEC), np.float32)

    def put(name, v):
        at, n = VEC[name]
        out[:, at:at + n] = feature_columns(v)

    for l in range(DEPTH):
        put(f"norm_g{l}", a["norm_g"][l])
        put(f"b_ada{l}", a["b_ada"][l])
        for k in range(CONV_K):
            put(f"conv_w{l}_{k}", a["conv_w"][l, k])
        put(f"conv_b{l}", a["conv_b"][l])
        put(f"d_skip{l}", np.repeat(a["d_skip"][l], SSD_DIM))
        put(f"ssd_g{l}", a["ssd_norm_g"][l])
        at = VEC[f"dtf_b{l}"][0]
        out[0:SSD_HEADS, at] = a["dt_bias"][l]
        out[DTF_F:DTF_F + FOX_HEADS, at] = a["b_forget"][l]
        out[0:SSD_HEADS, VEC[f"a_log{l}"][0]] = a["a_log"][l]
        for name, key in (("pre_g", "ffn_pre_norm_2"), ("mix_g", "mix_norm_2"),
                          ("post_g", "ffn_post_norm_2"), ("mem_g", "mem_norm_2")):
            put(f"{name}{l}", a[key][l])
        put(f"memq_g{l}", np.tile(a["mem_q_norm_2"][l], 2))
        put(f"memk_g{l}", np.tile(a["mem_k_norm_2"][l], 2))
    put("final_g", a["final_g"])
    put("mu", a["a_shift_mu_2"][0])
    for name, key in (("w0", "a_w0_2"), ("a0", "a_a0_2"), ("kk_scale", "a_kk_scale_2"),
                      ("k_a", "a_k_a_2"), ("r_k", "a_r_k_2"), ("lnx_g", "a_lnx_g_2"),
                      ("lnx_b", "a_lnx_b_2")):
        put(name, a[key][0].reshape(-1))
    put("bq_g", np.tile(a["b_q_norm_2"][0], 2))
    put("kv_g", a["kv_norm_2"])
    put("kvk_g", np.tile(a["kv_k_norm_2"], 2))
    return out


def token_columns(x):
    return np.ascontiguousarray(x.T.reshape(-1, P, x.shape[0]).transpose(1, 0, 2))


def kernel(**inputs):
    import concourse.bacc as bacc
    from concourse.bass_utils import run_bass_kernel_spmd

    a = {name: np.asarray(v) for name, v in inputs.items()}
    weights, stream = weight_stream(a)
    lora = np.zeros((P, 2 * RW * P), np.float32)
    lora[0:HD, 0:RW * P] = a["a_w_up_2"][0]
    lora[HD:P, RW * P:] = a["a_a_up_2"][0]
    ada = a["w_ada"].reshape(DEPTH, KD, P, ADA_RUNS // DEPTH, ADA_RUN, P).transpose(0, 3, 2, 4, 1, 5)
    arrays = {
        "ada": ada.reshape(ADA_RUNS, P, ADA_RUN * D),
        "const": CONST_ARRAY, "decay": decay_table(), "buckets": bucket_table(),
        "vec": packed_vectors(a),
        "x": token_columns(a["x"][0]), "c": np.ascontiguousarray(feature_columns(a["c"][0])),
        "positions": a["positions"].reshape(T),
        "mem": token_columns(a["mem_2"][0]),
        "lora": lora,
        "gate_up": a["a_g_up_2"][0],
        "rel": a["rel_bias_2"], **weights}
    arrays = {n: np.ascontiguousarray(v) for n, v in arrays.items()}
    nc = bacc.Bacc("TRN2", target_bir_lowering=False, num_devices=1)
    dram = {n: nc.dram_tensor(f"in_{n}", v.shape, mybir.dt.from_np(v.dtype), kind="ExternalInput").ap()
            for n, v in arrays.items()}
    dram["out"] = nc.dram_tensor("out", (P, KD, T), F32, kind="ExternalOutput").ap()
    dram["skew"] = nc.dram_tensor("skew", (12, P, NREL), F32, kind="Internal").ap()
    dram["stream"] = stream
    build(nc, dram)
    run = run_bass_kernel_spmd(nc, [{f"in_{n}": v for n, v in arrays.items()}], core_ids=[0])
    out = run.results[0]["out"]
    return np.ascontiguousarray(out.transpose(1, 0, 2).reshape(D, T).T)[None]
```
